# Optimizing a Trainium2 kernel written in Bass

```python
import jax, jax.numpy as jnp
from jax import lax
import numpy as np

D_MODEL = 1024
BATCH = 1
SEQ = 256
DEPTH = 1
DEC_BATCH = 1
DEC_SEQ = 1024
PAST_LEN = 128

GRID_W = 64
HEAD_DIM = 64
N_Q_HEADS = 8
N_KV_HEADS = 2
ATTN_WIDTH = N_Q_HEADS * HEAD_DIM
KV_WIDTH = N_KV_HEADS * HEAD_DIM
Q_BLOCK = 128
ROPE_THETA = 10000.0
GLA_HEADS = 4
GLA_DK = 64
GLA_DV = 128
GLA_KW = GLA_HEADS * GLA_DK
GLA_VW = GLA_HEADS * GLA_DV
GLA_LOWRANK = 16
GLA_GATE_NORM = 16.0
GLA_CHUNK = 64
N_EXPERTS = 16
EXPERT_FF = 1024
EC_CAPACITY = 2
PLE_DIM = 256
NORM_EPS = 1e-6
IN_WIDTH = (ATTN_WIDTH + 2 * KV_WIDTH + 2 * GLA_KW + 2 * GLA_VW
            + 2 * GLA_LOWRANK + 2 * D_MODEL)

kernel_name = "hybrid_gqa_gla_ec_encoder"

def rms_norm(x, g):
    xf = x.astype(jnp.float32)
    y = xf * lax.rsqrt(jnp.mean(xf * xf, axis=-1, keepdims=True) + NORM_EPS)
    return (y * g.astype(jnp.float32)).astype(x.dtype)

def axial_angles(T):
    rows = T // GRID_W
    r, c = jnp.meshgrid(jnp.arange(rows), jnp.arange(GRID_W), indexing="ij")
    r = r.reshape(-1).astype(jnp.float32)
    c = c.reshape(-1).astype(jnp.float32)
    half = HEAD_DIM // 2
    inv = ROPE_THETA ** (-jnp.arange(0, half, 2, dtype=jnp.float32) / half)
    return r[:, None] * inv, c[:, None] * inv

def rotate_half(x, ang):
    cos = jnp.cos(ang)[:, None, :]
    sin = jnp.sin(ang)[:, None, :]
    x1, x2 = jnp.split(x, 2, axis=-1)
    return jnp.concatenate([x1 * cos - x2 * sin, x2 * cos + x1 * sin], axis=-1)

def apply_axial_rope(x, ang_r, ang_c):
    xr, xc = jnp.split(x, 2, axis=-1)
    return jnp.concatenate([rotate_half(xr, ang_r), rotate_half(xc, ang_c)], axis=-1)

def gqa_attention(q, k, v, q_norm, k_norm):
    B, T, _ = q.shape
    dt = q.dtype
    G = N_Q_HEADS // N_KV_HEADS
    q = q.reshape(B, T, N_Q_HEADS, HEAD_DIM)
    k = k.reshape(B, T, N_KV_HEADS, HEAD_DIM)
    v = v.reshape(B, T, N_KV_HEADS, HEAD_DIM)
    ang_r, ang_c = axial_angles(T)
    q = apply_axial_rope(rms_norm(q, q_norm).astype(jnp.float32), ang_r, ang_c).astype(dt)
    k = apply_axial_rope(rms_norm(k, k_norm).astype(jnp.float32), ang_r, ang_c).astype(dt)
    nb = T // Q_BLOCK
    qb = q.reshape(B, nb, Q_BLOCK, N_KV_HEADS, G, HEAD_DIM).transpose(1, 0, 2, 3, 4, 5)
    scale = HEAD_DIM ** -0.5

    def block(qblk):
        s = jnp.einsum("bqkgd,bskd->bkgqs", qblk, k).astype(jnp.float32) * scale
        p = jax.nn.softmax(s, axis=-1).astype(v.dtype)
        return jnp.einsum("bkgqs,bskd->bqkgd", p, v)

    o = lax.map(block, qb)
    return o.transpose(1, 0, 2, 3, 4, 5).reshape(B, T, ATTN_WIDTH)

def gla_scan(q, k, v, g, strict):
    B, T, H, dk = q.shape
    dv = v.shape[-1]
    L = GLA_CHUNK
    n = T // L

    def chunks(a):
        return a.reshape(B, n, L, H, a.shape[-1]).transpose(1, 0, 3, 2, 4)

    mask = jnp.tril(jnp.ones((L, L), dtype=bool), k=-1 if strict else 0)

    def step(S, inp):
        qc, kc, vc, gc = inp
        b = jnp.cumsum(gc, axis=2)
        diff = b[:, :, :, None, :] - b[:, :, None, :, :]
        decay = jnp.exp(jnp.where(mask[:, :, None], diff, -jnp.inf))
        A = jnp.einsum("bhtd,bhsd,bhtsd->bhts", qc, kc, decay)
        o = jnp.einsum("bhts,bhse->bhte", A, vc) + jnp.einsum("bhtd,bhde->bhte", qc * jnp.exp(b), S)
        b_last = b[:, :, -1:, :]
        S = (jnp.exp(b_last[:, :, 0, :])[..., None] * S
             + jnp.einsum("bhsd,bhse->bhde", kc * jnp.exp(b_last - b), vc))
        return S, o

    S0 = jnp.zeros((B, H, dk, dv), jnp.float32)
    _, o = lax.scan(step, S0, (chunks(q), chunks(k), chunks(v), chunks(g)))
    return o.transpose(1, 0, 3, 2, 4).reshape(B, T, H, dv)

def gla_branch(q, k, v, r, a_f, a_b, w_af, b_af, w_ab, b_ab, gla_norm):
    B, T, _ = q.shape
    f32 = jnp.float32
    qf = q.astype(f32).reshape(B, T, GLA_HEADS, GLA_DK) * (GLA_DK ** -0.5)
    kf = k.astype(f32).reshape(B, T, GLA_HEADS, GLA_DK)
    vf = v.astype(f32).reshape(B, T, GLA_HEADS, GLA_DV)

    def log_gate(a, w, b):
        z = a.astype(f32) @ w.astype(f32) + b.astype(f32)
        return (jax.nn.log_sigmoid(z) / GLA_GATE_NORM).reshape(B, T, GLA_HEADS, GLA_DK)

    g_f = log_gate(a_f, w_af, b_af)
    g_b = log_gate(a_b, w_ab, b_ab)
    o_f = gla_scan(qf, kf, vf, g_f, False)
    flip = lambda t: jnp.flip(t, axis=1)
    o_b = flip(gla_scan(flip(qf), flip(kf), flip(vf), flip(g_b), True))
    o = rms_norm(o_f + o_b, gla_norm).reshape(B, T, GLA_VW)
    return (o * jax.nn.silu(r.astype(f32))).astype(r.dtype)

def expert_choice_ffn(h, w_router, w_gate, w_up, w_down):
    B, T, D = h.shape
    N = B * T
    tok = h.reshape(N, D)
    aff = jax.nn.softmax((tok @ w_router).astype(jnp.float32), axis=-1)
    C = EC_CAPACITY * N // N_EXPERTS
    gate, idx = lax.top_k(aff.T, C)
    xe = tok[idx]
    hid = jax.nn.silu(jnp.einsum("ecd,edf->ecf", xe, w_gate)) * jnp.einsum("ecd,edf->ecf", xe, w_up)
    ye = jnp.einsum("ecf,efd->ecd", hid, w_down) * gate[..., None].astype(tok.dtype)
    out = jnp.zeros_like(tok).at[idx.reshape(-1)].add(ye.reshape(-1, D))
    return out.reshape(B, T, D)

def hybrid_layer(x, p, g_mix, w_in, q_norm, k_norm, w_af, b_af, w_ab, b_ab, gla_norm,
                 w_attn_up, w_gla_up, w_out, g_moe, w_router, w_gate_e, w_up_e, w_down_e,
                 g_ple, w_ple_gate, w_ple_proj):
    h = rms_norm(x, g_mix)
    proj = h @ w_in
    sizes = (ATTN_WIDTH, KV_WIDTH, KV_WIDTH, GLA_KW, GLA_KW, GLA_VW, GLA_VW,
             GLA_LOWRANK, GLA_LOWRANK, D_MODEL, D_MODEL)
    offs = [int(o) for o in np.cumsum(sizes)[:-1]]
    aq, ak, av, lq, lk, lv, lr, laf, lab, gate_a, gate_l = jnp.split(proj, offs, axis=-1)
    o_attn = gqa_attention(aq, ak, av, q_norm, k_norm) @ w_attn_up
    o_gla = gla_branch(lq, lk, lv, lr, laf, lab, w_af, b_af, w_ab, b_ab, gla_norm) @ w_gla_up
    merged = jax.nn.sigmoid(gate_a) * o_attn + jax.nn.sigmoid(gate_l) * o_gla
    x = x + merged @ w_out
    x = x + expert_choice_ffn(rms_norm(x, g_moe), w_router, w_gate_e, w_up_e, w_down_e)
    x = x + jax.nn.sigmoid(rms_norm(x, g_ple) @ w_ple_gate) * (p @ w_ple_proj)
    return x

def trunk(x, p, g_mix, w_in, q_norm, k_norm, w_af, b_af, w_ab, b_ab, gla_norm,
          w_attn_up, w_gla_up, w_out, g_moe, w_router, w_gate_e, w_up_e, w_down_e,
          g_ple, w_ple_gate, w_ple_proj, g_final):
    for i in range(DEPTH):
        x = hybrid_layer(x, p[i], g_mix[i], w_in[i], q_norm[i], k_norm[i], w_af[i], b_af[i],
                         w_ab[i], b_ab[i], gla_norm[i], w_attn_up[i], w_gla_up[i], w_out[i],
                         g_moe[i], w_router[i], w_gate_e[i], w_up_e[i], w_down_e[i],
                         g_ple[i], w_ple_gate[i], w_ple_proj[i])
    return rms_norm(x, g_final)

def setup_inputs(seed: int = 0) -> dict:
    key = jax.random.key(seed)
    ks = jax.random.split(key, 32)
    f32 = jnp.float32
    nrm = lambda k, s, sc: jax.random.normal(k, s, f32) * sc
    gain = lambda k, s: 1.0 + 0.02 * jax.random.normal(k, s, f32)
    D = D_MODEL
    return {
        "x_prompt": nrm(ks[0], (BATCH, SEQ, D), 1.0),
        "x_sample": nrm(ks[1], (DEC_BATCH, DEC_SEQ, D), 1.0),
        "p_prompt": nrm(ks[2], (DEPTH, BATCH, SEQ, PLE_DIM), 1.0),
        "p_sample": nrm(ks[3], (DEPTH, DEC_BATCH, DEC_SEQ, PLE_DIM), 1.0),
        "g_mix": gain(ks[4], (DEPTH, D)),
        "w_in": nrm(ks[5], (DEPTH, D, IN_WIDTH), D ** -0.5),
        "q_norm": gain(ks[6], (DEPTH, HEAD_DIM)),
        "k_norm": gain(ks[7], (DEPTH, HEAD_DIM)),
        "w_af": nrm(ks[8], (DEPTH, GLA_LOWRANK, GLA_KW), GLA_LOWRANK ** -0.5),
        "b_af": nrm(ks[9], (DEPTH, GLA_KW), 0.1),
        "w_ab": nrm(ks[10], (DEPTH, GLA_LOWRANK, GLA_KW), GLA_LOWRANK ** -0.5),
        "b_ab": nrm(ks[11], (DEPTH, GLA_KW), 0.1),
        "gla_norm": gain(ks[12], (DEPTH, GLA_DV)),
        "w_attn_up": nrm(ks[13], (DEPTH, ATTN_WIDTH, D), ATTN_WIDTH ** -0.5),
        "w_gla_up": nrm(ks[14], (DEPTH, GLA_VW, D), GLA_VW ** -0.5),
        "w_out": nrm(ks[15], (DEPTH, D, D), D ** -0.5),
        "g_moe": gain(ks[16], (DEPTH, D)),
        "w_router": nrm(ks[17], (DEPTH, D, N_EXPERTS), D ** -0.5),
        "w_gate_e": nrm(ks[18], (DEPTH, N_EXPERTS, D, EXPERT_FF), D ** -0.5),
        "w_up_e": nrm(ks[19], (DEPTH, N_EXPERTS, D, EXPERT_FF), D ** -0.5),
        "w_down_e": nrm(ks[20], (DEPTH, N_EXPERTS, EXPERT_FF, D), EXPERT_FF ** -0.5),
        "g_ple": gain(ks[21], (DEPTH, D)),
        "w_ple_gate": nrm(ks[22], (DEPTH, D, D), D ** -0.5),
        "w_ple_proj": nrm(ks[23], (DEPTH, PLE_DIM, D), PLE_DIM ** -0.5),
        "g_final": gain(ks[24], (D,)),
    }

def reference(x_prompt, x_sample, p_prompt, p_sample, g_mix, w_in, q_norm, k_norm, w_af, b_af,
              w_ab, b_ab, gla_norm, w_attn_up, w_gla_up, w_out, g_moe, w_router, w_gate_e,
              w_up_e, w_down_e, g_ple, w_ple_gate, w_ple_proj, g_final):
    y_prompt = trunk(x_prompt, p_prompt, g_mix, w_in, q_norm, k_norm, w_af, b_af, w_ab, b_ab,
                     gla_norm, w_attn_up, w_gla_up, w_out, g_moe, w_router, w_gate_e, w_up_e,
                     w_down_e, g_ple, w_ple_gate, w_ple_proj, g_final)
    y_sample = trunk(x_sample, p_sample, g_mix, w_in, q_norm, k_norm, w_af, b_af, w_ab, b_ab,
                     gla_norm, w_attn_up, w_gla_up, w_out, g_moe, w_router, w_gate_e, w_up_e,
                     w_down_e, g_ple, w_ple_gate, w_ple_proj, g_final)
    return (y_prompt, y_sample)


_drawn_inputs = setup_inputs


def setup_inputs(seed=0):
    import zlib

    import numpy as np

    out = dict(_drawn_inputs(seed))
    spreads = {}
    factors = {'g_mix': 3.544,
     'q_norm': 8.0,
     'k_norm': 8.0,
     'b_af': 4.315,
     'b_ab': 4.243,
     'gla_norm': 6.504,
     'g_moe': 3.565,
     'g_ple': 8.0,
     'g_final': 2.852}
    for name, (base, spread) in spreads.items():
        noise = np.random.default_rng([zlib.crc32(name.encode()), seed]).standard_normal(out[name].shape)
        drawn = base * np.exp(spread * noise) if base else spread * noise
        out[name] = __import__('jax').numpy.asarray(drawn.astype(out[name].dtype))
    for name, factor in factors.items():
        out[name] = (out[name] * factor).astype(out[name].dtype)
    return out
```

```python
from contextlib import ExitStack

import concourse.bass as bass
from concourse import mybir

ALU = mybir.AluOpType
ACT = mybir.ActivationFunctionType
F32 = mybir.dt.float32
F32R = mybir.dt.float32r
U32 = mybir.dt.uint32
I32 = mybir.dt.int32
AX = mybir.AxisListType
ds = bass.ds

P = 128
D = 1024
KT = D // P
N_SAMPLE, N_PROMPT = 1024, 256
T = N_SAMPLE + N_PROMPT
NT = T // P
NT_S = N_SAMPLE // P
EPS = 1e-6

HEADS, KV_HEADS, HD = 8, 2, 64
QKV_W = (HEADS + 2 * KV_HEADS) * HD
GLA_H, DK, DV, LORA, CHUNK = 4, 64, 128, 16, 64
PAIRS = T // (2 * CHUNK)
GLA_HP = GLA_H // 2
GATE_NORM = 16.0

WB = 256
TM_BLOCKS = (QKV_W + GLA_H * DV) // WB
FM_BLOCKS = (2 * GLA_H * DK + GLA_H * DV + 2 * D) // WB
W_BLOCKS = TM_BLOCKS + FM_BLOCKS + 1
FM_TILES = 2 * FM_BLOCKS + 1
T_LQ, T_LK, T_LR, T_GA, T_GL, T_LORA = 0, 2, 4, 8, 16, 24

E = 16
FF = 1024
CAP_S, CAP_P = 2 * N_SAMPLE // E, 2 * N_PROMPT // E
CAP = CAP_S + CAP_P
PLE = 256
CW = 256
CHUNKS = T // CW
LEVELS = (32, 16, 8, 4, 2, 1)


class Chain:

    def __init__(self, sem, steps):
        self.sem, self.steps, self.at, self.i = sem, steps, 0, 0

    def turn(self, i):
        assert self.at in (0, self.steps), (self.at, self.steps)
        self.at, self.i = 0, i

    def step(self, ins):
        ins.then_inc(self.sem, 1)
        self.at += 1

    def link(self, eng, ins):
        self.step(ins)
        eng.wait_ge(self.sem, self.i * self.steps + self.at)


class Core:

    def __init__(self, nc, ctx, io):
        self.nc, self.ctx, self.io = nc, ctx, io
        self.in_use = []
        self.ps = ctx.enter_context(nc.psum_tensor("ps", [P, 8, 512], F32))
        self.ident = ctx.enter_context(nc.sbuf_tensor("ident", [P, P], F32))
        dram = lambda name, shape: nc.dram_tensor(name, shape, F32, kind="Internal").ap()
        self.tm = dram("tm_scratch", (TM_BLOCKS, NT, P, WB))
        self.fm = dram("fm_scratch", (FM_TILES, P, T))
        self.up_in = dram("up_in_scratch", (KT, P, T))
        self.x_res = dram("x_res_scratch", (T, D))
        self.xm = dram("xm_scratch", (T, D))

    def bank(self, n, width=512):
        return self.ps[:, n, 0:width]

    def sem(self, name):
        self.in_use.append(self.nc.alloc_semaphore(name=name))
        return self.in_use[-1]

    def recycle_sems(self):
        self.nc.clear_and_free_semaphores(self.in_use)
        self.in_use = []
        self.nc.all_engine_barrier()

    def sems(self, name, n):
        return [self.sem(f"{name}{b}") for b in range(n)]


def newton(dve, chain, rs, ms, tmp):
    chain.link(dve, dve.tensor_tensor(tmp, rs, rs, ALU.mult))
    chain.link(dve, dve.tensor_tensor(tmp, tmp, ms, ALU.mult))
    chain.link(dve, dve.tensor_scalar(tmp, tmp, -0.5, 1.5, ALU.mult, ALU.add))
    chain.link(dve, dve.tensor_tensor(rs, rs, tmp, ALU.mult))


NEWTON = 4


def split3(pe, out, lhs, rhs, start, stop):
    (lh, ll), (rh, rl) = lhs, rhs
    pe.matmul(out, lh, rh, start=start, stop=False)
    pe.matmul(out, lh, rl, start=False, stop=False)
    return pe.matmul(out, ll, rh, start=False, stop=stop)


def stage_norm(core, ah, al):
    nc, io = core.nc, core.io
    with ExitStack() as mem:
        sb = lambda name, shape, dt=F32: mem.enter_context(nc.sbuf_tensor(name, shape, dt))
        g = sb("n_gain", [P, D])
        x = sb("n_x", [P, 2, D])
        sq = sb("n_sq", [P, 2, D])
        xn = sb("n_xn", [P, 2, D])
        st = sb("n_stat", [P, 2, 4])
        s_const = core.sem("n_const")
        x_in = core.sems("n_x_in", 2)
        sq_done = core.sems("n_sq_done", 2)
        ms_done = core.sems("n_ms_done", 2)
        rt_done = core.sems("n_rt_done", 2)
        rs_chain = [Chain(core.sem(f"n_rs_chain{b}"), 1 + NEWTON) for b in range(2)]
        xn_done = core.sems("n_xn_done", 2)
        tr_done = core.sems("n_tr_done", 2)
        hi_done = core.sems("n_hi_done", 2)
        lo_done = core.sems("n_lo_done", 2)
        pt = [core.ps[:, 2 * b:2 * b + 2, :] for b in range(2)]
        block = mem.enter_context(nc.Block())

        @block.sync
        def _(sp):
            sp.dma_start(core.ident[:, :], io["ident"]).then_inc(s_const, 16)
            sp.dma_start(g[:, :], io["g_mix"].partition_broadcast(P)).then_inc(s_const, 16)
            with sp.Fori(0, NT // 2) as i:
                for b in range(2):
                    sp.wait_ge(xn_done[b], i)
                    sp.dma_start(x[:, b, :], io["x"][ds(i * 2 * P + b * P, P), :]).then_inc(x_in[b], 16)

        @block.scalar
        def _(act):
            def stats(i, b):
                act.wait_ge(x_in[b], i * 16 + 16)
                act.activation(sq[:, b, :], x[:, b, :], ACT.Square, accum_out=st[:, b, 0:1]).then_inc(sq_done[b], 1)
                act.wait_ge(ms_done[b], i + 1)
                act.activation(st[:, b, 2:3], st[:, b, 1:2], ACT.Sqrt).then_inc(rt_done[b], 1)

            def high(i, b):
                act.wait_ge(tr_done[b], i + 1)
                act.activation(ah[:, :, ds(i * 2 * P + b * P, P)], pt[b].rearrange("p a (c n) -> p (a c) n", n=P),
                               ACT.Copy).then_inc(hi_done[b], 1)

            with act.Fori(0, NT // 2) as i:
                for b in range(2):
                    stats(i, b)
                for b in range(2):
                    high(i, b)

        @block.vector
        def _(dve):
            dve.wait_ge(s_const, 32)
            with dve.Fori(0, NT // 2) as i:
                for b in range(2):
                    dve.wait_ge(sq_done[b], i + 1)
                    dve.tensor_scalar(st[:, b, 1:2], st[:, b, 0:1], 1.0 / D, EPS, ALU.mult, ALU.add).then_inc(ms_done[b], 1)
                    dve.wait_ge(rt_done[b], i + 1)
                    rs_chain[b].turn(i)
                    rs_chain[b].link(dve, dve.reciprocal(st[:, b, 3:4], st[:, b, 2:3]))
                    newton(dve, rs_chain[b], st[:, b, 3:4], st[:, b, 1:2], st[:, b, 2:3])
                    dve.wait_ge(tr_done[b], i)
                    dve.scalar_tensor_tensor(xn[:, b, :], x[:, b, :], st[:, b, 3:4], g[:, :], ALU.mult,
                                             ALU.mult).then_inc(xn_done[b], 1)
                for b in range(2):
                    tok = ds(i * 2 * P + b * P, P)
                    dve.wait_ge(hi_done[b], i + 1)
                    dve.tensor_tensor(al[:, :, tok], pt[b].rearrange("p a (c n) -> p (a c) n", n=P),
                                      ah[:, :, tok].bitcast(F32), ALU.subtract).then_inc(lo_done[b], 1)

        @block.tensor
        def _(pe):
            pe.wait_ge(s_const, 32)
            with pe.Fori(0, NT // 2) as i:
                for b in range(2):
                    pe.wait_ge(xn_done[b], i + 1)
                    pe.wait_ge(lo_done[b], i)
                    for k in range(KT):
                        last = pe.transpose(pt[b][:, k // 4, (k % 4) * P:(k % 4 + 1) * P],
                                            xn[:, b, k * P:(k + 1) * P], core.ident[:, :])
                    last.then_inc(tr_done[b], 1)


def stage_project(core, ah, al):
    nc, io = core.nc, core.io
    with ExitStack() as mem:
        sb = lambda name, shape, dt=F32: mem.enter_context(nc.sbuf_tensor(name, shape, dt))
        raw = [sb(f"w_raw{b}", [P, KT, WB]) for b in range(2)]
        hi = [sb(f"w_hi{b}", [P, KT, WB], F32R) for b in range(2)]
        lo = [sb(f"w_lo{b}", [P, KT, WB], F32R) for b in range(2)]
        TS = 5
        tm_out = sb("tm_out", [P, TS, WB])
        fm_out = sb("fm_out", [P, 2, T])
        w_in = core.sems("p_w_in", 2)
        hi_done = core.sems("p_hi_done", 2)
        lo_done = core.sems("p_lo_done", 2)
        w_used = core.sems("p_w_used", 2)
        tm_done = core.sems("p_tm_done", TS)
        tm_read = core.sems("p_tm_read", TS)
        tm_stored = core.sems("p_tm_stored", TS)
        fm_done = core.sem("p_fm_done")
        fm_read = core.sems("p_fm_read", 2)
        fm_stored = core.sems("p_fm_stored", 2)
        TM_USES = NT // TS
        fm_bank = [core.ps[:, 3 * t:3 * t + 3, :] for t in range(2)]
        tok = [(0, 512), (512, 512), (1024, 256)]
        block = mem.enter_context(nc.Block())

        @block.sync
        def _(sp):
            with sp.Fori(0, W_BLOCKS // 2) as i:
                for b in range(2):
                    sp.wait_ge(lo_done[b], i)
                    sp.dma_start(raw[b][:, :, :], io["w_blk"][ds(i * 2 + b, 1), :, :, :].rearrange(
                        "o p k c -> (o p) k c")).then_inc(w_in[b], 16)

        def walk(split, token_major, feature_major, lora, loop):
            split(0, 0)
            with loop(0, 2) as i:
                split(i, 1)
                token_major(i, 0)
                split(i + 1, 0)
                token_major(i, 1)
            split(2, 1)
            token_major(2, 0)
            split(3, 0)
            feature_major(2, 1, ACT.Copy)
            for i in (3, 4):
                split(i, 1)
                feature_major(i, 0, ACT.Copy)
                split(i + 1, 0)
                feature_major(i, 1, ACT.Copy if i == 3 else ACT.Sigmoid)
            with loop(5, 8) as i:
                split(i, 1)
                feature_major(i, 0, ACT.Sigmoid)
                split(i + 1, 0)
                feature_major(i, 1, ACT.Sigmoid)
            split(8, 1)
            feature_major(8, 0, ACT.Sigmoid)
            lora(8, 1)

        def tile_use(i, b, t):
            n = i * 2 + b
            return n if t % TS == TS - 1 else n * TM_USES + t // TS

        @block.scalar
        def _(act):
            def split(i, b):
                act.wait_ge(w_in[b], i * 16 + 16)
                act.wait_ge(w_used[b], i)
                act.activation(hi[b][:, :, :], raw[b][:, :, :], ACT.Copy).then_inc(hi_done[b], 1)

            def token_major(i, b):
                for t in range(NT):
                    s, use = t % TS, (i * 2 + b) * TM_USES + t // TS
                    if t < NT - 1:
                        act.wait_ge(tm_done[s], tile_use(i, b, t) + 1)
                    else:
                        act.wait_ge(w_used[b], i + 1)
                    act.wait_ge(tm_stored[s], use * 16)
                    act.activation(tm_out[:, s, :], core.bank(s, WB), ACT.Copy).then_inc(tm_read[s], 1)

            def fm_tile(i, b, use, t, func):
                if t == 0:
                    act.wait_ge(fm_done, use + 1)
                else:
                    act.wait_ge(w_used[b], i + 1)
                act.wait_ge(fm_stored[t], use * 16)
                act.activation(fm_out[:, t, 0:1024], fm_bank[t][:, 0:2, :], func)
                act.activation(fm_out[:, t, 1024:T], fm_bank[t][:, 2, 0:256], func).then_inc(fm_read[t], 1)

            def feature_major(i, b, func):
                for t in range(2):
                    fm_tile(i, b, i * 2 + b - TM_BLOCKS, t, func)

            def lora(i, b):
                fm_tile(i, b, FM_BLOCKS, 0, ACT.Copy)

            walk(split, token_major, feature_major, lora, act.Fori)

        @block.vector
        def _(dve):
            def split(i, b):
                dve.wait_ge(hi_done[b], i + 1)
                dve.tensor_tensor(lo[b][:, :, :], raw[b][:, :, :], hi[b][:, :, :].bitcast(F32),
                                  ALU.subtract).then_inc(lo_done[b], 1)

            split(0, 0)
            split(0, 1)
            with dve.Fori(1, W_BLOCKS // 2) as i:
                split(i, 0)
                split(i, 1)

        @block.gpsimd
        def _(pool):
            def split(i, b):
                pass

            def token_major(i, b):
                for t in range(NT):
                    s, use = t % TS, (i * 2 + b) * TM_USES + t // TS
                    pool.wait_ge(tm_read[s], use + 1)
                    pool.nop(nofuse=True)
                    pool.dma_start(core.tm[ds(i * 2 + b, 1), t, :, :].rearrange("o p c -> (o p) c"),
                                   tm_out[:, s, :]).then_inc(tm_stored[s], 16)

            def fm_tile(use, t):
                pool.wait_ge(fm_read[t], use + 1)
                pool.nop(nofuse=True)
                pool.dma_start(core.fm[ds(use * 2 + t, 1), :, :].rearrange("o p c -> (o p) c"),
                               fm_out[:, t, :]).then_inc(fm_stored[t], 16)

            def feature_major(i, b, func):
                for t in range(2):
                    fm_tile(i * 2 + b - TM_BLOCKS, t)

            def lora(i, b):
                fm_tile(FM_BLOCKS, 0)

            walk(split, token_major, feature_major, lora, pool.Fori)
            for s in range(TS):
                pool.wait_ge(tm_stored[s], 16 * TM_BLOCKS * TM_USES)
            pool.wait_ge(fm_stored[0], 16 * (FM_BLOCKS + 1))
            pool.wait_ge(fm_stored[1], 16 * FM_BLOCKS)

        @block.tensor
        def _(pe):
            def split(i, b):
                pass

            def token_major(i, b):
                pe.wait_ge(lo_done[b], i + 1)
                for t in range(NT):
                    s, use = t % TS, (i * 2 + b) * TM_USES + t // TS
                    pe.wait_ge(tm_read[s], use)
                    for k in range(KT):
                        x = [a[:, k, t * P:(t + 1) * P] for a in (ah, al)]
                        w = [a[:, k, :] for a in (hi[b], lo[b])]
                        last = split3(pe, core.bank(s, WB), x, w, k == 0, k == KT - 1)
                    last.then_inc(tm_done[s] if t < NT - 1 else w_used[b], 1)

            def fm_tile(b, t, use, done):
                pe.wait_ge(fm_read[t], use)
                for k in range(KT):
                    wh, wl = (a[:, k, t * P:(t + 1) * P] for a in (hi[b], lo[b]))
                    for w, x in ((wh, ah), (wh, al), (wl, ah)):
                        for n, (at, width) in enumerate(tok):
                            last = pe.matmul(fm_bank[t][:, n, 0:width], w, x[:, k, at:at + width],
                                             start=(k == 0 and w is wh and x is ah), stop=(k == KT - 1 and w is wl))
                last.then_inc(done, 1)

            def feature_major(i, b, func):
                pe.wait_ge(lo_done[b], i + 1)
                for t in range(2):
                    fm_tile(b, t, i * 2 + b - TM_BLOCKS, w_used[b] if t else fm_done)

            def lora(i, b):
                pe.wait_ge(lo_done[b], i + 1)
                fm_tile(b, 0, FM_BLOCKS, fm_done)

            def first_feature_major():
                for s in range(TS):
                    pe.wait_ge(tm_read[s], TM_BLOCKS * TM_USES)

            fm = feature_major
            def feature_major(i, b, func):
                if isinstance(i, int) and i * 2 + b == TM_BLOCKS:
                    first_feature_major()
                fm(i, b, func)

            walk(split, token_major, feature_major, lora, pe.Fori)


def stage_rope(core, qt, kt, v):
    nc, io = core.nc, core.io
    H = HEADS + KV_HEADS
    W = H * HD
    KD = 2 * KV_HEADS
    with ExitStack() as mem:
        sb = lambda name, shape, dt=F32: mem.enter_context(nc.sbuf_tensor(name, shape, dt))
        gain = sb("r_gain", [P, H, HD])
        x = sb("r_x", [P, 2, W])
        tab = sb("r_tab", [P, 2, 2, HD])
        sq = sb("r_sq", [P, 2, W])
        u = sb("r_u", [P, 2, W])
        out = sb("r_out", [P, 2, (HEADS + KD) * HD])
        st = sb("r_stat", [P, 2, 4, H])
        s_const = core.sem("r_const")
        x_in = core.sems("r_x_in", 2)
        v_in = core.sem("r_v_in")
        ms_done = core.sems("r_ms_done", 2)
        rt_done = core.sems("r_rt_done", 2)
        out_done = core.sems("r_out_done", 2)
        tr_done = core.sems("r_tr_done", 2)
        tr_read = core.sems("r_tr_read", 2)
        STEPS = 1 + 1 + 1 + NEWTON + 2 + 1 + 2
        chain = [Chain(core.sem(f"r_chain{b}"), STEPS) for b in range(2)]
        pt = [core.ps[:, 2 * b:2 * b + 2, 0:384] for b in range(2)]
        block = mem.enter_context(nc.Block())

        @block.sync
        def _(sp):
            for h in range(HEADS):
                sp.dma_start(gain[:, h, :], io["q_norm"].partition_broadcast(P)).then_inc(s_const, 16)
            for h in range(KV_HEADS):
                sp.dma_start(gain[:, HEADS + h, :], io["k_norm"].partition_broadcast(P)).then_inc(s_const, 16)
            with sp.Fori(0, NT // 2) as i:
                for b in range(2):
                    t = i * 2 + b
                    sp.wait_ge(out_done[b], i)
                    for k in range(3):
                        w = WB if k < 2 else W - 2 * WB
                        sp.dma_start(x[:, b, k * WB:k * WB + w],
                                     core.tm[k, ds(t, 1), :, 0:w].rearrange("o p c -> (o p) c")).then_inc(x_in[b], 16)
                    sp.dma_start(v[:, ds(t, 1), :], core.tm[2, ds(t, 1), :, W - 2 * WB:WB].rearrange("o p c -> p o c")).then_inc(v_in, 16)
                    sp.dma_start(tab[:, b, :, :], io["rope"][ds(t, 1), :, :, :].rearrange("o p a c -> (o p) a c")).then_inc(x_in[b], 16)
            sp.wait_ge(v_in, 16 * NT)

        @block.scalar
        def _(act):
            with act.Fori(0, NT // 2) as i:
                for b in range(2):
                    act.wait_ge(ms_done[b], i + 1)
                    act.activation(st[:, b, 2, :], st[:, b, 1, :], ACT.Sqrt).then_inc(rt_done[b], 1)
                for b in range(2):
                    tok = ds(i * 2 * P + b * P, P)
                    act.wait_ge(tr_done[b], i + 1)
                    act.activation(qt[:, 0:3, tok], pt[b][:, 0, :].rearrange("p (a n) -> p a n", n=P), ACT.Copy)
                    act.activation(qt[:, 3:4, tok], pt[b][:, 1, 0:P].rearrange("p (a n) -> p a n", n=P), ACT.Copy)
                    act.activation(kt[:, :, tok], pt[b][:, 1, P:3 * P].rearrange("p (a n) -> p a n", n=P),
                                   ACT.Copy).then_inc(tr_read[b], 1)

        @block.vector
        def _(dve):
            dve.wait_ge(s_const, 16 * H)
            heads = lambda a: a.rearrange("p (h d) -> p h d", d=HD)
            halves = lambda a, s: a.rearrange("p (h s n) -> p h s n", s=2, n=HD // 4)[:, :, s, :]
            with dve.Fori(0, NT // 2) as i:
                for b in range(2):
                    c = chain[b]
                    c.turn(i)
                    s = lambda k: st[:, b, k, :]
                    xb, ub = x[:, b, :], u[:, b, :]
                    dve.wait_ge(x_in[b], i * 64 + 64)
                    c.link(dve, dve.tensor_tensor(sq[:, b, :], xb, xb, ALU.mult))
                    c.link(dve, dve.tensor_reduce(s(0), heads(sq[:, b, :]), AX.X, ALU.add))
                    dve.tensor_scalar(s(1), s(0), 1.0 / HD, EPS, ALU.mult, ALU.add).then_inc(ms_done[b], 1)
                    dve.wait_ge(rt_done[b], i + 1)
                    c.link(dve, dve.reciprocal(s(3), s(2)))
                    newton(dve, c, s(3), s(1), s(2))
                    c.link(dve, dve.tensor_tensor(heads(xb), heads(xb), s(3).unsqueeze(2).broadcast_to((P, H, HD)), ALU.mult))
                    c.link(dve, dve.tensor_tensor(heads(xb), heads(xb), gain[:, :, :], ALU.mult))
                    cos, sin = (tab[:, b, k, :].unsqueeze(1).broadcast_to((P, H, HD)) for k in (0, 1))
                    c.link(dve, dve.tensor_tensor(heads(sq[:, b, :]), heads(xb), cos, ALU.mult))
                    tsin = lambda k: tab[:, b, 1, :].rearrange("p (a s n) -> p a s n", s=2, n=16)[:, :, k, :].unsqueeze(1)\
                        .broadcast_to((P, H, 2, 16))
                    q4 = lambda a, k: a.rearrange("p (h a s n) -> p h a s n", a=2, s=2, n=16)[:, :, :, k, :]
                    c.step(dve.tensor_tensor(q4(ub, 0), q4(xb, 1), tsin(0), ALU.mult))
                    c.link(dve, dve.tensor_tensor(q4(ub, 1), q4(xb, 0), tsin(1), ALU.mult))
                    dve.wait_ge(tr_done[b], i)
                    ob, sb_ = out[:, b, :], sq[:, b, :]
                    nq = HEADS * HD
                    dve.tensor_tensor(ob[:, 0:nq], sb_[:, 0:nq], ub[:, 0:nq], ALU.add)
                    kk = lambda a: heads(a[:, nq:W]).unsqueeze(2).broadcast_to((P, KV_HEADS, 2, HD))
                    dve.tensor_tensor(ob[:, nq:].rearrange("p (h r d) -> p h r d", h=KV_HEADS, r=2), kk(sb_), kk(ub),
                                      ALU.add).then_inc(out_done[b], 1)

        @block.tensor
        def _(pe):
            with pe.Fori(0, NT // 2) as i:
                for b in range(2):
                    pe.wait_ge(out_done[b], i + 1)
                    pe.wait_ge(tr_read[b], i)
                    for n in range(6):
                        last = pe.transpose(pt[b][:, n // 3, (n % 3) * P:(n % 3 + 1) * P],
                                            out[:, b, n * P:(n + 1) * P], core.ident[:, :])
                    last.then_inc(tr_done[b], 1)


def stage_attention(core, qt, kt, v):
    nc = core.nc
    ROUNDS = KV_HEADS
    with ExitStack() as mem:
        sb = lambda name, shape, dt=F32: mem.enter_context(nc.sbuf_tensor(name, shape, dt))
        qs = sb("a_qs", [P, 2, T])
        ks = sb("a_ks", [P, T])
        vs = sb("a_vs", [P, NT, HD])
        p = sb("a_p", [P, 2, N_SAMPLE])
        ptr = sb("a_ptr", [P, 2, NT_S, P])
        o = sb("a_o", [P, 2, 2, HD])
        at = sb("a_at", [P, 2, T])
        st = sb("a_stat", [P, 2, 4])
        units = [(hp, t, h) for hp in range(2) for t in range(NT) for h in range(2)]
        U = len(units)
        keys = lambda t: (0, NT_S) if t < NT_S else (NT_S, NT)
        staged = core.sem("a_staged")
        s_done = core.sems("a_s_done", 2)
        max_done = core.sems("a_max_done", 2)
        bias_done = core.sems("a_bias_done", 2)
        exp_done = core.sems("a_exp_done", 2)
        t_done = core.sem("a_t_done")
        ta_read = core.sem("a_ta_read")
        tb_read = core.sem("a_tb_read")
        pv_done = core.sems("a_pv_done", 2)
        rc_done = core.sems("a_rc_done", 2)
        o_done = core.sems("a_o_done", 2)
        ot_done = core.sem("a_ot_done")
        ot_read = core.sem("a_ot_read")
        at_stored = core.sems("a_at_stored", 2)
        ps_s = [core.ps[:, 2 * b:2 * b + 2, :] for b in range(2)]
        ps_t = core.ps[:, 4:6, :]
        ps_o = [core.ps[:, 6 + b, 0:HD] for b in range(2)]
        ps_ot = core.ps[:, 7, P:2 * P]
        SCALE = HD ** -0.5
        HU, TU = U // 2, U // 2
        block = mem.enter_context(nc.Block())

        @block.gpsimd
        def _(pool):
            with pool.Fori(0, ROUNDS) as i:
                pool.wait_ge(ot_done, i * TU)
                pool.tensor_copy(qs[:, :, :], qt[:, ds(i * 2, 2), :])
                pool.tensor_copy(ks[:, :].unsqueeze(1), kt[:, ds(i, 1), :])
                pool.tensor_copy(vs[:, :, :], v[:, :, ds(i * HD, HD)]).then_inc(staged, 1)

        def scores(eng, b, t):
            a, z = keys(t)
            n = (z - a) * P
            flat = ps_s[b].rearrange("p a c -> p (a c)")[:, 0:n]
            return flat, n

        @block.tensor
        def _(pe):
            def qk(i, u):
                hp, t, h = units[u]
                b, use = u % 2, i * HU + u // 2
                pe.wait_ge(exp_done[b], use)
                rows = slice(h * HD, h * HD + HD)
                a, z = keys(t)
                for n in range(a * P, z * P, 512):
                    w = min(512, z * P - n)
                    last = pe.matmul(ps_s[b][:, (n - a * P) // 512, 0:w], qs[rows, hp, t * P:(t + 1) * P],
                                     ks[rows, n:n + w], start=True, stop=True)
                last.then_inc(s_done[b], 1)

            def turn(i, u):
                hp, t, h = units[u]
                b, use = u % 2, i * HU + u // 2
                pe.wait_ge(exp_done[b], use + 1)
                pe.wait_ge(ta_read, i * U + u)
                pe.wait_ge(tb_read, i * U + u)
                a, z = keys(t)
                for n in range(z - a):
                    last = pe.transpose(ps_t[:, n // 4, (n % 4) * P:(n % 4 + 1) * P], p[:, b, n * P:(n + 1) * P],
                                        core.ident[:, :])
                last.then_inc(t_done, 1)

            def pv(i, u):
                hp, t, h = units[u]
                b, use = u % 2, i * HU + u // 2
                pe.wait_ge(ta_read, i * U + u + 1)
                pe.wait_ge(tb_read, i * U + u + 1)
                pe.wait_ge(o_done[b], use)
                if b:
                    pe.wait_ge(ot_read, i * TU + u // 2)
                a, z = keys(t)
                for n in range(z - a):
                    last = pe.matmul(ps_o[b], ptr[:, b, n, :], vs[:, a + n, :], start=(n == 0), stop=(n == z - a - 1))
                last.then_inc(pv_done[b], 1)

            def turn_out(i, u):
                pe.wait_ge(o_done[0], i * HU + u // 2 + 1)
                pe.wait_ge(o_done[1], i * HU + u // 2 + 1)
                pe.transpose(ps_ot, o[:, (u // 2) % 2, :, :].rearrange("p h d -> p (h d)"), core.ident[:, :]).then_inc(ot_done, 1)

            with pe.Fori(0, ROUNDS) as i:
                pe.wait_ge(staged, i + 1)
                qk(i, 0)
                for u in range(U):
                    if u + 1 < U:
                        qk(i, u + 1)
                    if u:
                        pv(i, u - 1)
                    if u >= 3 and u % 2:
                        turn_out(i, u - 2)
                    turn(i, u)
                pv(i, U - 1)
                turn_out(i, U - 1)

        @block.vector
        def _(dve):
            def row_max(i, u):
                b, use = u % 2, i * HU + u // 2
                flat, n = scores(dve, b, units[u][1])
                dve.wait_ge(s_done[b], use + 1)
                dve.tensor_reduce(st[:, b, 0:1], flat, AX.X, ALU.max, negate=True).then_inc(max_done[b], 1)
                dve.wait_ge(max_done[b], use + 1)
                dve.tensor_scalar(st[:, b, 1:2], st[:, b, 0:1], SCALE, None, ALU.mult).then_inc(bias_done[b], 1)

            def evict(i, u):
                b, use = u % 2, i * HU + u // 2
                n = min(4, keys(units[u][1])[1] - keys(units[u][1])[0])
                dve.wait_ge(t_done, i * U + u + 1)
                dve.wait_ge(pv_done[b], use)
                dve.tensor_copy(ptr[:, b, 0:n, :].rearrange("p a c -> p (a c)"), ps_t[:, 0, 0:n * P]).then_inc(ta_read, 1)

            def normalise(i, u):
                b, use = u % 2, i * HU + u // 2
                dve.reciprocal(st[:, b, 3:4], st[:, b, 2:3]).then_inc(rc_done[b], 1)
                dve.wait_ge(rc_done[b], use + 1)
                dve.wait_ge(pv_done[b], use + 1)
                tile = u // 2
                if tile >= 2:
                    dve.wait_ge(ot_done, i * TU + tile - 1)
                else:
                    dve.wait_ge(ot_done, i * TU)
                dve.tensor_scalar(o[:, tile % 2, b, :], ps_o[b], st[:, b, 3:4], None, ALU.mult).then_inc(o_done[b], 1)

            with dve.Fori(0, ROUNDS) as i:
                row_max(i, 0)
                for u in range(U):
                    if u + 1 < U:
                        if u + 1 >= 2:
                            pass
                        row_max(i, u + 1)
                    if u:
                        normalise(i, u - 1)
                    evict(i, u)
                normalise(i, U - 1)

        @block.scalar
        def _(act):
            def exp(i, u):
                b, use = u % 2, i * HU + u // 2
                flat, n = scores(act, b, units[u][1])
                act.wait_ge(bias_done[b], use + 1)
                act.wait_ge(o_done[b], use)
                act.activation(p[:, b, 0:n], flat, ACT.Exp, bias=st[:, b, 1:2], scale=SCALE,
                               accum_out=st[:, b, 2:3]).then_inc(exp_done[b], 1)

            def evict(i, u):
                b, use = u % 2, i * HU + u // 2
                t = units[u][1]
                act.wait_ge(t_done, i * U + u + 1)
                if t < NT_S:
                    act.wait_ge(pv_done[b], use)
                    act.activation(ptr[:, b, 4:8, :].rearrange("p a c -> p (a c)"), ps_t[:, 1, :], ACT.Copy).then_inc(tb_read, 1)
                else:
                    act.sem_inc(tb_read, 1)

            def evict_out(i, u):
                hp, t, _h = units[u]
                act.wait_ge(ot_done, i * TU + u // 2 + 1)
                if t == 0:
                    act.wait_ge(at_stored[hp], i * 16)
                act.activation(at[:, hp, t * P:(t + 1) * P], ps_ot, ACT.Copy).then_inc(ot_read, 1)

            with act.Fori(0, ROUNDS) as i:
                exp(i, 0)
                for u in range(U):
                    if u:
                        pass
                    evict(i, u)
                    if u + 1 < U:
                        exp(i, u + 1)
                    if u >= 3 and u % 2:
                        evict_out(i, u - 2)
                evict_out(i, U - 1)

        @block.sync
        def _(sp):
            with sp.Fori(0, ROUNDS) as i:
                for hp in range(2):
                    sp.wait_ge(ot_read, i * TU + (hp + 1) * NT)
                    sp.dma_start(core.up_in[ds(i * 2 + hp, 1), :, :].rearrange("o p t -> (o p) t"), at[:, hp, :]).then_inc(at_stored[hp], 16)
            for hp in range(2):
                sp.wait_ge(at_stored[hp], 16 * ROUNDS)


def stage_gla(core):
    nc, io = core.nc, core.io
    HP, NCH = GLA_HP, T // CHUNK
    SEAM = N_SAMPLE // CHUNK
    FLAT = HP * T
    with ExitStack() as mem:
        sb = lambda name, shape, dt=F32: mem.enter_context(nc.sbuf_tensor(name, shape, dt))
        q = sb("g_q", [P, HP, T])
        k = sb("g_k", [P, HP, T])
        bcum = sb("g_b", [P, 2, HP, T])
        v = sb("g_v", [P, PAIRS, GLA_H * DV])
        att = sb("g_att", [P, PAIRS, GLA_H, P])
        turns = [sb(f"g_turn{b}", [P, 2, HP, T]) for b in range(2)]
        ql, kl = ([turns[b][:, n, :, :] for b in range(2)] for n in range(2))
        both = sb("g_diff", [P, 2, HP, T])
        diff = [both[:, d, :, :] for d in range(2)]
        state = [sb(f"g_state{d}", [P, NCH, HP, DV]) for d in range(2)]
        decay = sb("g_decay", [P, 2, HP, NCH])
        mask = sb("g_mask", [P, len(LEVELS) + 1, P], I32)
        ones = sb("g_ones", [P, P])
        gain = sb("g_gain", [P, 1])
        bias = sb("g_bias", [P, 2, HP])
        w_lora = sb("g_w_lora", [2 * LORA, 2, HP, P])
        stat = sb("g_stat", [P, 4, PAIRS * GLA_H])
        lora = state[0][0:2 * LORA].rearrange("p c h d -> p (c h d)")[:, 0:T]
        reset = state[1][:, :, :, :].rearrange("p c h d -> p (c h d)")[:, 0:FLAT + 1]
        z = [ql[0], kl[0]]
        lg = [ql[1], kl[1]]
        kt = [diff[d].rearrange("p h t -> p (h t)").rearrange("p (a h c) -> p a h c", a=PAIRS, h=HP) for d in range(2)]
        by_pair = lambda x: x[:, :, :, :].rearrange("p d h t -> p (d h t)").rearrange("p (a h c) -> p a h c", a=PAIRS, h=GLA_H)
        out, sq = by_pair(both), by_pair(turns[0])
        r = att[:, :, :, :].rearrange("p a h c -> p (a h c)").rearrange("p (h t) -> p h t", h=GLA_H)
        sr = v[:, :, :].rearrange("p a c -> p (a c)").rearrange("p (h t) -> p h t", h=GLA_H)
        diag = [state[1][:, 2 * b:2 * b + 2, :, :].rearrange("p c h d -> p (c h d)") for b in range(2)]
        flat = lambda a: a.rearrange("p h t -> p (h t)")
        blocks = lambda a, m: flat(a).rearrange("p (n w) -> p n w", w=2 * m)
        chunks = lambda a: flat(a).rearrange("p (n w) -> p n w", w=CHUNK)
        tok = [(0, 512), (512, 512), (1024, 256)]

        ps = core.ps
        TWOS = PAIRS // 2
        TWO = [(a, h) for a in range(2) for h in range(GLA_H)]
        slot = lambda bank, a, h: ps[:, bank, (2 * a + h // 2) * P:(2 * a + h // 2 + 1) * P]
        spread = lambda bank: ps[:, bank, :].rearrange("p (a h t) -> p a h t", a=2, h=2)

        names = ("in_lora in_qk in_v in_mask in_r lora_z z_read z_abs z_exp z_ln g_done scan_done reset_done lvl_df lvl_db "
                 "lvl_exp lvl_q lvl_k lvl_mm lvl_read att_zero q_scaled dk_f dk_b dk_exp dk_kf dk_kb kt_tr kt_read "
                 "dec_done q_f q_b q_exp ds_mm s_step out_mm out_read sq_done ss_mm ms_done rt_done bc_mm bc_read diag_done "
                 "r_sig r_silu final stored ones_done")
        S = {n: core.sem("g_s_" + n) for n in names.split()}
        chain = Chain(core.sem("g_chain"), 0)
        NL = len(LEVELS)
        ENDS = ((SEAM - 1, NCH - 1), (0, SEAM))
        FIRSTS = ((0, SEAM), (NCH - 1, SEAM - 1))
        steps = [[(d, c) for d, c in ((0, n), (1, NCH - 1 - n)) if c not in ENDS[d]] for n in range(NCH)]
        states_by = [HP * sum(map(len, steps[:n])) for n in range(NCH + 1)]
        block = mem.enter_context(nc.Block())

        @block.sync
        def _(sp):
            sp.dma_start(lora, core.fm[T_LORA, 0:2 * LORA, :]).then_inc(S["in_lora"], 16)
            sp.dma_start(w_lora[:, :, :, :], io["w_lora"]).then_inc(S["in_lora"], 16)
            sp.dma_start(bias[:, :, :], io["b_lora"]).then_inc(S["in_lora"], 16)
            sp.dma_start(gain[:, :], io["gla_norm"]).then_inc(S["in_lora"], 16)
            sp.dma_start(q[:, :, :], core.fm[T_LQ:T_LQ + 2].rearrange("h p t -> p h t")).then_inc(S["in_qk"], 16)
            sp.dma_start(k[:, :, :], core.fm[T_LK:T_LK + 2].rearrange("h p t -> p h t")).then_inc(S["in_qk"], 16)
            sp.dma_start(mask[:, :, :], io["level_masks"]).then_inc(S["in_mask"], 16)
            for n in range(2):
                sp.dma_start(v[:, :, n * WB:(n + 1) * WB], core.tm[3 + n].rearrange("t p c -> p t c")).then_inc(S["in_v"], 16)
            sp.wait_ge(S["out_mm"], TWOS)
            sp.dma_start(r, core.fm[T_LR:T_LR + GLA_H].rearrange("h p t -> p h t")).then_inc(S["in_r"], 16)
            sp.wait_ge(S["final"], PAIRS)
            for h in range(GLA_H):
                sp.dma_start(core.up_in[KT // 2 + h].rearrange("p (a c) -> p a c", c=P), out[:, :, h, :]).then_inc(S["stored"], 16)
            sp.wait_ge(S["stored"], 16 * GLA_H)

        @block.tensor
        def _(pe):
            pe.wait_ge(S["in_lora"], 64)
            for u in range(2 * HP):
                d, h = divmod(u, HP)
                if u >= 2:
                    pe.wait_ge(S["z_read"], u - 1)
                for n, (at, w) in enumerate(tok):
                    last = pe.matmul(ps[:, 3 * (u % 2) + n, 0:w], w_lora[:, d, h, :], lora[:, at:at + w], start=True, stop=True)
                last.then_inc(S["lora_z"], 1)
            pe.wait_ge(S["z_read"], 2 * HP)
            for l in range(NL + 1):
                if l < NL:
                    pe.wait_ge(S["lvl_q"], l + 1)
                    pe.wait_ge(S["lvl_k"], l + 1)
                    qq, kk = ql[l % 2], kl[l % 2]
                else:
                    qq, kk = q, k
                for n in range(TWOS):
                    use = l * TWOS + n
                    if use >= 2:
                        pe.wait_ge(S["lvl_read"], 2 * (use - 1))
                    for a, h in TWO:
                        rows, t = slice((h % 2) * DK, (h % 2 + 1) * DK), slice((2 * n + a) * P, (2 * n + a + 1) * P)
                        last = pe.matmul(slot(2 * (use % 2) + h % 2, a, h), kk[rows, h // 2, t], qq[rows, h // 2, t],
                                         start=True, stop=True)
                    last.then_inc(S["lvl_mm"], 1)
            for d in range(2):
                pe.wait_ge(S["dk_kf" if d == 0 else "dk_kb"], 1)
                for n in range(PAIRS * HP // 4):
                    use = d * (PAIRS * HP // 4) + n
                    if use >= 4:
                        pe.wait_ge(S["kt_read"], use - 3)
                    for m in range(4):
                        a, h = divmod(n * 4 + m, HP)
                        last = pe.transpose(ps[:, 4 + use % 4, m * P:(m + 1) * P], (kl[0] if d == 0 else ql[0])[:, h, a * P:(a + 1) * P],
                                            core.ident[:, :])
                    last.then_inc(S["kt_tr"], 1)
            pe.wait_ge(S["kt_read"], 2 * (PAIRS * HP // 4))
            pe.wait_ge(S["lvl_read"], 2 * (NL + 1) * TWOS)
            pe.wait_ge(S["in_v"], 32)
            for n in range(NCH):
                if n >= 2:
                    pe.wait_ge(S["s_step"], states_by[n - 1])
                if not steps[n]:
                    continue
                for d, c in steps[n]:
                    rows = slice((c % 2) * CHUNK, (c % 2 + 1) * CHUNK)
                    for h in range(GLA_H):
                        o = (h % 2) * DK
                        last = pe.matmul(ps[o:o + DK, 2 * (n % 2) + d, (h // 2) * DV:(h // 2 + 1) * DV],
                                         kt[d][rows, c // 2, h // 2, o:o + DK], v[rows, c // 2, h * DV:(h + 1) * DV],
                                         start=True, stop=True, skip_group_check=True)
                last.then_inc(S["ds_mm"], 1)
            pe.wait_ge(S["s_step"], states_by[NCH])
            pe.wait_ge(S["q_f"], 1)
            pe.wait_ge(S["q_b"], 1)
            for n in range(TWOS):
                if n >= 2:
                    pe.wait_ge(S["out_read"], 2 * (n - 1))
                for pair, h in TWO:
                    a = 2 * n + pair
                    rows = slice((h % 2) * DK, (h % 2 + 1) * DK)
                    o = slot(4 + 2 * (n % 2) + h % 2, pair, h)
                    terms = []
                    for j in range(2):
                        c = 2 * a + j
                        cols, t = slice(j * CHUNK, (j + 1) * CHUNK), slice(c * CHUNK, (c + 1) * CHUNK)
                        if c not in (0, SEAM):
                            terms.append((o[:, cols], state[0][rows, c, h // 2, :], ql[1][rows, h // 2, t]))
                        if c not in (SEAM - 1, NCH - 1):
                            terms.append((o[:, cols], state[1][rows, c, h // 2, :], kl[1][rows, h // 2, t]))
                    pe.matmul(o, v[:, a, h * DV:(h + 1) * DV], att[:, a, h, :], start=True, stop=False, skip_group_check=True)
                    for m, (dst, lhs, rhs) in enumerate(terms):
                        last = pe.matmul(dst, lhs, rhs, start=False, stop=(m == len(terms) - 1), skip_group_check=True)
                last.then_inc(S["out_mm"], 1)
            pe.wait_ge(S["ones_done"], 1)
            for a in range(PAIRS):
                pe.wait_ge(S["sq_done"], a + 1)
                for h in range(GLA_H):
                    last = pe.matmul(ps[:, 0, a * GLA_H + h:a * GLA_H + h + 1], sq[:, a, h, :], ones[:, 0:1], start=True, stop=True)
            last.then_inc(S["ss_mm"], 1)
            for a in range(PAIRS):
                pe.wait_ge(S["diag_done"], a + 1)
                if a >= 2:
                    pe.wait_ge(S["bc_read"], a - 1)
                pe.matmul(ps[:, 2 + a % 2, :], ones[:, :], diag[a % 2], start=True, stop=True).then_inc(S["bc_mm"], 1)

        @block.scalar
        def _(act):
            for u in range(2 * HP):
                d, h = divmod(u, HP)
                act.wait_ge(S["z_read"], u + 1)
                act.activation(lg[d][:, h, :], z[d][:, h, :], ACT.Abs).then_inc(S["z_abs"], 1)
            for u in range(2 * HP):
                d, h = divmod(u, HP)
                act.wait_ge(S["z_abs"], u + 1)
                act.activation(lg[d][:, h, :], lg[d][:, h, :], ACT.Exp, scale=-1.0).then_inc(S["z_exp"], 1)
            for u in range(2 * HP):
                d, h = divmod(u, HP)
                act.wait_ge(S["z_exp"], u + 1)
                act.activation(lg[d][:, h, :], lg[d][:, h, :], ACT.Ln, bias=1.0).then_inc(S["z_ln"], 1)
            g = 1.0 / GATE_NORM
            for l, m in enumerate(LEVELS):
                b = l % 2
                if l >= 2:
                    act.wait_ge(S["lvl_mm"], (l - 1) * TWOS)
                else:
                    act.wait_ge(S["scan_done"], 2)
                act.wait_ge(S["lvl_df"], l + 1)
                df, db, qb, kb = (blocks(x, m) for x in (diff[0], diff[1], ql[b], kl[b]))
                act.activation(qb[:, :, m:2 * m], df[:, :, m:2 * m], ACT.Exp, scale=g)
                act.activation(kb[:, :, 0:m], df[:, :, 0:m], ACT.Exp, scale=-g)
                act.wait_ge(S["lvl_db"], l + 1)
                act.activation(qb[:, :, 0:m], db[:, :, 0:m], ACT.Exp, scale=g)
                act.activation(kb[:, :, m:2 * m], db[:, :, m:2 * m], ACT.Exp, scale=-g).then_inc(S["lvl_exp"], 1)
            act.wait_ge(S["dk_f"], 1)
            act.wait_ge(S["lvl_mm"], (NL - 1) * TWOS)
            act.activation(kl[0][:, :, :], diff[0][:, :, :], ACT.Exp, scale=-g)
            act.wait_ge(S["dk_b"], 1)
            act.activation(ql[0][:, :, :], diff[1][:, :, :], ACT.Exp, scale=-g).then_inc(S["dk_exp"], 1)
            act.activation(decay[:, 0, :, :], bcum[:, 0, :, CHUNK - 1::CHUNK], ACT.Exp, scale=g)
            act.activation(decay[:, 1, :, :], bcum[:, 1, :, 0::CHUNK], ACT.Exp, scale=g).then_inc(S["dec_done"], 1)
            act.wait_ge(S["lvl_mm"], NL * TWOS)
            act.activation(ql[1][:, :, :], bcum[:, 0, :, :], ACT.Exp, scale=g)
            act.activation(kl[1][:, :, :], bcum[:, 1, :, :], ACT.Exp, scale=g).then_inc(S["q_exp"], 1)
            n_kt = PAIRS * HP // 4
            for use in range(2 * n_kt):
                d, n = divmod(use, n_kt)
                act.wait_ge(S["kt_tr"], use + 1)
                act.activation(kt[d].rearrange("p a h c -> p (a h c)")[:, n * 512:(n + 1) * 512], ps[:, 4 + use % 4, :],
                               ACT.Copy).then_inc(S["kt_read"], 1)
            for a in range(PAIRS):
                act.wait_ge(S["out_read"], 2 * (a // 2 + 1))
                act.activation(sq[:, a, :, :], out[:, a, :, :], ACT.Square).then_inc(S["sq_done"], 1)
            act.wait_ge(S["in_r"], 16)
            act.activation(sr, r, ACT.Sigmoid).then_inc(S["r_sig"], 1)
            act.wait_ge(S["ms_done"], 1)
            act.activation(stat[:, 2, :], stat[:, 1, :], ACT.Sqrt).then_inc(S["rt_done"], 1)

        @block.vector
        def _(dve):
            link = lambda ins: chain.link(dve, ins)
            dve.memset(ones[:, :], 1.0).then_inc(S["ones_done"], 1)
            dve.memset(att[:, :, :, :].bitcast(U32), 0).then_inc(S["att_zero"], 1)
            link(dve.memset(reset, 1.0))
            link(dve.memset(reset[:, 0::CHUNK], 0.0))
            for u in range(2 * HP):
                d, h = divmod(u, HP)
                dve.wait_ge(S["in_lora"], 64)
                dve.wait_ge(S["lora_z"], u + 1)
                b = 3 * (u % 2)
                dve.tensor_scalar(z[d][:, h, 0:1024], ps[:, b:b + 2, :].rearrange("p a c -> p (a c)"), bias[:, d, h:h + 1], None, ALU.add)
                dve.tensor_scalar(z[d][:, h, 1024:T], ps[:, b + 2, 0:256], bias[:, d, h:h + 1], None, ALU.add).then_inc(S["z_read"], 1)
            dve.wait_ge(S["in_qk"], 32)
            dve.tensor_scalar(q[:, :, :], q[:, :, :], DK ** -0.5, None, ALU.mult).then_inc(S["q_scaled"], 1)
            for d in range(2):
                dve.wait_ge(S["z_ln"], HP * (d + 1))
                link(dve.scalar_tensor_tensor(flat(z[d]), flat(z[d]), 0.0, flat(lg[d]), ALU.min, ALU.subtract))
            fwd, bwd = (flat(bcum[:, d, :, :]) for d in range(2))
            dve.tensor_tensor_scan(fwd, reset[:, 0:FLAT], flat(z[0]), 0.0, ALU.mult, ALU.add).then_inc(S["scan_done"], 1)
            dve.tensor_tensor_scan(bwd[:, ::-1], reset[:, 1:FLAT + 1][:, ::-1], flat(z[1])[:, ::-1], 0.0, ALU.mult,
                                   ALU.add).then_inc(S["scan_done"], 1)
            dve.wait_ge(S["scan_done"], 2)
            dve.wait_ge(S["in_mask"], 16)

            def gather(l):
                for n in range(TWOS):
                    use = l * TWOS + n
                    dve.wait_ge(S["lvl_mm"], use + 1)
                    for par in range(2):
                        dve.copy_predicated(att[:, 2 * n:2 * n + 2, par::2, :],
                                            mask[:, l, :].unsqueeze(1).unsqueeze(1).broadcast_to((P, 2, 2, P)),
                                            spread(2 * (use % 2) + par)).then_inc(S["lvl_read"], 1)

            bf, bb = bcum[:, 0, :, :], bcum[:, 1, :, :]
            for l, m in enumerate(LEVELS):
                if l:
                    dve.wait_ge(S["lvl_exp"], l)
                seam = blocks(bf, m)[:, :, m - 1:m].broadcast_to((P, FLAT // (2 * m), 2 * m))
                dve.tensor_tensor(blocks(diff[0], m), blocks(bf, m), seam, ALU.subtract).then_inc(S["lvl_df"], 1)
                dve.wait_ge(S["lvl_exp"], l + 1)
                dve.wait_ge(S["q_scaled"], 1)
                dve.tensor_tensor(flat(ql[l % 2]), flat(ql[l % 2]), flat(q), ALU.mult).then_inc(S["lvl_q"], 1)
                if l:
                    gather(l - 1)
            last = chunks(bf)[:, :, CHUNK - 1:CHUNK].broadcast_to((P, HP * NCH, CHUNK))
            dve.tensor_tensor(chunks(diff[0]), chunks(bf), last, ALU.subtract).then_inc(S["dk_f"], 1)
            gather(NL - 1)
            dve.wait_ge(S["dk_exp"], 1)
            dve.tensor_tensor(flat(kl[0]), flat(kl[0]), flat(k), ALU.mult).then_inc(S["dk_kf"], 1)
            gather(NL)
            dve.wait_ge(S["q_exp"], 1)
            dve.tensor_tensor(flat(ql[1]), flat(ql[1]), flat(q), ALU.mult).then_inc(S["q_f"], 1)
            dve.wait_ge(S["dec_done"], 1)
            for n in range(NCH):
                dve.wait_ge(S["ds_mm"], sum(map(bool, steps[:n + 1])))
                if n:
                    dve.wait_ge(S["s_step"], states_by[n])
                for d, c in steps[n]:
                    to = c + 1 if d == 0 else c - 1
                    for h in range(HP):
                        add = ps[:, 2 * (n % 2) + d, h * DV:(h + 1) * DV]
                        if c in FIRSTS[d]:
                            dve.tensor_copy(state[d][:, to, h, :], add).then_inc(S["s_step"], 1)
                        else:
                            dve.scalar_tensor_tensor(state[d][:, to, h, :], state[d][:, c, h, :], decay[:, d, h, c:c + 1], add,
                                                     ALU.mult, ALU.add).then_inc(S["s_step"], 1)
            for n in range(TWOS):
                dve.wait_ge(S["out_mm"], n + 1)
                for par in range(2):
                    dve.tensor_copy(out[:, 2 * n:2 * n + 2, par::2, :], spread(4 + 2 * (n % 2) + par)).then_inc(S["out_read"], 1)
            dve.wait_ge(S["ss_mm"], 1)
            s = lambda n: stat[:, n, :]
            dve.tensor_scalar(s(1), ps[:, 0, 0:PAIRS * GLA_H], 1.0 / DV, EPS, ALU.mult, ALU.add).then_inc(S["ms_done"], 1)
            dve.wait_ge(S["rt_done"], 1)
            link(dve.reciprocal(s(3), s(2)))
            newton(dve, chain, s(3), s(1), s(2))

            def final(a):
                o = out[:, a, :, :].rearrange("p h t -> p (h t)")
                dve.wait_ge(S["bc_mm"], a + 1)
                dve.scalar_tensor_tensor(o, o, gain[:, 0:1], ps[:, 2 + a % 2, :], ALU.mult, ALU.mult).then_inc(S["bc_read"], 1)
                dve.wait_ge(S["bc_read"], a + 1)
                dve.wait_ge(S["r_silu"], 1)
                dve.tensor_tensor(out[:, a, :, :], out[:, a, :, :], sr[:, :, a * P:(a + 1) * P], ALU.mult).then_inc(S["final"], 1)

            for a in range(PAIRS):
                if a >= 2:
                    dve.wait_ge(S["bc_mm"], a - 1)
                dve.tensor_tensor(diag[a % 2].rearrange("p (h t) -> p h t", h=GLA_H),
                                  core.ident[:, :].unsqueeze(1).broadcast_to((P, GLA_H, P)),
                                  stat[:, 3, a * GLA_H:(a + 1) * GLA_H].unsqueeze(2).broadcast_to((P, GLA_H, P)),
                                  ALU.mult).then_inc(S["diag_done"], 1)
                if a:
                    final(a - 1)
            final(PAIRS - 1)

        @block.gpsimd
        def _(pool):
            bb = bcum[:, 1, :, :]
            pool.wait_ge(S["in_qk"], 32)
            pool.wait_ge(S["scan_done"], 2)
            for l, m in enumerate(LEVELS):
                if l:
                    pool.wait_ge(S["lvl_exp"], l)
                seam = blocks(bb, m)[:, :, m:m + 1].broadcast_to((P, FLAT // (2 * m), 2 * m))
                pool.tensor_tensor(blocks(diff[1], m), blocks(bb, m), seam, ALU.subtract).then_inc(S["lvl_db"], 1)
                pool.wait_ge(S["lvl_exp"], l + 1)
                pool.tensor_tensor(flat(kl[l % 2]), flat(kl[l % 2]), flat(k), ALU.mult).then_inc(S["lvl_k"], 1)
            first = chunks(bb)[:, :, 0:1].broadcast_to((P, HP * NCH, CHUNK))
            pool.tensor_tensor(chunks(diff[1]), chunks(bb), first, ALU.subtract).then_inc(S["dk_b"], 1)
            pool.wait_ge(S["dk_exp"], 1)
            pool.tensor_tensor(flat(ql[0]), flat(ql[0]), flat(k), ALU.mult).then_inc(S["dk_kb"], 1)
            pool.wait_ge(S["q_exp"], 1)
            pool.wait_ge(S["q_scaled"], 1)
            pool.tensor_tensor(flat(kl[1]), flat(kl[1]), flat(q), ALU.mult).then_inc(S["q_b"], 1)
            pool.wait_ge(S["r_sig"], 1)
            pool.tensor_tensor(sr, sr, r, ALU.mult).then_inc(S["r_silu"], 1)


def resident_weights(core, mem, tag, parts, stage_bufs):
    nc = core.nc
    kts = [n for n, _ in parts]
    hi = [mem.enter_context(nc.sbuf_tensor(f"{tag}_hi{n}", [P, k, D], F32R)) for n, (k, _) in enumerate(parts)]
    lo = [mem.enter_context(nc.sbuf_tensor(f"{tag}_lo{n}", [P, k, D], F32R)) for n, (k, _) in enumerate(parts)]
    w_in, w_hi, w_lo = (core.sems(f"{tag}_{x}", 2) for x in ("w_in", "w_hi", "w_lo"))
    blocks = [(n, c) for n in range(len(parts)) for c in range(D // WB)]

    def load(eng):
        for u, (n, c) in enumerate(blocks):
            if u >= 2:
                eng.wait_ge(w_lo[u % 2], u // 2)
            eng.dma_start(stage_bufs[u % 2][:, 0:kts[n], :], parts[n][1](c)).then_inc(w_in[u % 2], 16)

    def high(act):
        for u, (n, c) in enumerate(blocks):
            act.wait_ge(w_in[u % 2], 16 * (u // 2 + 1))
            act.activation(hi[n][:, :, c * WB:(c + 1) * WB], stage_bufs[u % 2][:, 0:kts[n], :], ACT.Copy).then_inc(w_hi[u % 2], 1)

    def low(dve):
        for u, (n, c) in enumerate(blocks):
            dve.wait_ge(w_hi[u % 2], u // 2 + 1)
            cols = slice(c * WB, (c + 1) * WB)
            dve.tensor_tensor(lo[n][:, :, cols], stage_bufs[u % 2][:, 0:kts[n], :], hi[n][:, :, cols].bitcast(F32),
                              ALU.subtract).then_inc(w_lo[u % 2], 1)

    def ready(pe):
        for b in range(2):
            pe.wait_ge(w_lo[b], len(blocks) // 2)

    return hi, lo, load, high, low, ready


def stage_merge(core, aff):
    nc, io = core.nc, core.io
    with ExitStack() as mem:
        sb = lambda name, shape, dt=F32: mem.enter_context(nc.sbuf_tensor(name, shape, dt))
        x = sb("m_x", [P, KT, CW])
        res = sb("m_res", [P, 2, D])
        kcols = lambda w, c: w.rearrange("(k p) n -> p k n", p=P)[:, :, c * WB:(c + 1) * WB]
        wh, wl, load_w, high_w, low_w, ready_w = resident_weights(
            core, mem, "m", [(KT, lambda c: kcols(io["w_up"], c)), (KT, lambda c: kcols(io["w_out"], c))],
            [x, res[:, :, :].rearrange("p b d -> p (b d)").rearrange("p (k c) -> p k c", k=KT)])
        xh, xl = sb("m_xh", [P, KT, CW], F32R), sb("m_xl", [P, KT, CW], F32R)
        mh, ml = sb("m_mh", [P, KT, CW], F32R), sb("m_ml", [P, KT, CW], F32R)
        GS = 4
        gates = sb("m_gates", [P, GS, 2, CW])
        xn = sb("m_xn", [P, 2, D])
        xt = sb("m_xt", [P, D])
        g = sb("m_gain", [P, D])
        w_r = sb("m_w_r", [P, KT, E])
        st = sb("m_stat", [P, 2, 8])
        lg = sb("m_lg", [P, 2, 2, E])
        one = lambda names: {n: core.sem("m_s_" + n) for n in names.split()}
        two = lambda names: {n: core.sems("m_s_" + n, 2) for n in names.split()}
        S = one("const x_in xh xl mlo")
        S2 = two("up prod sum mhi res_in out x1 sq ms rt xn x1_out xn_out tr xt rt_mm nmax ex aff aff_tr aff_out")
        g_in = core.sems("m_s_g_in", GS)
        chain = [Chain(core.sem(f"m_chain{b}"), 1 + NEWTON) for b in range(2)]
        chain2 = [Chain(core.sem(f"m_chain_r{b}"), 1) for b in range(2)]
        ps = core.ps
        LAST = CHUNKS - 1
        FT = KT
        block = mem.enter_context(nc.Block())

        @block.sync
        def _(sp):
            load_w(sp)
            sp.dma_start(g[:, :], io["g_moe"].partition_broadcast(P)).then_inc(S["const"], 16)
            sp.dma_start(w_r[:, :, :], io["w_router"].rearrange("(k p) n -> p k n", p=P)).then_inc(S["const"], 16)

            ready_w(sp)
            with sp.Fori(0, CHUNKS) as c:
                cols = ds(c * CW, CW)
                sp.wait_ge(S["xl"], c)
                sp.dma_start(x[:, :, :], core.up_in[:, :, cols].rearrange("k p t -> p k t")).then_inc(S["x_in"], 16)
                for ft in range(FT):
                    sp.wait_ge(S["mlo"], c * FT + (ft - GS + 1 if ft >= GS else 0))
                    for h in range(2):
                        sp.dma_start(gates[:, ft % GS, h, :], core.fm[T_GA + h * FT + ft, :, cols]).then_inc(g_in[ft % GS], 16)

        @block.gpsimd
        def _(pool):
            def load_res(c):
                for b in range(2):
                    pool.wait_ge(S2["x1_out"][b], c * 16)
                    pool.wait_ge(S2["xn"][b], c)
                    pool.nop(nofuse=True)
                    pool.dma_start(res[:, b, :], io["x"][ds(c * CW + b * P, P), :]).then_inc(S2["res_in"][b], 16)

            def store(c):
                for b in range(2):
                    rows = ds(c * CW + b * P, P)
                    pool.wait_ge(S2["x1"][b], c + 1)
                    pool.nop(nofuse=True)
                    pool.dma_start(core.x_res[rows, :], res[:, b, :]).then_inc(S2["x1_out"][b], 16)
                    pool.wait_ge(S2["xn"][b], c + 1)
                    pool.nop(nofuse=True)
                    pool.dma_start(core.xm[rows, :], xn[:, b, :]).then_inc(S2["xn_out"][b], 16)

            ready_w(pool)
            with pool.Fori(0, CHUNKS) as c:
                load_res(c)
                store(c)
            for b in range(2):
                pool.wait_ge(S2["x1_out"][b], 16 * CHUNKS)
                pool.wait_ge(S2["xn_out"][b], 16 * CHUNKS)

        def walk(split, up, tail, out, late, loop):
            split(0)
            up(0)
            split(1)
            out(0)
            with loop(1, LAST) as c:
                up(c)
                tail(c - 1)
                split(c + 1)
                out(c)
                late(c - 1)
            up(LAST)
            tail(LAST - 1)
            out(LAST)
            late(LAST - 1)
            tail(LAST)
            late(LAST)

        @block.tensor
        def _(pe):
            ready_w(pe)
            pe.wait_ge(S["const"], 32)

            def split(c):
                pass

            def up(c):
                pe.wait_ge(S["xl"], c + 1)
                for ft in range(FT):
                    b, use = ft % 2, c * (FT // 2) + ft // 2
                    pe.wait_ge(S2["prod"][b], use)
                    cols = slice(ft * P, (ft + 1) * P)
                    for part in range(2):
                        for k in range(4):
                            kk = 4 * part + k
                            last = split3(pe, ps[:, b, part * CW:(part + 1) * CW], (wh[0][:, kk, cols], wl[0][:, kk, cols]),
                                          (xh[:, kk, :], xl[:, kk, :]), k == 0, k == 3)
                    last.then_inc(S2["up"][b], 1)

            def out(c):
                for b in range(2):
                    pe.wait_ge(S["mlo"], FT * (c + 1))
                    pe.wait_ge(S2["x1"][b], c)
                    pe.wait_ge(S2["xt"][b], c)
                    for n in range(2):
                        for k in range(KT):
                            rows, cols = slice(b * P, (b + 1) * P), slice(n * 512, (n + 1) * 512)
                            last = split3(pe, ps[:, 2 + 2 * b + n, :], (mh[:, k, rows], ml[:, k, rows]),
                                          (wh[1][:, k, cols], wl[1][:, k, cols]), k == 0, k == KT - 1)
                    last.then_inc(S2["out"][b], 1)

            def tail(c):
                for b in range(2):
                    pe.wait_ge(S2["xn"][b], c + 1)
                    for k in range(KT):
                        last = pe.transpose(ps[:, 2 + 2 * b + k // 4, (k % 4) * P:(k % 4 + 1) * P], xn[:, b, k * P:(k + 1) * P],
                                            core.ident[:, :])
                    last.then_inc(S2["tr"][b], 1)
                for b in range(2):
                    pe.wait_ge(S2["xt"][b], c + 1)
                    pe.wait_ge(S2["aff_out"][b], c)
                    for k in range(KT):
                        last = pe.matmul(ps[:, 6 + b, 0:E], xt[:, k * P:(k + 1) * P], w_r[:, k, :], start=(k == 0), stop=(k == KT - 1))
                    last.then_inc(S2["rt_mm"][b], 1)

            def late(c):
                for b in range(2):
                    pe.wait_ge(S2["aff"][b], c + 1)
                    pe.transpose(ps[0:E, 6 + b, P:2 * P], lg[:, b, 1, :], core.ident[:, :]).then_inc(S2["aff_tr"][b], 1)

            walk(split, up, tail, out, late, pe.Fori)

        @block.scalar
        def _(act):
            high_w(act)

            def split(c):
                act.wait_ge(S["x_in"], c * 16 + 16)
                act.wait_ge(S2["up"][1], c * (FT // 2))
                act.activation(xh[:, :, :], x[:, :, :], ACT.Copy).then_inc(S["xh"], 1)

            def up(c):
                for ft in range(FT):
                    b, use = ft % 2, c * (FT // 2) + ft // 2
                    act.wait_ge(S2["sum"][b], use + 1)
                    if ft == 0:
                        act.wait_ge(S2["out"][1], c)
                    act.activation(mh[:, ft, :], gates[:, ft % GS, 0, :], ACT.Copy).then_inc(S2["mhi"][b], 1)

            def out(c):
                for b in range(2):
                    act.wait_ge(S2["x1"][b], c + 1)
                    act.wait_ge(S2["xn_out"][b], c * 16)
                    act.wait_ge(S2["tr"][b], c)
                    act.activation(xn[:, b, :], res[:, b, :], ACT.Square, accum_out=st[:, b, 0:1]).then_inc(S2["sq"][b], 1)
                    act.wait_ge(S2["ms"][b], c + 1)
                    act.activation(st[:, b, 2:3], st[:, b, 1:2], ACT.Sqrt).then_inc(S2["rt"][b], 1)

            def tail(c):
                for b in range(2):
                    act.wait_ge(S2["tr"][b], c + 1)
                    act.wait_ge(S2["rt_mm"][1 - b], c + b)
                    act.activation(xt[:, :].rearrange("p (a n) -> p a n", a=2), ps[:, 2 + 2 * b:4 + 2 * b, :], ACT.Copy).then_inc(S2["xt"][b], 1)
                for b in range(2):
                    act.wait_ge(S2["nmax"][b], c + 1)
                    act.activation(lg[:, b, 0, :], ps[:, 6 + b, 0:E], ACT.Exp, bias=st[:, b, 4:5], accum_out=st[:, b, 5:6]).then_inc(S2["ex"][b], 1)

            def late(c):
                for b in range(2):
                    act.wait_ge(S2["aff_tr"][b], c + 1)
                    act.activation(aff[:, ds(c * CW + b * P, P)], ps[0:E, 6 + b, P:2 * P], ACT.Copy).then_inc(S2["aff_out"][b], 1)

            walk(split, up, tail, out, late, act.Fori)

        @block.vector
        def _(dve):
            low_w(dve)
            dve.wait_ge(S["const"], 32)

            def split(c):
                dve.wait_ge(S["xh"], c + 1)
                dve.tensor_tensor(xl[:, :, :], x[:, :, :], xh[:, :, :].bitcast(F32), ALU.subtract).then_inc(S["xl"], 1)

            def up(c):
                for ft in range(FT):
                    b, use = ft % 2, c * (FT // 2) + ft // 2
                    s = ft % GS
                    dve.wait_ge(S2["up"][b], use + 1)
                    dve.wait_ge(g_in[s], 32 * (c * (FT // GS) + ft // GS + 1))
                    both = gates[:, s, :, :].rearrange("p a t -> p (a t)")
                    dve.tensor_tensor(both, ps[:, b, :], both, ALU.mult).then_inc(S2["prod"][b], 1)
                    dve.wait_ge(S2["prod"][b], use + 1)
                    dve.tensor_tensor(gates[:, s, 0, :], gates[:, s, 0, :], gates[:, s, 1, :], ALU.add).then_inc(S2["sum"][b], 1)
                    if ft:
                        low(c, ft - 1)
                low(c, FT - 1)

            def low(c, ft):
                b, use = ft % 2, c * (FT // 2) + ft // 2
                dve.wait_ge(S2["mhi"][b], use + 1)
                dve.tensor_tensor(ml[:, ft, :], gates[:, ft % GS, 0, :], mh[:, ft, :].bitcast(F32), ALU.subtract).then_inc(S["mlo"], 1)

            def out(c):
                for b in range(2):
                    s = lambda n: st[:, b, n:n + 1]
                    dve.wait_ge(S2["out"][b], c + 1)
                    dve.wait_ge(S2["res_in"][b], 16 * (c + 1))
                    dve.tensor_tensor(res[:, b, :].rearrange("p (a n) -> p a n", a=2), ps[:, 2 + 2 * b:4 + 2 * b, :],
                                      res[:, b, :].rearrange("p (a n) -> p a n", a=2), ALU.add).then_inc(S2["x1"][b], 1)
                for b in range(2):
                    s = lambda n: st[:, b, n:n + 1]
                    dve.wait_ge(S2["sq"][b], c + 1)
                    dve.tensor_scalar(s(1), s(0), 1.0 / D, EPS, ALU.mult, ALU.add).then_inc(S2["ms"][b], 1)
                    dve.wait_ge(S2["rt"][b], c + 1)
                    chain[b].turn(c)
                    chain[b].link(dve, dve.reciprocal(s(3), s(2)))
                    newton(dve, chain[b], s(3), s(1), s(2))
                    dve.wait_ge(S2["xn_out"][b], 16 * c)
                    dve.wait_ge(S2["tr"][b], c)
                    dve.scalar_tensor_tensor(xn[:, b, :], res[:, b, :], s(3), g[:, :], ALU.mult, ALU.mult).then_inc(S2["xn"][b], 1)

            def tail(c):
                for b in range(2):
                    dve.wait_ge(S2["rt_mm"][b], c + 1)
                    dve.tensor_reduce(st[:, b, 4:5], ps[:, 6 + b, 0:E], AX.X, ALU.max, negate=True).then_inc(S2["nmax"][b], 1)
                for b in range(2):
                    dve.wait_ge(S2["ex"][b], c + 1)
                    chain2[b].turn(c)
                    chain2[b].link(dve, dve.reciprocal(st[:, b, 6:7], st[:, b, 5:6]))
                    dve.wait_ge(S2["aff_tr"][b], c)
                    dve.tensor_scalar(lg[:, b, 1, :], lg[:, b, 0, :], st[:, b, 6:7], None, ALU.mult).then_inc(S2["aff"][b], 1)

            def late(c):
                pass

            walk(split, up, tail, out, late, dve.Fori)


def stage_topk(core, aff, idx_s, idx_p, gate_s, gate_p):
    nc = core.nc
    with ExitStack() as mem:
        sb = lambda name, shape, dt=F32: mem.enter_context(nc.sbuf_tensor(name, shape, dt))
        val = sb("t_val", [E, CAP])
        pos = sb("t_pos", [E, CAP], U32)
        posf = sb("t_posf", [E, CAP])
        chain = Chain(core.sem("t_chain"), 0)
        tr_done, idx_done = core.sem("t_tr_done"), core.sem("t_idx_done")
        ps = core.ps
        block = mem.enter_context(nc.Block())

        @block.vector
        def _(dve):
            link = lambda ins: chain.link(dve, ins)
            for tokens, slots in ((slice(N_SAMPLE, T), slice(CAP_S, CAP)), (slice(0, N_SAMPLE), slice(0, CAP_S))):
                a = aff[:, tokens]
                for n in range(slots.start, slots.stop, 8):
                    v8 = val[:, n:n + 8]
                    link(dve.max(v8, a))
                    chain.step(dve.max_index(pos[:, n:n + 8], v8, a))
                    link(dve.match_replace(a, v8, a, -1.0))
            link(dve.tensor_copy(posf[:, :], pos[:, :]))
            link(dve.tensor_scalar(posf[:, CAP_S:CAP], posf[:, CAP_S:CAP], float(N_SAMPLE), None, ALU.add))
            dve.wait_ge(tr_done, 1)
            dve.tensor_copy(idx_s[:, :], ps[:, 0, 0:E])
            dve.tensor_copy(idx_p[:, :], ps[0:CAP_P, 1, 0:E])
            dve.tensor_copy(gate_s[:, :], ps[:, 2, 0:E])
            dve.tensor_copy(gate_p[:, :], ps[0:CAP_P, 3, 0:E]).then_inc(idx_done, 1)
            dve.wait_ge(idx_done, 1)

        @block.tensor
        def _(pe):
            pe.wait_ge(chain.sem, 3 * (CAP // 8) + 2)
            i16 = core.ident[0:E, 0:E]
            pe.transpose(ps[:, 0, 0:E], posf[:, 0:CAP_S], i16)
            pe.transpose(ps[0:CAP_P, 1, 0:E], posf[:, CAP_S:CAP], i16)
            pe.transpose(ps[:, 2, 0:E], val[:, 0:CAP_S], i16)
            pe.transpose(ps[0:CAP_P, 3, 0:E], val[:, CAP_S:CAP], i16).then_inc(tr_done, 1)


def stage_experts(core, idx_s, idx_p, gate_s, gate_p):
    nc, io = core.nc, core.io
    FB = FF // WB
    FT, DT = FF // P, D // P
    groups = ((0, CAP_S, 0), (1, CAP_P, CAP_S))
    with ExitStack() as mem:
        sb = lambda name, shape, dt=F32: mem.enter_context(nc.sbuf_tensor(name, shape, dt))
        w_gu = [sb(f"e_w_gu{n}", [P, 2, KT, WB]) for n in range(FB)]
        w_d = [sb(f"e_w_d{n}", [P, KT, WB]) for n in range(FB)]
        rows = [sb("e_rows_s", [CAP_S, D]), sb("e_rows_p", [CAP_P, D])]
        x = sb("e_x", [P, KT, CAP])
        h = sb("e_h", [P, KT, CAP])
        sig = sb("e_sig", [P, 2, CAP])
        act_g = sb("e_act", [P, 2, CAP])
        yt = sb("e_yt", [P, 2, CAP])
        y = [sb("e_y_s", [CAP_S, D]), sb("e_y_p", [CAP_P, D])]
        at_get = [sb("e_at_get_s", [CAP_S, 1], U32), sb("e_at_get_p", [CAP_P, 1], U32)]
        at_put = [sb("e_at_put_s", [CAP_S, 1], U32), sb("e_at_put_p", [CAP_P, 1], U32)]
        idx, gate = (idx_s, idx_p), (gate_s, gate_p)
        gu_in, gu_used = core.sems("e_gu_in", FB), core.sems("e_gu_used", FB)
        d_in, d_used = core.sems("e_d_in", FB), core.sems("e_d_used", FB)
        names = "get_ready rows_in x_tr x_read put_ready added y_tr y_read"
        S = {n: core.sem("e_s_" + n) for n in names.split()}
        S2 = {n: core.sems("e_s_" + n, 2) for n in "gu sig silu hid dn dn_read".split()}
        ps = core.ps
        xbanks = [range(0, 3), range(3, 6), range(6, 8)]
        UP_AT = 256
        block = mem.enter_context(nc.Block())

        @block.sync
        def _(sp):
            cols = lambda w, e, n: w[ds(e, 1), :, n * WB:(n + 1) * WB].rearrange("o (k p) c -> (o p) k c", p=P)
            with sp.Fori(0, E) as e:
                for n in range(FB):
                    sp.wait_ge(gu_used[n], e)
                    for m, w in enumerate(("w_gate_e", "w_up_e")):
                        sp.dma_start(w_gu[n][:, m, :, :], cols(io[w], e, n)).then_inc(gu_in[n], 16)
                for n in range(FB):
                    sp.wait_ge(d_used[n], e)
                    sp.dma_start(w_d[n][:, :, :], cols(io["w_down_e"], e, n)).then_inc(d_in[n], 16)

        @block.gpsimd
        def _(pool):
            def gather(e):
                pool.wait_ge(S["x_tr"], e)
                for g, size, _ in groups:
                    pool.tensor_copy(at_get[g][:, :], idx[g][:, ds(e, 1)]).then_inc(S["get_ready"], 1)
                pool.wait_ge(S["get_ready"], e * 2 + 2)
                for g, size, _ in groups:
                    pool.nop(nofuse=True)
                    pool.indirect_dma_start(rows[g][:, :], None, core.xm, bass.IndirectOffsetOnAxis(ap=at_get[g][:, 0:1], axis=0)
                                            ).then_inc(S["rows_in"], 16)

            def add(e):
                pool.wait_ge(S["added"], e * 32)
                for g, size, _ in groups:
                    pool.tensor_copy(at_put[g][:, :], idx[g][:, ds(e, 1)]).then_inc(S["put_ready"], 1)
                pool.wait_ge(S["put_ready"], e * 2 + 2)
                pool.wait_ge(S["y_read"], e * 4 + 4)
                for g, size, _ in groups:
                    pool.nop(nofuse=True)
                    pool.indirect_dma_start(core.x_res, bass.IndirectOffsetOnAxis(ap=at_put[g][:, 0:1], axis=0), y[g][:, :], None,
                                            compute_op=ALU.add).then_inc(S["added"], 16)

            gather(0)
            with pool.Fori(0, E - 1) as e:
                gather(e + 1)
                add(e)
            add(E - 1)
            pool.wait_ge(S["added"], 32 * E)

        @block.tensor
        def _(pe):
            def product(out, w, cols, rhs):
                for k in range(KT):
                    last = pe.matmul(out, w[:, k, cols], rhs[:, k, :], start=(k == 0), stop=(k == KT - 1))
                return last

            with pe.Fori(0, E) as e:
                pe.wait_ge(S["rows_in"], e * 32 + 32)
                pe.wait_ge(S["y_read"], e * 4)
                for n, ks in enumerate(xbanks):
                    for k in ks:
                        for g, size, first in groups:
                            o = (k - ks[0]) * CAP + first
                            last = pe.transpose(ps[:, n, o:o + size], rows[g][:, k * P:(k + 1) * P], core.ident[0:size, 0:size])
                last.then_inc(S["x_tr"], 1)
                pe.wait_ge(S["x_read"], e * 3 + 3)
                for ft in range(FT):
                    b, n = ft % 2, ft // 2
                    if b == 0:
                        pe.wait_ge(gu_in[n], e * 32 + 32)
                    pe.wait_ge(S2["hid"][b], e * (FT // 2) + ft // 2)
                    cols = slice((ft % 2) * P, (ft % 2 + 1) * P)
                    product(ps[:, 3 + b, 0:CAP], w_gu[n][:, 0, :, :], cols, x)
                    last = product(ps[:, 3 + b, UP_AT:UP_AT + CAP], w_gu[n][:, 1, :, :], cols, x)
                    last.then_inc(S2["gu"][b], 1) if b == 0 else last.then_inc(gu_used[n], 1)
                for b in range(2):
                    pe.wait_ge(S2["hid"][b], e * (FT // 2) + FT // 2)

                def turn_back(dt):
                    b = dt % 2
                    pe.wait_ge(S2["dn_read"][b], e * (DT // 2) + dt // 2 + 1)
                    half, o = dt // 4, (dt % 4) * P
                    pe.transpose(ps[:, half, o:o + P], yt[:, b, 0:CAP_S], core.ident[:, :])
                    last = pe.transpose(ps[0:CAP_P, (2, 5)[half], o:o + P], yt[:, b, CAP_S:CAP], core.ident[:, :])
                    if dt % 4 == 3:
                        last.then_inc(S["y_tr"], 1)

                for dt in range(DT):
                    b, n = dt % 2, dt // 2
                    if b == 0:
                        pe.wait_ge(d_in[n], e * 16 + 16)
                    pe.wait_ge(S2["dn_read"][b], e * (DT // 2) + dt // 2)
                    last = product(ps[:, 6 + b, 0:CAP], w_d[n], slice((dt % 2) * P, (dt % 2 + 1) * P), h)
                    last.then_inc(S2["dn"][b], 1) if b == 0 else last.then_inc(d_used[n], 1)
                    if dt:
                        turn_back(dt - 1)
                turn_back(DT - 1)

        def gu_done(eng, e, ft):
            if ft % 2 == 0:
                eng.wait_ge(S2["gu"][0], e * (FT // 2) + ft // 2 + 1)
            else:
                eng.wait_ge(gu_used[ft // 2], e + 1)

        @block.scalar
        def _(act):
            with act.Fori(0, E) as e:
                act.wait_ge(S["x_tr"], e + 1)
                for n, ks in enumerate(xbanks):
                    act.activation(x[:, ks[0]:ks[0] + len(ks), :], ps[:, n, 0:len(ks) * CAP].rearrange("p (k c) -> p k c", c=CAP),
                                   ACT.Copy).then_inc(S["x_read"], 1)
                for ft in range(FT):
                    b = ft % 2
                    gu_done(act, e, ft)
                    act.wait_ge(S2["silu"][b], e * (FT // 2) + ft // 2)
                    act.activation(sig[:, b, :], ps[:, 3 + b, 0:CAP], ACT.Sigmoid).then_inc(S2["sig"][b], 1)
                for dt in range(DT):
                    b = dt % 2
                    if b == 0:
                        act.wait_ge(S2["dn"][0], e * (DT // 2) + dt // 2 + 1)
                    else:
                        act.wait_ge(d_used[dt // 2], e + 1)
                    act.activation(yt[:, b, :], ps[:, 6 + b, 0:CAP], ACT.Copy).then_inc(S2["dn_read"][b], 1)

        @block.vector
        def _(dve):
            with dve.Fori(0, E) as e:
                for ft in range(FT):
                    b = ft % 2
                    dve.wait_ge(S2["sig"][b], e * (FT // 2) + ft // 2 + 1)
                    dve.tensor_tensor(act_g[:, b, :], ps[:, 3 + b, 0:CAP], sig[:, b, :], ALU.mult).then_inc(S2["silu"][b], 1)
                    dve.wait_ge(S2["silu"][b], e * (FT // 2) + ft // 2 + 1)
                    dve.tensor_tensor(h[:, ft, :], ps[:, 3 + b, UP_AT:UP_AT + CAP], act_g[:, b, :], ALU.mult).then_inc(S2["hid"][b], 1)
                dve.wait_ge(S["added"], e * 32)
                for half in range(2):
                    dve.wait_ge(S["y_tr"], e * 2 + half + 1)
                    for g, size, _ in groups:
                        bank = (half, (2, 5)[half])[g]
                        dve.tensor_scalar(y[g][:, half * 512:(half + 1) * 512], ps[0:size, bank, :], gate[g][:, ds(e, 1)], None,
                                          ALU.mult).then_inc(S["y_read"], 1)


def stage_ple(core):
    nc, io = core.nc, core.io
    PT = PLE // P
    with ExitStack() as mem:
        sb = lambda name, shape, dt=F32: mem.enter_context(nc.sbuf_tensor(name, shape, dt))
        x = sb("l_x", [P, 2, D])
        xn = sb("l_xn", [P, 2, D])
        kcols = lambda w, c: w.rearrange("(k p) n -> p k n", p=P)[:, :, c * WB:(c + 1) * WB]
        staging = [a[:, :, :].rearrange("p b d -> p (b d)").rearrange("p (k c) -> p k c", k=KT) for a in (x, xn)]
        wh, wl, load_w, high_w, low_w, ready_w = resident_weights(
            core, mem, "l", [(KT, lambda c: kcols(io["w_ple_gate"], c)), (PT, lambda c: kcols(io["w_ple_proj"], c))], staging)
        g1, g2 = sb("l_gain", [P, D]), sb("l_gain_final", [P, D])
        p = sb("l_p", [P, 2, PLE])
        AT = KT + PT
        th, tl = sb("l_th", [P, 2, AT, P], F32R), sb("l_tl", [P, 2, AT, P], F32R)
        sig = sb("l_sig", [P, 2, D])
        y = sb("l_y", [P, 2, D])
        st = sb("l_stat", [P, 2, 8])
        S = {"const": core.sem("l_s_const")}
        S2 = {n: core.sems("l_s_" + n, 2) for n in "x_in sq ms rt xn tr hi lo gate proj sig mul res sq2 ms2 rt2 y out".split()}
        c1 = [Chain(core.sem(f"l_chain_a{b}"), 1 + NEWTON) for b in range(2)]
        c2 = [Chain(core.sem(f"l_chain_b{b}"), 1 + NEWTON) for b in range(2)]
        ps = core.ps
        tbanks = [range(0, 4), range(4, 8), range(8, AT)]
        H = NT // 2
        block = mem.enter_context(nc.Block())

        def walk(front, back, loop):
            front(0, 0)
            with loop(0, H - 1) as i:
                front(i, 1)
                back(i, 0)
                front(i + 1, 0)
                back(i, 1)
            front(H - 1, 1)
            back(H - 1, 0)
            back(H - 1, 1)

        @block.sync
        def _(sp):
            load_w(sp)
            sp.dma_start(g1[:, :], io["g_ple"].partition_broadcast(P)).then_inc(S["const"], 16)
            sp.dma_start(g2[:, :], io["g_final"].partition_broadcast(P)).then_inc(S["const"], 16)
            ready_w(sp)
            with sp.Fori(0, H) as i:
                for b in range(2):
                    rows = ds(i * 2 * P + b * P, P)
                    sp.wait_ge(S2["res"][b], i)
                    sp.wait_ge(S2["tr"][b], i)
                    sp.dma_start(x[:, b, :], core.x_res[rows, :]).then_inc(S2["x_in"][b], 16)
                    sp.dma_start(p[:, b, :], io["p"][rows, :]).then_inc(S2["x_in"][b], 16)

        @block.gpsimd
        def _(pool):
            with pool.Fori(0, H) as i:
                for b in range(2):
                    pool.wait_ge(S2["y"][b], i + 1)
                    pool.nop(nofuse=True)
                    pool.dma_start(io["out"][ds(i * 2 * P + b * P, P), :], y[:, b, :]).then_inc(S2["out"][b], 16)
            for b in range(2):
                pool.wait_ge(S2["out"][b], 16 * H)

        @block.tensor
        def _(pe):
            ready_w(pe)

            def front(i, b):
                pe.wait_ge(S2["xn"][b], i + 1)
                if b:
                    pe.wait_ge(S2["lo"][0], i + 1)
                else:
                    pe.wait_ge(S2["lo"][1], i)
                for n, ks in enumerate(tbanks):
                    for k in ks:
                        src = xn[:, b, k * P:(k + 1) * P] if k < KT else p[:, b, (k - KT) * P:(k - KT + 1) * P]
                        last = pe.transpose(ps[:, n, (k - ks[0]) * P:(k - ks[0] + 1) * P], src, core.ident[:, :])
                last.then_inc(S2["tr"][b], 1)

            def back(i, b):
                pe.wait_ge(S2["lo"][b], i + 1)
                if b:
                    pe.wait_ge(S2["mul"][0], i + 1)
                else:
                    pe.wait_ge(S2["mul"][1], i)
                for first, n_k, bank, n, done in ((0, KT, 3, 0, "gate"), (KT, PT, 5, 1, "proj")):
                    for half in range(2):
                        cols = slice(half * 512, (half + 1) * 512)
                        for k in range(n_k):
                            last = split3(pe, ps[:, bank + half, :], (th[:, b, first + k, :], tl[:, b, first + k, :]),
                                          (wh[n][:, k, cols], wl[n][:, k, cols]), k == 0, k == n_k - 1)
                    last.then_inc(S2[done][b], 1)

            walk(front, back, pe.Fori)

        @block.scalar
        def _(act):
            high_w(act)

            def front(i, b):
                act.wait_ge(S2["x_in"][b], i * 32 + 32)
                act.wait_ge(S2["y"][b], i)
                act.activation(sig[:, b, :], x[:, b, :], ACT.Square, accum_out=st[:, b, 0:1]).then_inc(S2["sq"][b], 1)
                act.wait_ge(S2["ms"][b], i + 1)
                act.activation(st[:, b, 2:3], st[:, b, 1:2], ACT.Sqrt).then_inc(S2["rt"][b], 1)
                act.wait_ge(S2["tr"][b], i + 1)
                act.wait_ge(S2["proj"][b], i)
                for n, ks in enumerate(tbanks):
                    ins = act.activation(th[:, b, ks[0]:ks[0] + len(ks), :],
                                         ps[:, n, 0:len(ks) * P].rearrange("p (k c) -> p k c", c=P), ACT.Copy)
                ins.then_inc(S2["hi"][b], 1)

            def back(i, b):
                act.wait_ge(S2["gate"][b], i + 1)
                act.activation(sig[:, b, :].rearrange("p (a n) -> p a n", a=2), ps[:, 3:5, :], ACT.Sigmoid).then_inc(S2["sig"][b], 1)
                act.wait_ge(S2["res"][b], i + 1)
                act.activation(sig[:, b, :], y[:, b, :], ACT.Square, accum_out=st[:, b, 4:5]).then_inc(S2["sq2"][b], 1)
                act.wait_ge(S2["ms2"][b], i + 1)
                act.activation(st[:, b, 6:7], st[:, b, 5:6], ACT.Sqrt).then_inc(S2["rt2"][b], 1)

            walk(front, back, act.Fori)

        @block.vector
        def _(dve):
            low_w(dve)
            dve.wait_ge(S["const"], 32)

            def rstd(i, b, chain, at, ms, rt, sq):
                s = lambda n: st[:, b, at + n:at + n + 1]
                dve.wait_ge(S2[sq][b], i + 1)
                dve.tensor_scalar(s(1), s(0), 1.0 / D, EPS, ALU.mult, ALU.add).then_inc(S2[ms][b], 1)
                dve.wait_ge(S2[rt][b], i + 1)
                chain[b].turn(i)
                chain[b].link(dve, dve.reciprocal(s(3), s(2)))
                newton(dve, chain[b], s(3), s(1), s(2))
                return s(3)

            def front(i, b):
                rs = rstd(i, b, c1, 0, "ms", "rt", "sq")
                dve.wait_ge(S2["tr"][b], i)
                dve.scalar_tensor_tensor(xn[:, b, :], x[:, b, :], rs, g1[:, :], ALU.mult, ALU.mult).then_inc(S2["xn"][b], 1)
                dve.wait_ge(S2["hi"][b], i + 1)
                for n, ks in enumerate(tbanks):
                    t = slice(ks[0], ks[0] + len(ks))
                    ins = dve.tensor_tensor(tl[:, b, t, :], ps[:, n, 0:len(ks) * P].rearrange("p (k c) -> p k c", c=P),
                                            th[:, b, t, :].bitcast(F32), ALU.subtract)
                ins.then_inc(S2["lo"][b], 1)

            def back(i, b):
                halves = lambda a: a[:, b, :].rearrange("p (a n) -> p a n", a=2)
                dve.wait_ge(S2["sig"][b], i + 1)
                dve.wait_ge(S2["proj"][b], i + 1)
                dve.wait_ge(S2["out"][b], i * 16)
                dve.tensor_tensor(halves(y), halves(sig), ps[:, 5:7, :], ALU.mult).then_inc(S2["mul"][b], 1)
                dve.wait_ge(S2["mul"][b], i + 1)
                dve.tensor_tensor(y[:, b, :], y[:, b, :], x[:, b, :], ALU.add).then_inc(S2["res"][b], 1)
                rs = rstd(i, b, c2, 4, "ms2", "rt2", "sq2")
                dve.scalar_tensor_tensor(y[:, b, :], y[:, b, :], rs, g2[:, :], ALU.mult, ALU.mult).then_inc(S2["y"][b], 1)

            walk(front, back, dve.Fori)


def program(nc, io, stages=None):
    with ExitStack() as ctx:
        core = Core(nc, ctx, io)
        with ExitStack() as act_mem:
            ah = act_mem.enter_context(nc.sbuf_tensor("act_hi", [P, KT, T], F32R))
            al = act_mem.enter_context(nc.sbuf_tensor("act_lo", [P, KT, T], F32R))
            stage_norm(core, ah, al)
            stage_project(core, ah, al)
        with ExitStack() as att_mem:
            qt = att_mem.enter_context(nc.sbuf_tensor("q_t", [P, HEADS // 2, T], F32))
            kt = att_mem.enter_context(nc.sbuf_tensor("k_t", [P, KV_HEADS, T], F32))
            v = att_mem.enter_context(nc.sbuf_tensor("v_tok", [P, NT, KV_HEADS * HD], F32))
            stage_rope(core, qt, kt, v)
            stage_attention(core, qt, kt, v)
        stage_gla(core)
        core.recycle_sems()
        with ExitStack() as moe_mem:
            sb = lambda name, shape, dt=F32: moe_mem.enter_context(nc.sbuf_tensor(name, shape, dt))
            idx_s, idx_p = sb("idx_s", [CAP_S, E], U32), sb("idx_p", [CAP_P, E], U32)
            gate_s, gate_p = sb("gate_s", [CAP_S, E]), sb("gate_p", [CAP_P, E])
            with ExitStack() as aff_mem:
                aff = aff_mem.enter_context(nc.sbuf_tensor("aff", [E, T], F32))
                stage_merge(core, aff)
                stage_topk(core, aff, idx_s, idx_p, gate_s, gate_p)
            stage_experts(core, idx_s, idx_p, gate_s, gate_p)
        core.recycle_sems()
        stage_ple(core)


def host_inputs(**a):
    import numpy as np

    w = {k: np.asarray(v) for k, v in a.items()}
    out = {"ident": np.eye(P, dtype=np.float32)}
    out["x"] = np.concatenate([w["x_sample"][0], w["x_prompt"][0]])
    out["g_mix"] = w["g_mix"][0]
    for name in ("q_norm", "k_norm", "w_router", "w_gate_e", "w_up_e", "w_down_e", "w_out", "w_ple_gate", "w_ple_proj",
                 "g_moe", "g_ple"):
        out[name] = w[name][0]
    out["g_final"] = w["g_final"]
    out["w_up"] = np.concatenate([w["w_attn_up"][0], w["w_gla_up"][0]])
    out["p"] = np.concatenate([w["p_sample"][0, 0], w["p_prompt"][0, 0]])
    inv = (np.float32(10000.0) ** (-np.arange(0, 32, 2, dtype=np.float32) / np.float32(32))).astype(np.float32)
    pos = np.concatenate([np.arange(N_SAMPLE), np.arange(N_PROMPT)])
    row, col = ((n.astype(np.float32)[:, None] * inv).astype(np.float32) for n in (pos // 64, pos % 64))
    cos = np.concatenate([np.cos(a) for a in (row, row, col, col)], axis=1)
    sin = np.concatenate([-np.sin(row), np.sin(row), -np.sin(col), np.sin(col)], axis=1)
    out["rope"] = np.stack([cos, sin], axis=1).astype(np.float32).reshape(NT, P, 2, HD)
    lora_w = np.zeros((2 * LORA, 2, GLA_HP, P), np.float32)
    lora_w[:LORA, 0] = w["w_af"][0].reshape(LORA, GLA_HP, P)
    lora_w[LORA:, 1] = w["w_ab"][0].reshape(LORA, GLA_HP, P)
    out["w_lora"] = lora_w
    out["b_lora"] = np.ascontiguousarray(np.stack([w["b_af"][0], w["b_ab"][0]]).reshape(2, GLA_HP, P).transpose(2, 0, 1))
    out["gla_norm"] = w["gla_norm"][0].reshape(DV, 1)
    s_, t_ = np.arange(P)[:, None], np.arange(P)[None, :]
    masks = [(s_ // (2 * m) == t_ // (2 * m)) & (s_ // m != t_ // m) for m in LEVELS] + [s_ == t_]
    out["level_masks"] = np.ascontiguousarray(np.stack(masks, axis=1).astype(np.int32))
    w_in = w["w_in"][0]
    a0 = QKV_W
    qkv, lq_lk = w_in[:, :a0], w_in[:, a0:a0 + 2 * GLA_H * DK]
    a1 = a0 + 2 * GLA_H * DK
    lv, lr = w_in[:, a1:a1 + GLA_H * DV], w_in[:, a1 + GLA_H * DV:a1 + 2 * GLA_H * DV]
    a2 = a1 + 2 * GLA_H * DV
    lora, gates = w_in[:, a2:a2 + 2 * LORA], w_in[:, a2 + 2 * LORA:]
    pad = np.zeros((D, WB - 2 * LORA), np.float32)
    cols = np.concatenate([qkv, lv, lq_lk, lr, gates, lora, pad], axis=1)
    out["w_blk"] = np.ascontiguousarray(cols.reshape(KT, P, W_BLOCKS, WB).transpose(2, 1, 0, 3))
    return out


def kernel(**inputs):
    import numpy as np
    import concourse.bacc as bacc
    from concourse.bass_utils import run_bass_kernel_spmd

    nc = bacc.Bacc("TRN2", target_bir_lowering=False, num_devices=1)
    arrays = {f"in_{n}": a for n, a in host_inputs(**inputs).items()}
    io = {n[3:]: nc.dram_tensor(n, a.shape, mybir.dt.from_np(a.dtype), kind="ExternalInput").ap() for n, a in arrays.items()}
    io["out"] = nc.dram_tensor("out", (T, D), F32, kind="ExternalOutput").ap()
    program(nc, io)
    out = run_bass_kernel_spmd(nc, [arrays], core_ids=[0]).results[0]["out"]
    return out[N_SAMPLE:][None], out[:N_SAMPLE][None]
```

```python
from contextlib import ExitStack

import concourse.bass as bass
from concourse import mybir

ALU = mybir.AluOpType
ACT = mybir.ActivationFunctionType
F32 = mybir.dt.float32
F32R = mybir.dt.float32r
U32 = mybir.dt.uint32
I32 = mybir.dt.int32
AX = mybir.AxisListType
ds = bass.ds

P = 128
D = 1024
KT = D // P
N_SAMPLE, N_PROMPT = 1024, 256
T = N_SAMPLE + N_PROMPT
NT = T // P
NT_S = N_SAMPLE // P
EPS = 1e-6

HEADS, KV_HEADS, HD = 8, 2, 64
QKV_W = (HEADS + 2 * KV_HEADS) * HD
GLA_H, DK, DV, LORA, CHUNK = 4, 64, 128, 16, 64
PAIRS = T // (2 * CHUNK)
GLA_HP = GLA_H // 2
GATE_NORM = 16.0

WB = 256
TM_BLOCKS = (QKV_W + GLA_H * DV) // WB
FM_BLOCKS = (2 * GLA_H * DK + GLA_H * DV + 2 * D) // WB
W_BLOCKS = TM_BLOCKS + FM_BLOCKS + 1
MID_BLOCKS = 5
GATE_BLOCKS = W_BLOCKS - TM_BLOCKS - MID_BLOCKS
FM_TILES = 2 * (MID_BLOCKS + GATE_BLOCKS)
T_LQ, T_LK, T_LR, T_LORA, T_GA, T_GL = 0, 2, 4, 8, 10, 18
CHUNKS_512 = [(0, 512), (512, 512), (1024, 256)]

E = 16
FF = 1024
CAP_S, CAP_P = 2 * N_SAMPLE // E, 2 * N_PROMPT // E
CAP = CAP_S + CAP_P
PLE = 256
CW = 256
CHUNKS = T // CW
LEVELS = (32, 16, 8, 4, 2, 1)


class Chain:

    def __init__(self, sem, steps):
        self.sem, self.steps, self.at, self.i = sem, steps, 0, 0

    def turn(self, i):
        assert self.at in (0, self.steps), (self.at, self.steps)
        self.at, self.i = 0, i

    def step(self, ins):
        ins.then_inc(self.sem, 1)
        self.at += 1

    def link(self, eng, ins):
        self.step(ins)
        eng.wait_ge(self.sem, self.i * self.steps + self.at)


class Core:

    def __init__(self, nc, ctx, io):
        self.nc, self.ctx, self.io = nc, ctx, io
        self.in_use = []
        self.ps = ctx.enter_context(nc.psum_tensor("ps", [P, 8, 512], F32))
        self.ident = ctx.enter_context(nc.sbuf_tensor("ident", [P, P], F32))
        dram = lambda name, shape: nc.dram_tensor(name, shape, F32, kind="Internal").ap()
        self.tm = dram("tm_scratch", (TM_BLOCKS, NT, P, WB))
        self.fm = dram("fm_scratch", (FM_TILES, P, T))
        self.up_in = dram("up_in_scratch", (KT, P, T))
        self.x_res = dram("x_res_scratch", (T, D))
        self.xm = dram("xm_scratch", (T, D))

    def bank(self, n, width=512):
        return self.ps[:, n, 0:width]

    def sem(self, name):
        self.in_use.append(self.nc.alloc_semaphore(name=name))
        return self.in_use[-1]

    def recycle_sems(self):
        self.nc.clear_and_free_semaphores(self.in_use)
        self.in_use = []
        self.nc.all_engine_barrier()

    def sems(self, name, n):
        return [self.sem(f"{name}{b}") for b in range(n)]


def newton(dve, chain, rs, ms, tmp):
    chain.link(dve, dve.tensor_tensor(tmp, rs, rs, ALU.mult))
    chain.link(dve, dve.tensor_tensor(tmp, tmp, ms, ALU.mult))
    chain.link(dve, dve.tensor_scalar(tmp, tmp, -0.5, 1.5, ALU.mult, ALU.add))
    chain.link(dve, dve.tensor_tensor(rs, rs, tmp, ALU.mult))


NEWTON = 4


def split3(pe, out, lhs, rhs, start, stop):
    (lh, ll), (rh, rl) = lhs, rhs
    pe.matmul(out, lh, rh, start=start, stop=False)
    pe.matmul(out, lh, rl, start=False, stop=False)
    return pe.matmul(out, ll, rh, start=False, stop=stop)


def stage_norm(core, ah, al):
    nc, io = core.nc, core.io
    with ExitStack() as mem:
        sb = lambda name, shape, dt=F32: mem.enter_context(nc.sbuf_tensor(name, shape, dt))
        g = sb("n_gain", [P, D])
        x = sb("n_x", [P, 2, D])
        sq = sb("n_sq", [P, 2, D])
        xn = sb("n_xn", [P, 2, D])
        st = sb("n_stat", [P, 2, 4])
        s_const = core.sem("n_const")
        x_in = core.sems("n_x_in", 2)
        sq_done = core.sems("n_sq_done", 2)
        ms_done = core.sems("n_ms_done", 2)
        rt_done = core.sems("n_rt_done", 2)
        rs_chain = [Chain(core.sem(f"n_rs_chain{b}"), 1 + NEWTON) for b in range(2)]
        xn_done = core.sems("n_xn_done", 2)
        tr_done = core.sems("n_tr_done", 2)
        hi_done = core.sems("n_hi_done", 2)
        lo_done = core.sems("n_lo_done", 2)
        pt = [core.ps[:, 2 * b:2 * b + 2, :] for b in range(2)]
        block = mem.enter_context(nc.Block())

        @block.sync
        def _(sp):
            sp.dma_start(core.ident[:, :], io["ident"]).then_inc(s_const, 16)
            sp.dma_start(g[:, :], io["g_mix"].partition_broadcast(P)).then_inc(s_const, 16)
            with sp.Fori(0, NT // 2) as i:
                for b in range(2):
                    sp.wait_ge(xn_done[b], i)
                    sp.dma_start(x[:, b, :], io["x"][ds(i * 2 * P + b * P, P), :]).then_inc(x_in[b], 16)

        @block.scalar
        def _(act):
            def stats(i, b):
                act.wait_ge(x_in[b], i * 16 + 16)
                act.activation(sq[:, b, :], x[:, b, :], ACT.Square, accum_out=st[:, b, 0:1]).then_inc(sq_done[b], 1)
                act.wait_ge(ms_done[b], i + 1)
                act.activation(st[:, b, 2:3], st[:, b, 1:2], ACT.Sqrt).then_inc(rt_done[b], 1)

            def high(i, b):
                act.wait_ge(tr_done[b], i + 1)
                act.activation(ah[:, :, ds(i * 2 * P + b * P, P)], pt[b].rearrange("p a (c n) -> p (a c) n", n=P),
                               ACT.Copy).then_inc(hi_done[b], 1)

            with act.Fori(0, NT // 2) as i:
                for b in range(2):
                    stats(i, b)
                for b in range(2):
                    high(i, b)

        @block.vector
        def _(dve):
            dve.wait_ge(s_const, 32)
            with dve.Fori(0, NT // 2) as i:
                for b in range(2):
                    dve.wait_ge(sq_done[b], i + 1)
                    dve.tensor_scalar(st[:, b, 1:2], st[:, b, 0:1], 1.0 / D, EPS, ALU.mult, ALU.add).then_inc(ms_done[b], 1)
                    dve.wait_ge(rt_done[b], i + 1)
                    rs_chain[b].turn(i)
                    rs_chain[b].link(dve, dve.reciprocal(st[:, b, 3:4], st[:, b, 2:3]))
                    newton(dve, rs_chain[b], st[:, b, 3:4], st[:, b, 1:2], st[:, b, 2:3])
                    dve.wait_ge(tr_done[b], i)
                    dve.scalar_tensor_tensor(xn[:, b, :], x[:, b, :], st[:, b, 3:4], g[:, :], ALU.mult,
                                             ALU.mult).then_inc(xn_done[b], 1)
                for b in range(2):
                    tok = ds(i * 2 * P + b * P, P)
                    dve.wait_ge(hi_done[b], i + 1)
                    dve.tensor_tensor(al[:, :, tok], pt[b].rearrange("p a (c n) -> p (a c) n", n=P),
                                      ah[:, :, tok].bitcast(F32), ALU.subtract).then_inc(lo_done[b], 1)

        @block.tensor
        def _(pe):
            pe.wait_ge(s_const, 32)
            with pe.Fori(0, NT // 2) as i:
                for b in range(2):
                    pe.wait_ge(xn_done[b], i + 1)
                    pe.wait_ge(lo_done[b], i)
                    for k in range(KT):
                        last = pe.transpose(pt[b][:, k // 4, (k % 4) * P:(k % 4 + 1) * P],
                                            xn[:, b, k * P:(k + 1) * P], core.ident[:, :])
                    last.then_inc(tr_done[b], 1)


def nth(first, i=0, per=0):
    assert per % 2 == 0
    return i * per + first, first % 2, i * (per // 2) + first // 2


class WeightRing:

    def __init__(self, core, mem):
        sb = lambda name, dt: [mem.enter_context(core.nc.sbuf_tensor(f"{name}{b}", [P, KT, WB], dt)) for b in range(2)]
        self.raw = mem.enter_context(core.nc.sbuf_tensor("w_raw", [P, KT, WB], F32))
        self.hi, self.lo = sb("w_hi", F32R), sb("w_lo", F32R)
        self.blocks = core.io["w_blk"]
        self.loaded, self.high_done, self.low_done, self.used = (core.sems("w_" + x, 2) for x in "loaded high low used".split())

    def load(self, eng, block):
        n, b, use = block
        eng.wait_ge(self.low_done[1 - b], use + b)
        n = n if isinstance(n, int) else ds(n, 1)
        src = self.blocks[n:n + 1] if isinstance(n, int) else self.blocks[n]
        eng.dma_start(self.raw[:, :, :], src.rearrange("o p k c -> (o p) k c")).then_inc(self.loaded[b], 16)

    def high(self, act, block):
        _, b, use = block
        act.wait_ge(self.loaded[b], use * 16 + 16)
        act.wait_ge(self.used[b], use)
        act.activation(self.hi[b][:, :, :], self.raw[:, :, :], ACT.Copy).then_inc(self.high_done[b], 1)

    def low(self, eng, block):
        _, b, use = block
        eng.wait_ge(self.high_done[b], use + 1)
        eng.tensor_tensor(self.lo[b][:, :, :], self.raw[:, :, :], self.hi[b][:, :, :].bitcast(F32),
                          ALU.subtract).then_inc(self.low_done[b], 1)

    def ready(self, pe, block):
        _, b, use = block
        pe.wait_ge(self.low_done[b], use + 1)


def stage_token_major(core, ah, al, ring):
    nc = core.nc
    with ExitStack() as mem:
        TS = 5
        out = mem.enter_context(nc.sbuf_tensor("tm_out", [P, TS, WB], F32))
        done = core.sems("tm_done", TS)
        read = core.sems("tm_read", TS)
        stored = core.sems("tm_stored", TS)
        USES = NT // TS
        PAIRED = TM_BLOCKS // 2
        assert TM_BLOCKS % 2 == 1
        block = mem.enter_context(nc.Block())

        def walk(split, product, loop):
            split(nth(0))
            with loop(0, PAIRED) as i:
                split(nth(1, i, 2))
                product(nth(0, i, 2))
                split(nth(2, i, 2))
                product(nth(1, i, 2))
            split(nth(TM_BLOCKS))
            product(nth(TM_BLOCKS - 1))

        def skip(n):
            pass

        @block.sync
        def _(sp):
            with sp.Fori(0, PAIRED + 1) as i:
                for b in range(2):
                    ring.load(sp, nth(b, i, 2))

        @block.scalar
        def _(act):
            def product(blk):
                n, b, w_use = blk
                for t in range(NT):
                    s, use = t % TS, n * USES + t // TS
                    if t < NT - 1:
                        act.wait_ge(done[s], (n if s == TS - 1 else use) + 1)
                    else:
                        act.wait_ge(ring.used[b], w_use + 1)
                    act.wait_ge(stored[s], use * 16)
                    act.activation(out[:, s, :], core.bank(s, WB), ACT.Copy).then_inc(read[s], 1)

            walk(lambda blk: ring.high(act, blk), product, act.Fori)

        @block.vector
        def _(dve):
            walk(lambda blk: ring.low(dve, blk), skip, dve.Fori)

        @block.gpsimd
        def _(pool):
            def product(blk):
                n, _, _ = blk
                for t in range(NT):
                    s, use = t % TS, n * USES + t // TS
                    pool.wait_ge(read[s], use + 1)
                    pool.nop(nofuse=True)
                    dst = core.tm[n, t] if isinstance(n, int) else core.tm[ds(n, 1), t, :, :].rearrange("o p c -> (o p) c")
                    pool.dma_start(dst, out[:, s, :]).then_inc(stored[s], 16)

            walk(skip, product, pool.Fori)
            for s in range(TS):
                pool.wait_ge(stored[s], 16 * TM_BLOCKS * USES)

        @block.tensor
        def _(pe):
            def product(blk):
                n, b, _ = blk
                ring.ready(pe, blk)
                for t in range(NT):
                    s, use = t % TS, n * USES + t // TS
                    pe.wait_ge(read[s], use)
                    for k in range(KT):
                        x = [a[:, k, t * P:(t + 1) * P] for a in (ah, al)]
                        last = split3(pe, core.bank(s, WB), x, (ring.hi[b][:, k, :], ring.lo[b][:, k, :]), k == 0, k == KT - 1)
                    last.then_inc(done[s] if t < NT - 1 else ring.used[b], 1)

            walk(skip, product, pe.Fori)


def stage_rope(core, ah, al, ring, qt, kt, v):
    nc, io = core.nc, core.io
    H = HEADS + KV_HEADS
    W = H * HD
    KD = 2 * KV_HEADS
    with ExitStack() as mem:
        sb = lambda name, shape, dt=F32: mem.enter_context(nc.sbuf_tensor(name, shape, dt))
        fm_out = sb("fm_out", [P, 2, T])
        gain = sb("r_gain", [P, H, HD])
        x = sb("r_x", [P, 2, W])
        tab = sb("r_tab", [P, 2, 2, HD])
        sq = sb("r_sq", [P, 2, W])
        u = sb("r_u", [P, 2, W])
        out = sb("r_out", [P, 2, (HEADS + KD) * HD])
        st = sb("r_stat", [P, 2, 4, H])
        s_const = core.sem("r_const")
        x_in = core.sems("r_x_in", 2)
        v_in = core.sem("r_v_in")
        ms_done = core.sems("r_ms_done", 2)
        rt_done = core.sems("r_rt_done", 2)
        out_done = core.sems("r_out_done", 2)
        tr_done = core.sem("r_tr_done")
        tr_read = core.sem("r_tr_read")
        fm_done = core.sem("r_fm_done")
        fm_read = core.sems("r_fm_read", 2)
        fm_stored = core.sems("r_fm_stored", 2)
        STEPS = 1 + 1 + 1 + NEWTON + 2 + 1 + 2
        chain = [Chain(core.sem(f"r_chain{b}"), STEPS) for b in range(2)]
        fm_bank = [core.ps[:, 3 * t:3 * t + 3, :] for t in range(2)]
        pt = core.ps[:, 6:8, 0:384]
        PASSES = (MID_BLOCKS - 1) // 2
        assert NT == 4 * PASSES + 2
        block = mem.enter_context(nc.Block())

        def walk(split, fm, rope, loop):
            with loop(0, PASSES) as i:
                for f in range(4):
                    if f % 2 == 0:
                        split(nth(TM_BLOCKS + 1 + f // 2, i, 2))
                    fm(nth(TM_BLOCKS + f // 2, i, 2), f % 2, i * 2 + f // 2)
                    rope(i * 4 + f, f % 2, i * 2 + f // 2)
            fm(nth(TM_BLOCKS + MID_BLOCKS - 1), 0, MID_BLOCKS - 1)
            for t in (NT - 2, NT - 1):
                rope(t, t % 2, t // 2)

        def skip(*_):
            pass

        def tile_of(t):
            return slice(t, t + 1) if isinstance(t, int) else ds(t, 1)

        def tokens(t):
            return slice(t * P, (t + 1) * P) if isinstance(t, int) else ds(t * P, P)

        @block.sync
        def _(sp):
            for h in range(HEADS):
                sp.dma_start(gain[:, h, :], io["q_norm"].partition_broadcast(P)).then_inc(s_const, 16)
            for h in range(KV_HEADS):
                sp.dma_start(gain[:, HEADS + h, :], io["k_norm"].partition_broadcast(P)).then_inc(s_const, 16)

            def rope(t, b, use):
                sp.wait_ge(out_done[b], use)
                for k in range(3):
                    w = WB if k < 2 else W - 2 * WB
                    sp.dma_start(x[:, b, k * WB:k * WB + w], core.tm[k, tile_of(t), :, 0:w].rearrange("o p c -> (o p) c")
                                 ).then_inc(x_in[b], 16)
                sp.dma_start(v[:, tile_of(t), :], core.tm[2, tile_of(t), :, W - 2 * WB:WB].rearrange("o p c -> p o c")).then_inc(v_in, 16)
                sp.dma_start(tab[:, b, :, :], io["rope"][tile_of(t), :, :, :].rearrange("o p a c -> (o p) a c")).then_inc(x_in[b], 16)

            walk(lambda blk: ring.load(sp, blk), skip, rope, sp.Fori)
            sp.wait_ge(v_in, 16 * NT)

        @block.gpsimd
        def _(pool):
            def fm(blk, t, use):
                pool.wait_ge(fm_read[t], use + 1)
                pool.nop(nofuse=True)
                tile = use * 2 + t
                pool.dma_start(core.fm[tile_of(tile), :, :].rearrange("o p c -> (o p) c"), fm_out[:, t, :]).then_inc(fm_stored[t], 16)

            walk(lambda blk: ring.low(pool, blk), fm, skip, pool.Fori)
            pool.wait_ge(fm_stored[0], 16 * MID_BLOCKS)
            pool.wait_ge(fm_stored[1], 16 * (MID_BLOCKS - 1))

        @block.scalar
        def _(act):
            def fm(blk, t, use):
                _, b, w_use = blk
                if t == 0:
                    act.wait_ge(fm_done, use + 1)
                else:
                    act.wait_ge(ring.used[b], w_use + 1)
                act.wait_ge(fm_stored[t], use * 16)
                act.activation(fm_out[:, t, 0:1024], fm_bank[t][:, 0:2, :], ACT.Copy)
                act.activation(fm_out[:, t, 1024:T], fm_bank[t][:, 2, 0:256], ACT.Copy).then_inc(fm_read[t], 1)

            def root(b, use):
                act.wait_ge(ms_done[b], use + 1)
                act.activation(st[:, b, 2, :], st[:, b, 1, :], ACT.Sqrt).then_inc(rt_done[b], 1)

            def fm_and_root(blk, t, use):
                root(t, use)
                fm(blk, t, use)

            def rope(t, b, use):
                if isinstance(t, int) and t == NT - 1:
                    root(b, use)
                tok = tokens(t)
                act.wait_ge(tr_done, t + 1)
                act.activation(qt[:, 0:3, tok], pt[:, 0, :].rearrange("p (a n) -> p a n", n=P), ACT.Copy)
                act.activation(qt[:, 3:4, tok], pt[:, 1, 0:P].rearrange("p (a n) -> p a n", n=P), ACT.Copy)
                act.activation(kt[:, :, tok], pt[:, 1, P:3 * P].rearrange("p (a n) -> p a n", n=P), ACT.Copy).then_inc(tr_read, 1)

            walk(lambda blk: ring.high(act, blk), fm_and_root, rope, act.Fori)

        @block.vector
        def _(dve):
            dve.wait_ge(s_const, 16 * H)
            heads = lambda a: a.rearrange("p (h d) -> p h d", d=HD)

            def rope(t, b, use):
                c = chain[b]
                c.turn(use)
                s = lambda k: st[:, b, k, :]
                xb, ub = x[:, b, :], u[:, b, :]
                dve.wait_ge(x_in[b], use * 64 + 64)
                c.link(dve, dve.tensor_tensor(sq[:, b, :], xb, xb, ALU.mult))
                c.link(dve, dve.tensor_reduce(s(0), heads(sq[:, b, :]), AX.X, ALU.add))
                dve.tensor_scalar(s(1), s(0), 1.0 / HD, EPS, ALU.mult, ALU.add).then_inc(ms_done[b], 1)
                dve.wait_ge(rt_done[b], use + 1)
                c.link(dve, dve.reciprocal(s(3), s(2)))
                newton(dve, c, s(3), s(1), s(2))
                c.link(dve, dve.tensor_tensor(heads(xb), heads(xb), s(3).unsqueeze(2).broadcast_to((P, H, HD)), ALU.mult))
                c.link(dve, dve.tensor_tensor(heads(xb), heads(xb), gain[:, :, :], ALU.mult))
                cos = tab[:, b, 0, :].unsqueeze(1).broadcast_to((P, H, HD))
                c.link(dve, dve.tensor_tensor(heads(sq[:, b, :]), heads(xb), cos, ALU.mult))
                tsin = lambda k: tab[:, b, 1, :].rearrange("p (a s n) -> p a s n", s=2, n=16)[:, :, k, :].unsqueeze(1)\
                    .broadcast_to((P, H, 2, 16))
                q4 = lambda a, k: a.rearrange("p (h a s n) -> p h a s n", a=2, s=2, n=16)[:, :, :, k, :]
                c.step(dve.tensor_tensor(q4(ub, 0), q4(xb, 1), tsin(0), ALU.mult))
                c.link(dve, dve.tensor_tensor(q4(ub, 1), q4(xb, 0), tsin(1), ALU.mult))
                if not isinstance(t, int) or t >= 2:
                    dve.wait_ge(tr_read, (use - 1) * 2 + b + 1 if isinstance(use, int) else use * 2 + b - 1 if b else use * 2)
                ob, sb_ = out[:, b, :], sq[:, b, :]
                nq = HEADS * HD
                dve.tensor_tensor(ob[:, 0:nq], sb_[:, 0:nq], ub[:, 0:nq], ALU.add)
                kk = lambda a: heads(a[:, nq:W]).unsqueeze(2).broadcast_to((P, KV_HEADS, 2, HD))
                dve.tensor_tensor(ob[:, nq:].rearrange("p (h r d) -> p h r d", h=KV_HEADS, r=2), kk(sb_), kk(ub),
                                  ALU.add).then_inc(out_done[b], 1)

            walk(skip, skip, rope, dve.Fori)

        @block.tensor
        def _(pe):
            def fm(blk, t, use):
                _, b, _ = blk
                if t == 0:
                    ring.ready(pe, blk)
                pe.wait_ge(fm_read[t], use)
                for k in range(KT):
                    wh, wl = (a[:, k, t * P:(t + 1) * P] for a in (ring.hi[b], ring.lo[b]))
                    for w, a in ((wh, ah), (wh, al), (wl, ah)):
                        for n, (at, width) in enumerate(CHUNKS_512):
                            last = pe.matmul(fm_bank[t][:, n, 0:width], w, a[:, k, at:at + width],
                                             start=(k == 0 and w is wh and a is ah), stop=(k == KT - 1 and w is wl))
                lora = isinstance(use, int) and use == MID_BLOCKS - 1
                last.then_inc(fm_done if t == 0 else ring.used[b], 1)
                if lora:
                    pe.sem_inc(ring.used[b], 1)

            def rope(t, b, use):
                pe.wait_ge(out_done[b], use + 1)
                pe.wait_ge(tr_read, t)
                for n in range(6):
                    last = pe.transpose(pt[:, n // 3, (n % 3) * P:(n % 3 + 1) * P], out[:, b, n * P:(n + 1) * P], core.ident[:, :])
                last.then_inc(tr_done, 1)

            walk(skip, fm, rope, pe.Fori)


def stage_attention(core, ah, al, ring, qt, kt, v):
    nc = core.nc
    ROUNDS = KV_HEADS
    with ExitStack() as mem:
        sb = lambda name, shape, dt=F32: mem.enter_context(nc.sbuf_tensor(name, shape, dt))
        fm_out = sb("a_fm_out", [P, 2, T])
        qs = sb("a_qs", [P, 2, T])
        ks = sb("a_ks", [P, T])
        vs = sb("a_vs", [P, NT, HD])
        p = sb("a_p", [P, 2, N_SAMPLE])
        ptr = sb("a_ptr", [P, 2, NT_S, P])
        o = sb("a_o", [P, 2, 2, HD])
        at = sb("a_at", [P, T])
        st = sb("a_stat", [P, 2, 4])
        units = [(hp, t, h) for hp in range(2) for t in range(NT) for h in range(2)]
        U = len(units)
        keys = lambda t: (0, NT_S) if t < NT_S else (NT_S, NT)
        JB, CH = GATE_BLOCKS // ROUNDS, len(CHUNKS_512)
        groups = [(j, t, c) for j in range(JB) for t in range(2) for c in range(CH)]
        G = len(groups)
        long_units = [n for n, (_, t, _) in enumerate(units) if t < NT_S]
        LEAD = 2
        group_at = {long_units[LEAD + g * (len(long_units) - LEAD) // G]: g for g in range(G)}
        assert len(group_at) == G and JB % 2 == 0
        unit_of = {g: n for n, g in group_at.items()}
        split_at = {0: 0, **{unit_of[2 * CH * (j - 1) + CH]: j for j in range(1, JB)}}
        GATES = TM_BLOCKS + MID_BLOCKS
        block_of = lambda i, j: nth(GATES + j, i, JB)
        staged = core.sem("a_staged")
        s_done = core.sems("a_s_done", 2)
        max_done = core.sems("a_max_done", 2)
        bias_done = core.sems("a_bias_done", 2)
        exp_done = core.sems("a_exp_done", 2)
        t_done = core.sem("a_t_done")
        ta_read = core.sem("a_ta_read")
        tb_read = core.sem("a_tb_read")
        pv_done = core.sems("a_pv_done", 2)
        rc_done = core.sems("a_rc_done", 2)
        o_done = core.sems("a_o_done", 2)
        ot_done = core.sem("a_ot_done")
        ot_read = core.sem("a_ot_read")
        at_stored = core.sem("a_at_stored")
        g_done = core.sem("a_g_done")
        g_read = core.sem("a_g_read")
        fm_stored = core.sems("a_fm_stored", 2)
        ps_s = [core.ps[:, 2 * b:2 * b + 2, :] for b in range(2)]
        ps_t = core.ps[:, 4:6, :]
        ps_o = [core.ps[:, 6, b * HD:(b + 1) * HD] for b in range(2)]
        ps_ot = core.ps[:, 7, 0:P]
        ps_g = core.ps[:, 7, :]
        SCALE = HD ** -0.5
        HU, TU = U // 2, U // 2
        block = mem.enter_context(nc.Block())

        @block.sync
        def _(sp):
            with sp.Fori(0, ROUNDS) as i:
                for j in range(JB):
                    ring.load(sp, block_of(i, j))
                for hp in range(2):
                    sp.wait_ge(ot_read, i * TU + (hp + 1) * NT)
                    sp.dma_start(core.up_in[ds(i * 2 + hp, 1), :, :].rearrange("o p t -> (o p) t"), at[:, :]).then_inc(at_stored, 16)
            sp.wait_ge(at_stored, 16 * 2 * ROUNDS)

        @block.gpsimd
        def _(pool):
            with pool.Fori(0, ROUNDS) as i:
                pool.wait_ge(ot_done, i * TU)
                pool.tensor_copy(qs[:, :, :], qt[:, ds(i * 2, 2), :])
                pool.tensor_copy(ks[:, :].unsqueeze(1), kt[:, ds(i, 1), :])
                pool.tensor_copy(vs[:, :, :], v[:, :, ds(i * HD, HD)]).then_inc(staged, 1)
                for u in range(U):
                    if u in split_at:
                        ring.low(pool, block_of(i, split_at[u]))
                    if u in group_at:
                        g = group_at[u]
                        j, t, c = groups[g]
                        if c == CH - 1:
                            pool.wait_ge(g_read, i * G + g + 1)
                            pool.nop(nofuse=True)
                            pool.dma_start(core.fm[ds(i * (2 * JB) + T_GA + 2 * j + t, 1), :, :].rearrange("o p c -> (o p) c"),
                                           fm_out[:, t, :]).then_inc(fm_stored[t], 16)
            for t in range(2):
                pool.wait_ge(fm_stored[t], 16 * GATE_BLOCKS)

        def scores(b, t):
            a, z = keys(t)
            n = (z - a) * P
            return ps_s[b].rearrange("p a c -> p (a c)")[:, 0:n], n

        @block.tensor
        def _(pe):
            def qk(i, u):
                hp, t, h = units[u]
                b, use = u % 2, i * HU + u // 2
                pe.wait_ge(exp_done[b], use)
                rows = slice(h * HD, h * HD + HD)
                a, z = keys(t)
                for n in range(a * P, z * P, 512):
                    w = min(512, z * P - n)
                    last = pe.matmul(ps_s[b][:, (n - a * P) // 512, 0:w], qs[rows, hp, t * P:(t + 1) * P],
                                     ks[rows, n:n + w], start=True, stop=True)
                last.then_inc(s_done[b], 1)

            def turn(i, u):
                hp, t, h = units[u]
                b, use = u % 2, i * HU + u // 2
                pe.wait_ge(exp_done[b], use + 1)
                pe.wait_ge(ta_read, i * U + u)
                pe.wait_ge(tb_read, i * U + u)
                a, z = keys(t)
                for n in range(z - a):
                    last = pe.transpose(ps_t[:, n // 4, (n % 4) * P:(n % 4 + 1) * P], p[:, b, n * P:(n + 1) * P],
                                        core.ident[:, :])
                last.then_inc(t_done, 1)

            def pv(i, u):
                hp, t, h = units[u]
                b, use = u % 2, i * HU + u // 2
                pe.wait_ge(ta_read, i * U + u + 1)
                pe.wait_ge(tb_read, i * U + u + 1)
                pe.wait_ge(o_done[1 - b], i * HU + (u + 1) // 2)
                a, z = keys(t)
                for n in range(z - a):
                    last = pe.matmul(ps_o[b], ptr[:, b, n, :], vs[:, a + n, :], start=(n == 0), stop=(n == z - a - 1))
                last.then_inc(pv_done[b], 1)

            def turn_out(i, u):
                pe.wait_ge(o_done[1], i * HU + u // 2 + 1)
                pe.wait_ge(g_read, i * G + sum(n < u + 2 for n in group_at))
                pe.wait_ge(ot_read, i * TU + u // 2)
                pe.transpose(ps_ot, o[:, (u // 2) % 2, :, :].rearrange("p h d -> p (h d)"), core.ident[:, :]).then_inc(ot_done, 1)

            def group(i, u):
                g = group_at[u]
                j, t, c = groups[g]
                blk = block_of(i, j)
                b = blk[1]
                if (t, c) == (0, 0):
                    ring.ready(pe, blk)
                pe.wait_ge(g_read, i * G + g)
                pe.wait_ge(ot_read, i * TU + (u - 1) // 2)
                first, width = CHUNKS_512[c]
                for k in range(KT):
                    x = [a[:, k, first:first + width] for a in (ah, al)]
                    w = [a[:, k, t * P:(t + 1) * P] for a in (ring.hi[b], ring.lo[b])]
                    last = split3(pe, ps_g[:, 0:width], w, x, k == 0, k == KT - 1)
                last.then_inc(ring.used[b] if (t, c) == (1, CH - 1) else g_done, 1)

            with pe.Fori(0, ROUNDS) as i:
                pe.wait_ge(staged, i + 1)
                qk(i, 0)
                for u in range(U):
                    if u >= 3 and u % 2:
                        turn_out(i, u - 2)
                    if u + 1 < U:
                        qk(i, u + 1)
                    if u:
                        pv(i, u - 1)
                    if u in group_at:
                        group(i, u)
                    turn(i, u)
                pv(i, U - 1)
                turn_out(i, U - 1)

        @block.vector
        def _(dve):
            def row_max(i, u):
                b, use = u % 2, i * HU + u // 2
                flat, n = scores(b, units[u][1])
                dve.wait_ge(s_done[b], use + 1)
                dve.tensor_reduce(st[:, b, 0:1], flat, AX.X, ALU.max, negate=True).then_inc(max_done[b], 1)
                dve.wait_ge(max_done[b], use + 1)
                dve.tensor_scalar(st[:, b, 1:2], st[:, b, 0:1], SCALE, None, ALU.mult).then_inc(bias_done[b], 1)

            def evict(i, u):
                b, use = u % 2, i * HU + u // 2
                n = min(4, keys(units[u][1])[1] - keys(units[u][1])[0])
                dve.wait_ge(t_done, i * U + u + 1)
                dve.wait_ge(pv_done[b], use)
                dve.tensor_copy(ptr[:, b, 0:n, :].rearrange("p a c -> p (a c)"), ps_t[:, 0, 0:n * P]).then_inc(ta_read, 1)

            def normalise(i, u):
                b, use = u % 2, i * HU + u // 2
                dve.reciprocal(st[:, b, 3:4], st[:, b, 2:3]).then_inc(rc_done[b], 1)
                dve.wait_ge(rc_done[b], use + 1)
                dve.wait_ge(pv_done[b], use + 1)
                tile = u // 2
                dve.wait_ge(ot_done, i * TU + max(tile - 1, 0))
                dve.tensor_scalar(o[:, tile % 2, b, :], ps_o[b], st[:, b, 3:4], None, ALU.mult).then_inc(o_done[b], 1)

            with dve.Fori(0, ROUNDS) as i:
                row_max(i, 0)
                for u in range(U):
                    if u + 1 < U:
                        row_max(i, u + 1)
                    if u:
                        normalise(i, u - 1)
                    evict(i, u)
                normalise(i, U - 1)

        @block.scalar
        def _(act):
            def exp(i, u):
                b, use = u % 2, i * HU + u // 2
                flat, n = scores(b, units[u][1])
                act.wait_ge(bias_done[b], use + 1)
                act.wait_ge(o_done[b], use)
                act.activation(p[:, b, 0:n], flat, ACT.Exp, bias=st[:, b, 1:2], scale=SCALE,
                               accum_out=st[:, b, 2:3]).then_inc(exp_done[b], 1)

            def evict(i, u):
                b, use = u % 2, i * HU + u // 2
                t = units[u][1]
                act.wait_ge(t_done, i * U + u + 1)
                if t < NT_S:
                    act.wait_ge(pv_done[b], use)
                    act.activation(ptr[:, b, 4:8, :].rearrange("p a c -> p (a c)"), ps_t[:, 1, :], ACT.Copy).then_inc(tb_read, 1)
                else:
                    act.sem_inc(tb_read, 1)

            def evict_out(i, u):
                hp, t, _h = units[u]
                act.wait_ge(ot_done, i * TU + u // 2 + 1)
                if t == 0:
                    act.wait_ge(at_stored, (i * 2 + hp) * 16)
                act.activation(at[:, t * P:(t + 1) * P], ps_ot, ACT.Copy).then_inc(ot_read, 1)

            def group(i, u):
                g = group_at[u]
                j, t, c = groups[g]
                _, b, w_use = block_of(i, j)
                if (t, c) == (1, CH - 1):
                    act.wait_ge(ring.used[b], w_use + 1)
                else:
                    act.wait_ge(g_done, i * (G - JB) + g - j + 1)
                if c == 0:
                    act.wait_ge(fm_stored[t], (i * JB + j) * 16)
                first, width = CHUNKS_512[c]
                act.activation(fm_out[:, t, first:first + width], ps_g[:, 0:width], ACT.Copy).then_inc(g_read, 1)

            with act.Fori(0, ROUNDS) as i:
                exp(i, 0)
                for u in range(U):
                    if u >= 3 and u % 2:
                        evict_out(i, u - 2)
                    if u in split_at:
                        ring.high(act, block_of(i, split_at[u]))
                    if u + 1 < U:
                        exp(i, u + 1)
                    if u in group_at:
                        group(i, u)
                    evict(i, u)
                evict_out(i, U - 1)


def stage_gla(core):
    nc, io = core.nc, core.io
    HP, NCH = GLA_HP, T // CHUNK
    SEAM = N_SAMPLE // CHUNK
    FLAT = HP * T
    with ExitStack() as mem:
        sb = lambda name, shape, dt=F32: mem.enter_context(nc.sbuf_tensor(name, shape, dt))
        q = sb("g_q", [P, HP, T])
        k = sb("g_k", [P, HP, T])
        bcum = sb("g_b", [P, 2, HP, T])
        v = sb("g_v", [P, PAIRS, GLA_H * DV])
        att = sb("g_att", [P, PAIRS, GLA_H, P])
        turns = [sb(f"g_turn{b}", [P, 2, HP, T]) for b in range(2)]
        ql, kl = ([turns[b][:, n, :, :] for b in range(2)] for n in range(2))
        both = sb("g_diff", [P, 2, HP, T])
        diff = [both[:, d, :, :] for d in range(2)]
        state = [sb(f"g_state{d}", [P, NCH, HP, DV]) for d in range(2)]
        decay = sb("g_decay", [P, 2, HP, NCH])
        mask = sb("g_mask", [P, len(LEVELS) + 1, P], I32)
        ones = sb("g_ones", [P, P])
        gain = sb("g_gain", [P, 1])
        bias = sb("g_bias", [P, 2, HP])
        w_lora = sb("g_w_lora", [2 * LORA, 2, HP, P])
        stat = sb("g_stat", [P, 4, PAIRS * GLA_H])
        lora = state[0][0:2 * LORA].rearrange("p c h d -> p (c h d)")[:, 0:T]
        reset = state[1][:, :, :, :].rearrange("p c h d -> p (c h d)")[:, 0:FLAT + 1]
        z = [ql[0], kl[0]]
        lg = [ql[1], kl[1]]
        kt = [diff[d].rearrange("p h t -> p (h t)").rearrange("p (a h c) -> p a h c", a=PAIRS, h=HP) for d in range(2)]
        by_pair = lambda x: x[:, :, :, :].rearrange("p d h t -> p (d h t)").rearrange("p (a h c) -> p a h c", a=PAIRS, h=GLA_H)
        out, sq = by_pair(both), by_pair(turns[0])
        r = att[:, :, :, :].rearrange("p a h c -> p (a h c)").rearrange("p (h t) -> p h t", h=GLA_H)
        sr = v[:, :, :].rearrange("p a c -> p (a c)").rearrange("p (h t) -> p h t", h=GLA_H)
        diag = [state[1][:, 2 * b:2 * b + 2, :, :].rearrange("p c h d -> p (c h d)") for b in range(2)]
        flat = lambda a: a.rearrange("p h t -> p (h t)")
        blocks = lambda a, m: flat(a).rearrange("p (n w) -> p n w", w=2 * m)
        chunks = lambda a: flat(a).rearrange("p (n w) -> p n w", w=CHUNK)
        tok = [(0, 512), (512, 512), (1024, 256)]

        ps = core.ps
        TWOS = PAIRS // 2
        TWO = [(a, h) for a in range(2) for h in range(GLA_H)]
        slot = lambda bank, a, h: ps[:, bank, (2 * a + h // 2) * P:(2 * a + h // 2 + 1) * P]
        spread = lambda bank: ps[:, bank, :].rearrange("p (a h t) -> p a h t", a=2, h=2)

        names = ("in_lora in_qk in_v in_mask in_r lora_z z_read z_abs z_exp z_ln g_done scan_done reset_done lvl_df lvl_db "
                 "lvl_exp lvl_q lvl_k lvl_mm lvl_read att_zero q_scaled dk_f dk_b dk_exp dk_kf dk_kb kt_tr kt_read "
                 "dec_done q_f q_b q_exp ds_mm s_step out_mm out_read sq_done ss_mm ms_done rt_done bc_mm bc_read diag_done "
                 "r_sig r_silu final stored ones_done")
        S = {n: core.sem("g_s_" + n) for n in names.split()}
        chain = Chain(core.sem("g_chain"), 0)
        NL = len(LEVELS)
        ENDS = ((SEAM - 1, NCH - 1), (0, SEAM))
        FIRSTS = ((0, SEAM), (NCH - 1, SEAM - 1))
        steps = [[(d, c) for d, c in ((0, n), (1, NCH - 1 - n)) if c not in ENDS[d]] for n in range(NCH)]
        states_by = [HP * sum(map(len, steps[:n])) for n in range(NCH + 1)]
        block = mem.enter_context(nc.Block())

        @block.sync
        def _(sp):
            sp.dma_start(lora, core.fm[T_LORA, 0:2 * LORA, :]).then_inc(S["in_lora"], 16)
            sp.dma_start(w_lora[:, :, :, :], io["w_lora"]).then_inc(S["in_lora"], 16)
            sp.dma_start(bias[:, :, :], io["b_lora"]).then_inc(S["in_lora"], 16)
            sp.dma_start(gain[:, :], io["gla_norm"]).then_inc(S["in_lora"], 16)
            sp.dma_start(q[:, :, :], core.fm[T_LQ:T_LQ + 2].rearrange("h p t -> p h t")).then_inc(S["in_qk"], 16)
            sp.dma_start(k[:, :, :], core.fm[T_LK:T_LK + 2].rearrange("h p t -> p h t")).then_inc(S["in_qk"], 16)
            sp.dma_start(mask[:, :, :], io["level_masks"]).then_inc(S["in_mask"], 16)
            for n in range(2):
                sp.dma_start(v[:, :, n * WB:(n + 1) * WB], core.tm[3 + n].rearrange("t p c -> p t c")).then_inc(S["in_v"], 16)
            sp.wait_ge(S["out_mm"], TWOS)
            sp.dma_start(r, core.fm[T_LR:T_LR + GLA_H].rearrange("h p t -> p h t")).then_inc(S["in_r"], 16)
            sp.wait_ge(S["final"], PAIRS)
            for h in range(GLA_H):
                sp.dma_start(core.up_in[KT // 2 + h].rearrange("p (a c) -> p a c", c=P), out[:, :, h, :]).then_inc(S["stored"], 16)
            sp.wait_ge(S["stored"], 16 * GLA_H)

        @block.tensor
        def _(pe):
            pe.wait_ge(S["in_lora"], 64)
            for u in range(2 * HP):
                d, h = divmod(u, HP)
                if u >= 2:
                    pe.wait_ge(S["z_read"], u - 1)
                for n, (at, w) in enumerate(tok):
                    last = pe.matmul(ps[:, 3 * (u % 2) + n, 0:w], w_lora[:, d, h, :], lora[:, at:at + w], start=True, stop=True)
                last.then_inc(S["lora_z"], 1)
            pe.wait_ge(S["z_read"], 2 * HP)
            for l in range(NL + 1):
                if l < NL:
                    pe.wait_ge(S["lvl_q"], l + 1)
                    pe.wait_ge(S["lvl_k"], l + 1)
                    qq, kk = ql[l % 2], kl[l % 2]
                else:
                    qq, kk = q, k
                for n in range(TWOS):
                    use = l * TWOS + n
                    if use >= 2:
                        pe.wait_ge(S["lvl_read"], 2 * (use - 1))
                    for a, h in TWO:
                        rows, t = slice((h % 2) * DK, (h % 2 + 1) * DK), slice((2 * n + a) * P, (2 * n + a + 1) * P)
                        last = pe.matmul(slot(2 * (use % 2) + h % 2, a, h), kk[rows, h // 2, t], qq[rows, h // 2, t],
                                         start=True, stop=True)
                    last.then_inc(S["lvl_mm"], 1)
            for d in range(2):
                pe.wait_ge(S["dk_kf" if d == 0 else "dk_kb"], 1)
                for n in range(PAIRS * HP // 4):
                    use = d * (PAIRS * HP // 4) + n
                    if use >= 4:
                        pe.wait_ge(S["kt_read"], use - 3)
                    for m in range(4):
                        a, h = divmod(n * 4 + m, HP)
                        last = pe.transpose(ps[:, 4 + use % 4, m * P:(m + 1) * P], (kl[0] if d == 0 else ql[0])[:, h, a * P:(a + 1) * P],
                                            core.ident[:, :])
                    last.then_inc(S["kt_tr"], 1)
            pe.wait_ge(S["kt_read"], 2 * (PAIRS * HP // 4))
            pe.wait_ge(S["lvl_read"], 2 * (NL + 1) * TWOS)
            pe.wait_ge(S["in_v"], 32)
            for n in range(NCH):
                if n >= 2:
                    pe.wait_ge(S["s_step"], states_by[n - 1])
                if not steps[n]:
                    continue
                for d, c in steps[n]:
                    rows = slice((c % 2) * CHUNK, (c % 2 + 1) * CHUNK)
                    for h in range(GLA_H):
                        o = (h % 2) * DK
                        last = pe.matmul(ps[o:o + DK, 2 * (n % 2) + d, (h // 2) * DV:(h // 2 + 1) * DV],
                                         kt[d][rows, c // 2, h // 2, o:o + DK], v[rows, c // 2, h * DV:(h + 1) * DV],
                                         start=True, stop=True, skip_group_check=True)
                last.then_inc(S["ds_mm"], 1)
            pe.wait_ge(S["s_step"], states_by[NCH])
            pe.wait_ge(S["q_f"], 1)
            pe.wait_ge(S["q_b"], 1)
            for n in range(TWOS):
                if n >= 2:
                    pe.wait_ge(S["out_read"], 2 * (n - 1))
                for pair, h in TWO:
                    a = 2 * n + pair
                    rows = slice((h % 2) * DK, (h % 2 + 1) * DK)
                    o = slot(4 + 2 * (n % 2) + h % 2, pair, h)
                    terms = []
                    for j in range(2):
                        c = 2 * a + j
                        cols, t = slice(j * CHUNK, (j + 1) * CHUNK), slice(c * CHUNK, (c + 1) * CHUNK)
                        if c not in (0, SEAM):
                            terms.append((o[:, cols], state[0][rows, c, h // 2, :], ql[1][rows, h // 2, t]))
                        if c not in (SEAM - 1, NCH - 1):
                            terms.append((o[:, cols], state[1][rows, c, h // 2, :], kl[1][rows, h // 2, t]))
                    pe.matmul(o, v[:, a, h * DV:(h + 1) * DV], att[:, a, h, :], start=True, stop=False, skip_group_check=True)
                    for m, (dst, lhs, rhs) in enumerate(terms):
                        last = pe.matmul(dst, lhs, rhs, start=False, stop=(m == len(terms) - 1), skip_group_check=True)
                last.then_inc(S["out_mm"], 1)
            pe.wait_ge(S["ones_done"], 1)
            for a in range(PAIRS):
                pe.wait_ge(S["sq_done"], a + 1)
                for h in range(GLA_H):
                    last = pe.matmul(ps[:, 0, a * GLA_H + h:a * GLA_H + h + 1], sq[:, a, h, :], ones[:, 0:1], start=True, stop=True)
            last.then_inc(S["ss_mm"], 1)
            for a in range(PAIRS):
                pe.wait_ge(S["diag_done"], a + 1)
                if a >= 2:
                    pe.wait_ge(S["bc_read"], a - 1)
                pe.matmul(ps[:, 2 + a % 2, :], ones[:, :], diag[a % 2], start=True, stop=True).then_inc(S["bc_mm"], 1)

        @block.scalar
        def _(act):
            for u in range(2 * HP):
                d, h = divmod(u, HP)
                act.wait_ge(S["z_read"], u + 1)
                act.activation(lg[d][:, h, :], z[d][:, h, :], ACT.Abs).then_inc(S["z_abs"], 1)
            for u in range(2 * HP):
                d, h = divmod(u, HP)
                act.wait_ge(S["z_abs"], u + 1)
                act.activation(lg[d][:, h, :], lg[d][:, h, :], ACT.Exp, scale=-1.0).then_inc(S["z_exp"], 1)
            for u in range(2 * HP):
                d, h = divmod(u, HP)
                act.wait_ge(S["z_exp"], u + 1)
                act.activation(lg[d][:, h, :], lg[d][:, h, :], ACT.Ln, bias=1.0).then_inc(S["z_ln"], 1)
            g = 1.0 / GATE_NORM
            for l, m in enumerate(LEVELS):
                b = l % 2
                if l >= 2:
                    act.wait_ge(S["lvl_mm"], (l - 1) * TWOS)
                else:
                    act.wait_ge(S["scan_done"], 2)
                act.wait_ge(S["lvl_df"], l + 1)
                df, db, qb, kb = (blocks(x, m) for x in (diff[0], diff[1], ql[b], kl[b]))
                act.activation(qb[:, :, m:2 * m], df[:, :, m:2 * m], ACT.Exp, scale=g)
                act.activation(kb[:, :, 0:m], df[:, :, 0:m], ACT.Exp, scale=-g)
                act.wait_ge(S["lvl_db"], l + 1)
                act.activation(qb[:, :, 0:m], db[:, :, 0:m], ACT.Exp, scale=g)
                act.activation(kb[:, :, m:2 * m], db[:, :, m:2 * m], ACT.Exp, scale=-g).then_inc(S["lvl_exp"], 1)
            act.wait_ge(S["dk_f"], 1)
            act.wait_ge(S["lvl_mm"], (NL - 1) * TWOS)
            act.activation(kl[0][:, :, :], diff[0][:, :, :], ACT.Exp, scale=-g)
            act.wait_ge(S["dk_b"], 1)
            act.activation(ql[0][:, :, :], diff[1][:, :, :], ACT.Exp, scale=-g).then_inc(S["dk_exp"], 1)
            act.activation(decay[:, 0, :, :], bcum[:, 0, :, CHUNK - 1::CHUNK], ACT.Exp, scale=g)
            act.activation(decay[:, 1, :, :], bcum[:, 1, :, 0::CHUNK], ACT.Exp, scale=g).then_inc(S["dec_done"], 1)
            act.wait_ge(S["lvl_mm"], NL * TWOS)
            act.activation(ql[1][:, :, :], bcum[:, 0, :, :], ACT.Exp, scale=g)
            act.activation(kl[1][:, :, :], bcum[:, 1, :, :], ACT.Exp, scale=g).then_inc(S["q_exp"], 1)
            n_kt = PAIRS * HP // 4
            for use in range(2 * n_kt):
                d, n = divmod(use, n_kt)
                act.wait_ge(S["kt_tr"], use + 1)
                act.activation(kt[d].rearrange("p a h c -> p (a h c)")[:, n * 512:(n + 1) * 512], ps[:, 4 + use % 4, :],
                               ACT.Copy).then_inc(S["kt_read"], 1)
            for a in range(PAIRS):
                act.wait_ge(S["out_read"], 2 * (a // 2 + 1))
                act.activation(sq[:, a, :, :], out[:, a, :, :], ACT.Square).then_inc(S["sq_done"], 1)
            act.wait_ge(S["in_r"], 16)
            act.activation(sr, r, ACT.Sigmoid).then_inc(S["r_sig"], 1)
            act.wait_ge(S["ms_done"], 1)
            act.activation(stat[:, 2, :], stat[:, 1, :], ACT.Sqrt).then_inc(S["rt_done"], 1)

        @block.vector
        def _(dve):
            link = lambda ins: chain.link(dve, ins)
            dve.memset(ones[:, :], 1.0).then_inc(S["ones_done"], 1)
            dve.memset(att[:, :, :, :].bitcast(U32), 0).then_inc(S["att_zero"], 1)
            link(dve.memset(reset, 1.0))
            link(dve.memset(reset[:, 0::CHUNK], 0.0))
            for u in range(2 * HP):
                d, h = divmod(u, HP)
                dve.wait_ge(S["in_lora"], 64)
                dve.wait_ge(S["lora_z"], u + 1)
                b = 3 * (u % 2)
                dve.tensor_scalar(z[d][:, h, 0:1024], ps[:, b:b + 2, :].rearrange("p a c -> p (a c)"), bias[:, d, h:h + 1], None, ALU.add)
                dve.tensor_scalar(z[d][:, h, 1024:T], ps[:, b + 2, 0:256], bias[:, d, h:h + 1], None, ALU.add).then_inc(S["z_read"], 1)
            dve.wait_ge(S["in_qk"], 32)
            dve.tensor_scalar(q[:, :, :], q[:, :, :], DK ** -0.5, None, ALU.mult).then_inc(S["q_scaled"], 1)
            for d in range(2):
                dve.wait_ge(S["z_ln"], HP * (d + 1))
                link(dve.scalar_tensor_tensor(flat(z[d]), flat(z[d]), 0.0, flat(lg[d]), ALU.min, ALU.subtract))
            fwd, bwd = (flat(bcum[:, d, :, :]) for d in range(2))
            dve.tensor_tensor_scan(fwd, reset[:, 0:FLAT], flat(z[0]), 0.0, ALU.mult, ALU.add).then_inc(S["scan_done"], 1)
            dve.tensor_tensor_scan(bwd[:, ::-1], reset[:, 1:FLAT + 1][:, ::-1], flat(z[1])[:, ::-1], 0.0, ALU.mult,
                                   ALU.add).then_inc(S["scan_done"], 1)
            dve.wait_ge(S["scan_done"], 2)
            dve.wait_ge(S["in_mask"], 16)

            def gather(l):
                for n in range(TWOS):
                    use = l * TWOS + n
                    dve.wait_ge(S["lvl_mm"], use + 1)
                    for par in range(2):
                        dve.copy_predicated(att[:, 2 * n:2 * n + 2, par::2, :],
                                            mask[:, l, :].unsqueeze(1).unsqueeze(1).broadcast_to((P, 2, 2, P)),
                                            spread(2 * (use % 2) + par)).then_inc(S["lvl_read"], 1)

            bf, bb = bcum[:, 0, :, :], bcum[:, 1, :, :]
            for l, m in enumerate(LEVELS):
                if l:
                    dve.wait_ge(S["lvl_exp"], l)
                seam = blocks(bf, m)[:, :, m - 1:m].broadcast_to((P, FLAT // (2 * m), 2 * m))
                dve.tensor_tensor(blocks(diff[0], m), blocks(bf, m), seam, ALU.subtract).then_inc(S["lvl_df"], 1)
                dve.wait_ge(S["lvl_exp"], l + 1)
                dve.wait_ge(S["q_scaled"], 1)
                dve.tensor_tensor(flat(ql[l % 2]), flat(ql[l % 2]), flat(q), ALU.mult).then_inc(S["lvl_q"], 1)
                if l:
                    gather(l - 1)
            last = chunks(bf)[:, :, CHUNK - 1:CHUNK].broadcast_to((P, HP * NCH, CHUNK))
            dve.tensor_tensor(chunks(diff[0]), chunks(bf), last, ALU.subtract).then_inc(S["dk_f"], 1)
            gather(NL - 1)
            dve.wait_ge(S["dk_exp"], 1)
            dve.tensor_tensor(flat(kl[0]), flat(kl[0]), flat(k), ALU.mult).then_inc(S["dk_kf"], 1)
            gather(NL)
            dve.wait_ge(S["q_exp"], 1)
            dve.tensor_tensor(flat(ql[1]), flat(ql[1]), flat(q), ALU.mult).then_inc(S["q_f"], 1)
            dve.wait_ge(S["dec_done"], 1)
            for n in range(NCH):
                dve.wait_ge(S["ds_mm"], sum(map(bool, steps[:n + 1])))
                if n:
                    dve.wait_ge(S["s_step"], states_by[n])
                for d, c in steps[n]:
                    to = c + 1 if d == 0 else c - 1
                    for h in range(HP):
                        add = ps[:, 2 * (n % 2) + d, h * DV:(h + 1) * DV]
                        if c in FIRSTS[d]:
                            dve.tensor_copy(state[d][:, to, h, :], add).then_inc(S["s_step"], 1)
                        else:
                            dve.scalar_tensor_tensor(state[d][:, to, h, :], state[d][:, c, h, :], decay[:, d, h, c:c + 1], add,
                                                     ALU.mult, ALU.add).then_inc(S["s_step"], 1)
            for n in range(TWOS):
                dve.wait_ge(S["out_mm"], n + 1)
                for par in range(2):
                    dve.tensor_copy(out[:, 2 * n:2 * n + 2, par::2, :], spread(4 + 2 * (n % 2) + par)).then_inc(S["out_read"], 1)
            dve.wait_ge(S["ss_mm"], 1)
            s = lambda n: stat[:, n, :]
            dve.tensor_scalar(s(1), ps[:, 0, 0:PAIRS * GLA_H], 1.0 / DV, EPS, ALU.mult, ALU.add).then_inc(S["ms_done"], 1)
            dve.wait_ge(S["rt_done"], 1)
            link(dve.reciprocal(s(3), s(2)))
            newton(dve, chain, s(3), s(1), s(2))

            def final(a):
                o = out[:, a, :, :].rearrange("p h t -> p (h t)")
                dve.wait_ge(S["bc_mm"], a + 1)
                dve.scalar_tensor_tensor(o, o, gain[:, 0:1], ps[:, 2 + a % 2, :], ALU.mult, ALU.mult).then_inc(S["bc_read"], 1)
                dve.wait_ge(S["bc_read"], a + 1)
                dve.wait_ge(S["r_silu"], 1)
                dve.tensor_tensor(out[:, a, :, :], out[:, a, :, :], sr[:, :, a * P:(a + 1) * P], ALU.mult).then_inc(S["final"], 1)

            for a in range(PAIRS):
                if a >= 2:
                    dve.wait_ge(S["bc_mm"], a - 1)
                dve.tensor_tensor(diag[a % 2].rearrange("p (h t) -> p h t", h=GLA_H),
                                  core.ident[:, :].unsqueeze(1).broadcast_to((P, GLA_H, P)),
                                  stat[:, 3, a * GLA_H:(a + 1) * GLA_H].unsqueeze(2).broadcast_to((P, GLA_H, P)),
                                  ALU.mult).then_inc(S["diag_done"], 1)
                if a:
                    final(a - 1)
            final(PAIRS - 1)

        @block.gpsimd
        def _(pool):
            bb = bcum[:, 1, :, :]
            pool.wait_ge(S["in_qk"], 32)
            pool.wait_ge(S["scan_done"], 2)
            for l, m in enumerate(LEVELS):
                if l:
                    pool.wait_ge(S["lvl_exp"], l)
                seam = blocks(bb, m)[:, :, m:m + 1].broadcast_to((P, FLAT // (2 * m), 2 * m))
                pool.tensor_tensor(blocks(diff[1], m), blocks(bb, m), seam, ALU.subtract).then_inc(S["lvl_db"], 1)
                pool.wait_ge(S["lvl_exp"], l + 1)
                pool.tensor_tensor(flat(kl[l % 2]), flat(kl[l % 2]), flat(k), ALU.mult).then_inc(S["lvl_k"], 1)
            first = chunks(bb)[:, :, 0:1].broadcast_to((P, HP * NCH, CHUNK))
            pool.tensor_tensor(chunks(diff[1]), chunks(bb), first, ALU.subtract).then_inc(S["dk_b"], 1)
            pool.wait_ge(S["dk_exp"], 1)
            pool.tensor_tensor(flat(ql[0]), flat(ql[0]), flat(k), ALU.mult).then_inc(S["dk_kb"], 1)
            pool.wait_ge(S["q_exp"], 1)
            pool.wait_ge(S["q_scaled"], 1)
            pool.tensor_tensor(flat(kl[1]), flat(kl[1]), flat(q), ALU.mult).then_inc(S["q_b"], 1)
            pool.wait_ge(S["r_sig"], 1)
            pool.tensor_tensor(sr, sr, r, ALU.mult).then_inc(S["r_silu"], 1)


def resident_weights(core, mem, tag, parts, stage_bufs):
    nc = core.nc
    kts = [n for n, _ in parts]
    hi = [mem.enter_context(nc.sbuf_tensor(f"{tag}_hi{n}", [P, k, D], F32R)) for n, (k, _) in enumerate(parts)]
    lo = [mem.enter_context(nc.sbuf_tensor(f"{tag}_lo{n}", [P, k, D], F32R)) for n, (k, _) in enumerate(parts)]
    w_in, w_hi, w_lo = (core.sems(f"{tag}_{x}", 2) for x in ("w_in", "w_hi", "w_lo"))
    blocks = [(n, c) for n in range(len(parts)) for c in range(D // WB)]

    def load(eng):
        for u, (n, c) in enumerate(blocks):
            if u >= 2:
                eng.wait_ge(w_lo[u % 2], u // 2)
            eng.dma_start(stage_bufs[u % 2][:, 0:kts[n], :], parts[n][1](c)).then_inc(w_in[u % 2], 16)

    def high(act):
        for u, (n, c) in enumerate(blocks):
            act.wait_ge(w_in[u % 2], 16 * (u // 2 + 1))
            act.activation(hi[n][:, :, c * WB:(c + 1) * WB], stage_bufs[u % 2][:, 0:kts[n], :], ACT.Copy).then_inc(w_hi[u % 2], 1)

    def low(dve):
        for u, (n, c) in enumerate(blocks):
            dve.wait_ge(w_hi[u % 2], u // 2 + 1)
            cols = slice(c * WB, (c + 1) * WB)
            dve.tensor_tensor(lo[n][:, :, cols], stage_bufs[u % 2][:, 0:kts[n], :], hi[n][:, :, cols].bitcast(F32),
                              ALU.subtract).then_inc(w_lo[u % 2], 1)

    def ready(pe):
        for b in range(2):
            pe.wait_ge(w_lo[b], len(blocks) // 2)

    return hi, lo, load, high, low, ready


def stage_merge(core, aff):
    nc, io = core.nc, core.io
    with ExitStack() as mem:
        sb = lambda name, shape, dt=F32: mem.enter_context(nc.sbuf_tensor(name, shape, dt))
        x = sb("m_x", [P, KT, CW])
        res = sb("m_res", [P, 2, D])
        kcols = lambda w, c: w.rearrange("(k p) n -> p k n", p=P)[:, :, c * WB:(c + 1) * WB]
        wh, wl, load_w, high_w, low_w, ready_w = resident_weights(
            core, mem, "m", [(KT, lambda c: kcols(io["w_up"], c)), (KT, lambda c: kcols(io["w_out"], c))],
            [x, res[:, :, :].rearrange("p b d -> p (b d)").rearrange("p (k c) -> p k c", k=KT)])
        xh, xl = sb("m_xh", [P, KT, CW], F32R), sb("m_xl", [P, KT, CW], F32R)
        mh, ml = sb("m_mh", [P, KT, CW], F32R), sb("m_ml", [P, KT, CW], F32R)
        GS = 4
        gates = sb("m_gates", [P, GS, 2, CW])
        xn = sb("m_xn", [P, 2, D])
        xt = sb("m_xt", [P, D])
        g = sb("m_gain", [P, D])
        w_r = sb("m_w_r", [P, KT, E])
        st = sb("m_stat", [P, 2, 8])
        lg = sb("m_lg", [P, 2, 2, E])
        one = lambda names: {n: core.sem("m_s_" + n) for n in names.split()}
        two = lambda names: {n: core.sems("m_s_" + n, 2) for n in names.split()}
        S = one("const x_in xh xl mlo gate")
        S2 = two("up prod sum mhi res_in out x1 sq ms rt xn x1_out xn_out tr xt rt_mm nmax ex aff aff_tr aff_out")
        g_in = core.sems("m_s_g_in", GS)
        chain = [Chain(core.sem(f"m_chain{b}"), 1 + NEWTON) for b in range(2)]
        chain2 = [Chain(core.sem(f"m_chain_r{b}"), 1) for b in range(2)]
        ps = core.ps
        LAST = CHUNKS - 1
        FT = KT
        block = mem.enter_context(nc.Block())

        @block.sync
        def _(sp):
            load_w(sp)
            sp.dma_start(g[:, :], io["g_moe"].partition_broadcast(P)).then_inc(S["const"], 16)
            sp.dma_start(w_r[:, :, :], io["w_router"].rearrange("(k p) n -> p k n", p=P)).then_inc(S["const"], 16)

            ready_w(sp)
            with sp.Fori(0, CHUNKS) as c:
                cols = ds(c * CW, CW)
                sp.wait_ge(S["xl"], c)
                sp.dma_start(x[:, :, :], core.up_in[:, :, cols].rearrange("k p t -> p k t")).then_inc(S["x_in"], 16)
                for ft in range(FT):
                    sp.wait_ge(S["mlo"], c * FT + (ft - GS + 1 if ft >= GS else 0))
                    for h in range(2):
                        sp.dma_start(gates[:, ft % GS, h, :], core.fm[T_GA + h * FT + ft, :, cols]).then_inc(g_in[ft % GS], 16)

        @block.gpsimd
        def _(pool):
            def load_res(c):
                for b in range(2):
                    pool.wait_ge(S2["x1_out"][b], c * 16)
                    pool.wait_ge(S2["xn"][b], c)
                    pool.nop(nofuse=True)
                    pool.dma_start(res[:, b, :], io["x"][ds(c * CW + b * P, P), :]).then_inc(S2["res_in"][b], 16)

            def store(c):
                for b in range(2):
                    rows = ds(c * CW + b * P, P)
                    pool.wait_ge(S2["x1"][b], c + 1)
                    pool.nop(nofuse=True)
                    pool.dma_start(core.x_res[rows, :], res[:, b, :]).then_inc(S2["x1_out"][b], 16)
                    pool.wait_ge(S2["xn"][b], c + 1)
                    pool.nop(nofuse=True)
                    pool.dma_start(core.xm[rows, :], xn[:, b, :]).then_inc(S2["xn_out"][b], 16)

            ready_w(pool)
            with pool.Fori(0, CHUNKS) as c:
                load_res(c)
                store(c)
            for b in range(2):
                pool.wait_ge(S2["x1_out"][b], 16 * CHUNKS)
                pool.wait_ge(S2["xn_out"][b], 16 * CHUNKS)

        def walk(split, up, tail, out, late, loop):
            split(0)
            up(0)
            split(1)
            out(0)
            with loop(1, LAST) as c:
                up(c)
                tail(c - 1)
                split(c + 1)
                out(c)
                late(c - 1)
            up(LAST)
            tail(LAST - 1)
            out(LAST)
            late(LAST - 1)
            tail(LAST)
            late(LAST)

        @block.tensor
        def _(pe):
            ready_w(pe)
            pe.wait_ge(S["const"], 32)

            def split(c):
                pass

            def up(c):
                pe.wait_ge(S["xl"], c + 1)
                for ft in range(FT):
                    b, use = ft % 2, c * (FT // 2) + ft // 2
                    pe.wait_ge(S2["prod"][b], use)
                    cols = slice(ft * P, (ft + 1) * P)
                    for part in range(2):
                        for k in range(4):
                            kk = 4 * part + k
                            last = split3(pe, ps[:, b, part * CW:(part + 1) * CW], (wh[0][:, kk, cols], wl[0][:, kk, cols]),
                                          (xh[:, kk, :], xl[:, kk, :]), k == 0, k == 3)
                    last.then_inc(S2["up"][b], 1)

            def out(c):
                for b in range(2):
                    pe.wait_ge(S["mlo"], FT * (c + 1))
                    pe.wait_ge(S2["x1"][b], c)
                    pe.wait_ge(S2["xt"][b], c)
                    for n in range(2):
                        for k in range(KT):
                            rows, cols = slice(b * P, (b + 1) * P), slice(n * 512, (n + 1) * 512)
                            last = split3(pe, ps[:, 2 + 2 * b + n, :], (mh[:, k, rows], ml[:, k, rows]),
                                          (wh[1][:, k, cols], wl[1][:, k, cols]), k == 0, k == KT - 1)
                    last.then_inc(S2["out"][b], 1)

            def tail(c):
                for b in range(2):
                    pe.wait_ge(S2["xn"][b], c + 1)
                    for k in range(KT):
                        last = pe.transpose(ps[:, 2 + 2 * b + k // 4, (k % 4) * P:(k % 4 + 1) * P], xn[:, b, k * P:(k + 1) * P],
                                            core.ident[:, :])
                    last.then_inc(S2["tr"][b], 1)
                for b in range(2):
                    pe.wait_ge(S2["xt"][b], c + 1)
                    pe.wait_ge(S2["aff_out"][b], c)
                    for k in range(KT):
                        last = pe.matmul(ps[:, 6 + b, 0:E], xt[:, k * P:(k + 1) * P], w_r[:, k, :], start=(k == 0), stop=(k == KT - 1))
                    last.then_inc(S2["rt_mm"][b], 1)

            def late(c):
                for b in range(2):
                    pe.wait_ge(S2["aff"][b], c + 1)
                    pe.transpose(ps[0:E, 6 + b, P:2 * P], lg[:, b, 1, :], core.ident[:, :]).then_inc(S2["aff_tr"][b], 1)

            walk(split, up, tail, out, late, pe.Fori)

        @block.scalar
        def _(act):
            high_w(act)

            def gate(c, ft):
                s = ft % GS
                act.wait_ge(g_in[s], 32 * (c * (FT // GS) + ft // GS + 1))
                act.activation(gates[:, s, :, :], gates[:, s, :, :], ACT.Sigmoid).then_inc(S["gate"], 1)

            def split(c):
                act.wait_ge(S["x_in"], c * 16 + 16)
                act.wait_ge(S2["up"][1], c * (FT // 2))
                act.activation(xh[:, :, :], x[:, :, :], ACT.Copy).then_inc(S["xh"], 1)

            def up(c):
                gate(c, 0)
                for ft in range(FT):
                    b, use = ft % 2, c * (FT // 2) + ft // 2
                    if ft + 1 < FT:
                        gate(c, ft + 1)
                    act.wait_ge(S2["sum"][b], use + 1)
                    if ft == 0:
                        act.wait_ge(S2["out"][1], c)
                    act.activation(mh[:, ft, :], gates[:, ft % GS, 0, :], ACT.Copy).then_inc(S2["mhi"][b], 1)

            def out(c):
                for b in range(2):
                    act.wait_ge(S2["x1"][b], c + 1)
                    act.wait_ge(S2["xn_out"][b], c * 16)
                    act.wait_ge(S2["tr"][b], c)
                    act.activation(xn[:, b, :], res[:, b, :], ACT.Square, accum_out=st[:, b, 0:1]).then_inc(S2["sq"][b], 1)
                    act.wait_ge(S2["ms"][b], c + 1)
                    act.activation(st[:, b, 2:3], st[:, b, 1:2], ACT.Sqrt).then_inc(S2["rt"][b], 1)

            def tail(c):
                for b in range(2):
                    act.wait_ge(S2["tr"][b], c + 1)
                    act.wait_ge(S2["rt_mm"][1 - b], c + b)
                    act.activation(xt[:, :].rearrange("p (a n) -> p a n", a=2), ps[:, 2 + 2 * b:4 + 2 * b, :], ACT.Copy).then_inc(S2["xt"][b], 1)
                for b in range(2):
                    act.wait_ge(S2["nmax"][b], c + 1)
                    act.activation(lg[:, b, 0, :], ps[:, 6 + b, 0:E], ACT.Exp, bias=st[:, b, 4:5], accum_out=st[:, b, 5:6]).then_inc(S2["ex"][b], 1)

            def late(c):
                for b in range(2):
                    act.wait_ge(S2["aff_tr"][b], c + 1)
                    act.activation(aff[:, ds(c * CW + b * P, P)], ps[0:E, 6 + b, P:2 * P], ACT.Copy).then_inc(S2["aff_out"][b], 1)

            walk(split, up, tail, out, late, act.Fori)

        @block.vector
        def _(dve):
            low_w(dve)
            dve.wait_ge(S["const"], 32)

            def split(c):
                dve.wait_ge(S["xh"], c + 1)
                dve.tensor_tensor(xl[:, :, :], x[:, :, :], xh[:, :, :].bitcast(F32), ALU.subtract).then_inc(S["xl"], 1)

            def up(c):
                for ft in range(FT):
                    b, use = ft % 2, c * (FT // 2) + ft // 2
                    s = ft % GS
                    dve.wait_ge(S2["up"][b], use + 1)
                    dve.wait_ge(S["gate"], c * FT + ft + 1)
                    both = gates[:, s, :, :].rearrange("p a t -> p (a t)")
                    dve.tensor_tensor(both, ps[:, b, :], both, ALU.mult).then_inc(S2["prod"][b], 1)
                    dve.wait_ge(S2["prod"][b], use + 1)
                    dve.tensor_tensor(gates[:, s, 0, :], gates[:, s, 0, :], gates[:, s, 1, :], ALU.add).then_inc(S2["sum"][b], 1)
                    if ft:
                        low(c, ft - 1)
                low(c, FT - 1)

            def low(c, ft):
                b, use = ft % 2, c * (FT // 2) + ft // 2
                dve.wait_ge(S2["mhi"][b], use + 1)
                dve.tensor_tensor(ml[:, ft, :], gates[:, ft % GS, 0, :], mh[:, ft, :].bitcast(F32), ALU.subtract).then_inc(S["mlo"], 1)

            def out(c):
                for b in range(2):
                    s = lambda n: st[:, b, n:n + 1]
                    dve.wait_ge(S2["out"][b], c + 1)
                    dve.wait_ge(S2["res_in"][b], 16 * (c + 1))
                    dve.tensor_tensor(res[:, b, :].rearrange("p (a n) -> p a n", a=2), ps[:, 2 + 2 * b:4 + 2 * b, :],
                                      res[:, b, :].rearrange("p (a n) -> p a n", a=2), ALU.add).then_inc(S2["x1"][b], 1)
                for b in range(2):
                    s = lambda n: st[:, b, n:n + 1]
                    dve.wait_ge(S2["sq"][b], c + 1)
                    dve.tensor_scalar(s(1), s(0), 1.0 / D, EPS, ALU.mult, ALU.add).then_inc(S2["ms"][b], 1)
                    dve.wait_ge(S2["rt"][b], c + 1)
                    chain[b].turn(c)
                    chain[b].link(dve, dve.reciprocal(s(3), s(2)))
                    newton(dve, chain[b], s(3), s(1), s(2))
                    dve.wait_ge(S2["xn_out"][b], 16 * c)
                    dve.wait_ge(S2["tr"][b], c)
                    dve.scalar_tensor_tensor(xn[:, b, :], res[:, b, :], s(3), g[:, :], ALU.mult, ALU.mult).then_inc(S2["xn"][b], 1)

            def tail(c):
                for b in range(2):
                    dve.wait_ge(S2["rt_mm"][b], c + 1)
                    dve.tensor_reduce(st[:, b, 4:5], ps[:, 6 + b, 0:E], AX.X, ALU.max, negate=True).then_inc(S2["nmax"][b], 1)
                for b in range(2):
                    dve.wait_ge(S2["ex"][b], c + 1)
                    chain2[b].turn(c)
                    chain2[b].link(dve, dve.reciprocal(st[:, b, 6:7], st[:, b, 5:6]))
                    dve.wait_ge(S2["aff_tr"][b], c)
                    dve.tensor_scalar(lg[:, b, 1, :], lg[:, b, 0, :], st[:, b, 6:7], None, ALU.mult).then_inc(S2["aff"][b], 1)

            def late(c):
                pass

            walk(split, up, tail, out, late, dve.Fori)


class TopK:

    def __init__(self, core, mem, aff):
        sb = lambda name, shape, dt=F32: mem.enter_context(core.nc.sbuf_tensor(name, shape, dt))
        self.core, self.aff = core, aff
        self.val = sb("t_val", [E, CAP])
        self.pos = sb("t_pos", [E, CAP], U32)
        self.posf = sb("t_posf", [E, CAP])
        self.idx = (sb("idx_s", [CAP_S, E], U32), sb("idx_p", [CAP_P, E], U32))
        self.gate = (sb("gate_s", [CAP_S, E]), sb("gate_p", [CAP_P, E]))
        self.chain = Chain(core.sem("t_chain"), 0)
        self.tr_done, self.done = core.sem("t_tr_done"), core.sem("t_done")

    def vector(self, dve):
        link = lambda ins: self.chain.link(dve, ins)
        val, pos, posf, ps = self.val, self.pos, self.posf, self.core.ps
        for tokens, slots in ((slice(N_SAMPLE, T), slice(CAP_S, CAP)), (slice(0, N_SAMPLE), slice(0, CAP_S))):
            a = self.aff[:, tokens]
            for n in range(slots.start, slots.stop, 8):
                v8 = val[:, n:n + 8]
                link(dve.max(v8, a))
                self.chain.step(dve.max_index(pos[:, n:n + 8], v8, a))
                link(dve.match_replace(a, v8, a, -1.0))
        link(dve.tensor_copy(posf[:, :], pos[:, :]))
        link(dve.tensor_scalar(posf[:, CAP_S:CAP], posf[:, CAP_S:CAP], float(N_SAMPLE), None, ALU.add))
        dve.wait_ge(self.tr_done, 1)
        dve.tensor_copy(self.idx[0][:, :], ps[:, 0, 0:E])
        dve.tensor_copy(self.idx[1][:, :], ps[0:CAP_P, 1, 0:E])
        dve.tensor_copy(self.gate[0][:, :], ps[:, 2, 0:E])
        dve.tensor_copy(self.gate[1][:, :], ps[0:CAP_P, 3, 0:E]).then_inc(self.done, 1)
        dve.wait_ge(self.done, 1)

    def tensor(self, pe):
        pe.wait_ge(self.chain.sem, 3 * (CAP // 8) + 2)
        i16, ps = self.core.ident[0:E, 0:E], self.core.ps
        pe.transpose(ps[:, 0, 0:E], self.posf[:, 0:CAP_S], i16)
        pe.transpose(ps[0:CAP_P, 1, 0:E], self.posf[:, CAP_S:CAP], i16)
        pe.transpose(ps[:, 2, 0:E], self.val[:, 0:CAP_S], i16)
        pe.transpose(ps[0:CAP_P, 3, 0:E], self.val[:, CAP_S:CAP], i16).then_inc(self.tr_done, 1)


class HeldWeights:

    def __init__(self, core, mem, tag, source, k_tiles):
        self.kt = k_tiles
        self.hi = mem.enter_context(core.nc.sbuf_tensor(f"{tag}_hi", [P, k_tiles, D], F32R))
        self.lo = mem.enter_context(core.nc.sbuf_tensor(f"{tag}_lo", [P, k_tiles, D], F32R))
        self.source = source.rearrange("(k p) n -> p k n", p=P)


class Splitter:

    def __init__(self, core, tag, pieces):
        self.pieces = [(w.source[:, k, c], w.hi[:, k, c], w.lo[:, k, c], raw) for w, k, c, raw in pieces]
        self.loaded = core.sems(f"{tag}_loaded", len(pieces))
        self.high_done, self.done = core.sem(f"{tag}_high"), core.sem(f"{tag}_done")

    def load(self, eng):
        for sem, (source, _, _, raw) in zip(self.loaded, self.pieces):
            eng.dma_start(raw, source).then_inc(sem, 16)

    def high(self, act):
        for sem, (_, hi, _, raw) in zip(self.loaded, self.pieces):
            act.wait_ge(sem, 16)
            act.activation(hi, raw, ACT.Copy).then_inc(self.high_done, 1)

    def low(self, eng):
        for n, (_, hi, lo, raw) in enumerate(self.pieces):
            eng.wait_ge(self.high_done, n + 1)
            eng.tensor_tensor(lo, raw, hi.bitcast(F32), ALU.subtract).then_inc(self.done, 1)

    def wait(self, eng):
        eng.wait_ge(self.done, len(self.pieces))


def stage_experts(core, spare, ahead):
    nc, io = core.nc, core.io
    FB = FF // WB
    FT, DT = FF // P, D // P
    groups = ((0, CAP_S, 0), (1, CAP_P, CAP_S))
    with ExitStack() as mem:
        sb = lambda name, shape, dt=F32: mem.enter_context(nc.sbuf_tensor(name, shape, dt))
        top = TopK(core, mem, spare[0:E, :])
        idx, gate = top.idx, top.gate
        w_gu = [sb(f"e_w_gu{n}", [P, 2, KT, WB]) for n in range(FB)]
        w_d = [sb(f"e_w_d{n}", [P, KT, WB]) for n in range(FB)]
        rows = [sb("e_rows_s", [CAP_S, D]), sb("e_rows_p", [CAP_P, D])]
        x = sb("e_x", [P, KT, CAP])
        h = spare[:, :].rearrange("p (k c) -> p k c", c=CAP)
        sig = sb("e_sig", [P, 2, CAP])
        yt = sb("e_yt", [P, 2, CAP])
        y = [sb("e_y_s", [CAP_S, D]), sb("e_y_p", [CAP_P, D])]
        at_get = [sb("e_at_get_s", [CAP_S, 1], U32), sb("e_at_get_p", [CAP_P, 1], U32)]
        at_put = [sb("e_at_put_s", [CAP_S, 1], U32), sb("e_at_put_p", [CAP_P, 1], U32)]
        gu_in, gu_used = core.sems("e_gu_in", FB), core.sems("e_gu_used", FB)
        d_in, d_used = core.sems("e_d_in", FB), core.sems("e_d_used", FB)
        names = "get_ready rows_in x_tr x_read put_ready added y_tr y_read"
        S = {n: core.sem("e_s_" + n) for n in names.split()}
        S2 = {n: core.sems("e_s_" + n, 2) for n in "gu sig silu hid dn dn_read".split()}
        w_gate, w_proj = ahead
        splitter = Splitter(core, "e_ahead", [(w_gate, slice(0, KT), slice(n * WB, (n + 1) * WB), w_d[n][:, :, :]) for n in range(FB)]
                            + [(w_proj, slice(k, k + 1), slice(0, D), (rows, y)[k][0][:, :].rearrange("p (o c) -> p o c", o=1))
                               for k in range(2)])
        ps = core.ps
        x_groups = ((0, range(0, 3)), (2, range(3, 6)), (4, range(6, 8)))
        XG = len(x_groups)
        x_bank = lambda n: n % 2
        UP_AT = 256
        block = mem.enter_context(nc.Block())

        @block.sync
        def _(sp):
            cols = lambda w, e, n: w[ds(e, 1), :, n * WB:(n + 1) * WB].rearrange("o (k p) c -> (o p) k c", p=P)
            splitter.load(sp)
            with sp.Fori(0, E) as e:
                for n in range(FB):
                    sp.wait_ge(gu_used[n], e)
                    for m, w in enumerate(("w_gate_e", "w_up_e")):
                        sp.dma_start(w_gu[n][:, m, :, :], cols(io[w], e, n)).then_inc(gu_in[n], 16)
                splitter.wait(sp)
                for n in range(FB):
                    sp.wait_ge(d_used[n], e)
                    sp.dma_start(w_d[n][:, :, :], cols(io["w_down_e"], e, n)).then_inc(d_in[n], 16)

        @block.gpsimd
        def _(pool):
            def gather(e):
                pool.wait_ge(S["x_tr"], e * XG)
                for g, size, _ in groups:
                    pool.tensor_copy(at_get[g][:, :], idx[g][:, ds(e, 1)]).then_inc(S["get_ready"], 1)
                pool.wait_ge(S["get_ready"], e * 2 + 2)
                for g, size, _ in groups:
                    pool.nop(nofuse=True)
                    pool.indirect_dma_start(rows[g][:, :], None, core.xm, bass.IndirectOffsetOnAxis(ap=at_get[g][:, 0:1], axis=0)
                                            ).then_inc(S["rows_in"], 16)

            def add(e):
                pool.wait_ge(S["added"], e * 32)
                for g, size, _ in groups:
                    pool.tensor_copy(at_put[g][:, :], idx[g][:, ds(e, 1)]).then_inc(S["put_ready"], 1)
                pool.wait_ge(S["put_ready"], e * 2 + 2)
                pool.wait_ge(S["y_read"], e * 4 + 4)
                for g, size, _ in groups:
                    pool.nop(nofuse=True)
                    pool.indirect_dma_start(core.x_res, bass.IndirectOffsetOnAxis(ap=at_put[g][:, 0:1], axis=0), y[g][:, :], None,
                                            compute_op=ALU.add).then_inc(S["added"], 16)

            splitter.low(pool)
            splitter.wait(pool)
            pool.wait_ge(top.done, 1)
            gather(0)
            with pool.Fori(0, E - 1) as e:
                gather(e + 1)
                add(e)
            add(E - 1)
            pool.wait_ge(S["added"], 32 * E)

        @block.tensor
        def _(pe):
            top.tensor(pe)

            def turn(e, n):
                pe.wait_ge(S["rows_in"], e * 32 + 32)
                pe.wait_ge(S["x_read"], e * XG + max(n - 1, 0) if n < 2 else e * XG + 1)
                for k in x_groups[n][1]:
                    for g, size, first in groups:
                        o = (k - x_groups[n][1][0]) * CAP + first
                        last = pe.transpose(ps[:, x_bank(n), o:o + size], rows[g][:, k * P:(k + 1) * P], core.ident[0:size, 0:size])
                last.then_inc(S["x_tr"], 1)

            def gate_up(e):
                pe.wait_ge(S["x_read"], e * XG + XG)
                for ft in range(FT):
                    b, n = ft % 2, ft // 2
                    if b == 0:
                        pe.wait_ge(gu_in[n], e * 32 + 32)
                    pe.wait_ge(S2["hid"][b], e * (FT // 2) + ft // 2)
                    cols = slice((ft % 2) * P, (ft % 2 + 1) * P)
                    for m, at in ((0, 0), (1, UP_AT)):
                        for k in range(KT):
                            last = pe.matmul(ps[:, 3 + b, at:at + CAP], w_gu[n][:, m, k, cols], x[:, k, :], start=(k == 0),
                                             stop=(k == KT - 1))
                    last.then_inc(S2["gu"][b], 1) if b == 0 else last.then_inc(gu_used[n], 1)

            def turn_back(e, dt):
                b = dt % 2
                pe.wait_ge(S2["dn_read"][b], e * (DT // 2) + dt // 2 + 1)
                half, o = dt // 4, (dt % 4) * P
                if dt % 4 == 0:
                    pe.wait_ge(S["y_read"], e * 4 + half * 2)
                pe.transpose(ps[:, 2, o:o + P], yt[:, b, 0:CAP_S], core.ident[:, :])
                last = pe.transpose(ps[0:CAP_P, 5, o:o + P], yt[:, b, CAP_S:CAP], core.ident[:, :])
                if dt % 4 == 3:
                    last.then_inc(S["y_tr"], 1)

            def down(e, then):
                for dt in range(DT):
                    b, n = dt % 2, dt // 2
                    if b == 0:
                        pe.wait_ge(d_in[n], e * 16 + 16)
                    pe.wait_ge(S2["dn_read"][b], e * (DT // 2) + dt // 2)
                    for k in range(KT):
                        if dt == 0 and k >= KT - 2:
                            pe.wait_ge(S2["hid"][k % 2], e * (FT // 2) + FT // 2)
                        last = pe.matmul(ps[:, 6 + b, 0:CAP], w_d[n][:, k, b * P:(b + 1) * P], h[:, k, :], start=(k == 0),
                                         stop=(k == KT - 1))
                    last.then_inc(S2["dn"][b], 1) if b == 0 else last.then_inc(d_used[n], 1)
                    then(dt)
                    if dt:
                        turn_back(e, dt - 1)
                turn_back(e, DT - 1)

            def turn_next(e):
                def after(dt):
                    for n, (at, _) in enumerate(x_groups):
                        if dt == at:
                            turn(e + 1, n)
                return after

            pe.wait_ge(top.done, 1)
            for n in range(XG):
                turn(0, n)
            with pe.Fori(0, E - 1) as e:
                gate_up(e)
                down(e, turn_next(e))
            gate_up(E - 1)
            down(E - 1, lambda dt: None)

        def gu_done(eng, e, ft):
            if ft % 2 == 0:
                eng.wait_ge(S2["gu"][0], e * (FT // 2) + ft // 2 + 1)
            else:
                eng.wait_ge(gu_used[ft // 2], e + 1)

        @block.scalar
        def _(act):
            splitter.high(act)

            def read_turned(e, n):
                ks = x_groups[n][1]
                act.wait_ge(S["x_tr"], e * XG + n + 1)
                act.activation(x[:, ks[0]:ks[0] + len(ks), :], ps[:, x_bank(n), 0:len(ks) * CAP].rearrange("p (k c) -> p k c", c=CAP),
                               ACT.Copy).then_inc(S["x_read"], 1)

            def hidden(e):
                for ft in range(FT):
                    b = ft % 2
                    gu_done(act, e, ft)
                    act.wait_ge(S2["hid"][b], e * (FT // 2) + ft // 2)
                    act.activation(sig[:, b, :], ps[:, 3 + b, 0:CAP], ACT.Sigmoid).then_inc(S2["sig"][b], 1)

            def down(e, then):
                for dt in range(DT):
                    b = dt % 2
                    if b == 0:
                        act.wait_ge(S2["dn"][0], e * (DT // 2) + dt // 2 + 1)
                    else:
                        act.wait_ge(d_used[dt // 2], e + 1)
                    act.activation(yt[:, b, :], ps[:, 6 + b, 0:CAP], ACT.Copy).then_inc(S2["dn_read"][b], 1)
                    then(dt)

            def read_next(e):
                def after(dt):
                    for n, (at, _) in enumerate(x_groups):
                        if dt == at:
                            read_turned(e + 1, n)
                return after

            for n in range(XG):
                read_turned(0, n)
            with act.Fori(0, E - 1) as e:
                hidden(e)
                down(e, read_next(e))
            hidden(E - 1)
            down(E - 1, lambda dt: None)

        @block.vector
        def _(dve):
            top.vector(dve)
            splitter.wait(dve)
            with dve.Fori(0, E) as e:
                for ft in range(FT):
                    b = ft % 2
                    dve.wait_ge(S2["sig"][b], e * (FT // 2) + ft // 2 + 1)
                    dve.tensor_tensor(sig[:, b, :], ps[:, 3 + b, 0:CAP], sig[:, b, :], ALU.mult).then_inc(S2["silu"][b], 1)
                    dve.wait_ge(S2["silu"][b], e * (FT // 2) + ft // 2 + 1)
                    if ft == 0:
                        dve.wait_ge(d_used[FB - 1], e)
                    dve.tensor_tensor(h[:, ft, :], ps[:, 3 + b, UP_AT:UP_AT + CAP], sig[:, b, :], ALU.mult).then_inc(S2["hid"][b], 1)
                dve.wait_ge(S["added"], e * 32)
                for half in range(2):
                    dve.wait_ge(S["y_tr"], e * 2 + half + 1)
                    for g, size, _ in groups:
                        dve.tensor_scalar(y[g][:, half * 512:(half + 1) * 512], ps[0:size, (2, 5)[g], :], gate[g][:, ds(e, 1)], None,
                                          ALU.mult).then_inc(S["y_read"], 1)


def stage_ple(core, w_gate, w_proj):
    nc, io = core.nc, core.io
    PT = PLE // P
    with ExitStack() as mem:
        sb = lambda name, shape, dt=F32: mem.enter_context(nc.sbuf_tensor(name, shape, dt))
        x = sb("l_x", [P, 2, D])
        xn = sb("l_xn", [P, 2, D])
        g1, g2 = sb("l_gain", [P, D]), sb("l_gain_final", [P, D])
        p = sb("l_p", [P, 2, PLE])
        AT = KT + PT
        th, tl = sb("l_th", [P, 2, AT, P], F32R), sb("l_tl", [P, 2, AT, P], F32R)
        sig = sb("l_sig", [P, 2, D])
        y = sb("l_y", [P, 2, D])
        st = sb("l_stat", [P, 2, 8])
        S = {"const": core.sem("l_s_const")}
        S2 = {n: core.sems("l_s_" + n, 2) for n in "x_in sq ms rt xn tr hi lo gate proj sig mul res sq2 ms2 rt2 y out".split()}
        c1 = [Chain(core.sem(f"l_chain_a{b}"), 1 + NEWTON) for b in range(2)]
        c2 = [Chain(core.sem(f"l_chain_b{b}"), 1 + NEWTON) for b in range(2)]
        ps = core.ps
        tbanks = [range(0, 4), range(4, 8), range(8, AT)]
        H = NT // 2
        block = mem.enter_context(nc.Block())

        def walk(norm, turn, gate, proj, close, loop):
            norm(0, 0)
            turn(0, 0)
            norm(0, 1)
            with loop(0, H - 1) as i:
                for b in range(2):
                    gate(i, b)
                    turn(i + b, 1 - b)
                    proj(i, b)
                    close(i, b)
                    norm(i + 1, b)
            gate(H - 1, 0)
            turn(H - 1, 1)
            proj(H - 1, 0)
            close(H - 1, 0)
            gate(H - 1, 1)
            proj(H - 1, 1)
            close(H - 1, 1)

        def skip(i, b):
            pass

        @block.sync
        def _(sp):
            def load(i, b):
                rows = ds(i * 2 * P + b * P, P)
                sp.wait_ge(S2["res"][b], i)
                sp.wait_ge(S2["tr"][b], i)
                sp.dma_start(x[:, b, :], core.x_res[rows, :]).then_inc(S2["x_in"][b], 16)
                sp.dma_start(p[:, b, :], io["p"][rows, :]).then_inc(S2["x_in"][b], 16)

            def store(i, b):
                sp.wait_ge(S2["y"][b], i + 1)
                sp.dma_start(io["out"][ds(i * 2 * P + b * P, P), :], y[:, b, :]).then_inc(S2["out"][b], 16)

            load(0, 0)
            sp.dma_start(g1[:, :], io["g_ple"].partition_broadcast(P)).then_inc(S["const"], 16)
            load(0, 1)
            sp.dma_start(g2[:, :], io["g_final"].partition_broadcast(P)).then_inc(S["const"], 16)
            with sp.Fori(0, H - 1) as i:
                for b in range(2):
                    load(i + 1, b)
                    store(i, b)
            for b in range(2):
                store(H - 1, b)
            for b in range(2):
                sp.wait_ge(S2["out"][b], 16 * H)

        @block.tensor
        def _(pe):
            def turn(i, b):
                pe.wait_ge(S2["xn"][b], i + 1)
                pe.wait_ge(S2["lo"][1 - b], i + b)
                for n, ks in enumerate(tbanks):
                    for k in ks:
                        src = xn[:, b, k * P:(k + 1) * P] if k < KT else p[:, b, (k - KT) * P:(k - KT + 1) * P]
                        last = pe.transpose(ps[:, n, (k - ks[0]) * P:(k - ks[0] + 1) * P], src, core.ident[:, :])
                last.then_inc(S2["tr"][b], 1)

            def product(b, first, w, bank):
                for half in range(2):
                    cols = slice(half * 512, (half + 1) * 512)
                    for k in range(w.kt):
                        last = split3(pe, ps[:, bank + half, :], (th[:, b, first + k, :], tl[:, b, first + k, :]),
                                      (w.hi[:, k, cols], w.lo[:, k, cols]), k == 0, k == w.kt - 1)
                return last

            def gate(i, b):
                pe.wait_ge(S2["lo"][b], i + 1)
                pe.wait_ge(S2["sig"][1 - b], i + b)
                product(b, 0, w_gate, 3).then_inc(S2["gate"][b], 1)

            def proj(i, b):
                pe.wait_ge(S2["mul"][1 - b], i + b)
                product(b, KT, w_proj, 5).then_inc(S2["proj"][b], 1)

            walk(skip, turn, gate, proj, skip, pe.Fori)

        @block.scalar
        def _(act):
            def norm(i, b):
                act.wait_ge(S2["x_in"][b], i * 32 + 32)
                act.activation(sig[:, b, :], x[:, b, :], ACT.Square, accum_out=st[:, b, 0:1]).then_inc(S2["sq"][b], 1)
                act.wait_ge(S2["ms"][b], i + 1)
                act.activation(st[:, b, 2:3], st[:, b, 1:2], ACT.Sqrt).then_inc(S2["rt"][b], 1)

            def turn(i, b):
                act.wait_ge(S2["tr"][b], i + 1)
                act.wait_ge(S2["proj"][b], i)
                for n, ks in enumerate(tbanks):
                    ins = act.activation(th[:, b, ks[0]:ks[0] + len(ks), :],
                                         ps[:, n, 0:len(ks) * P].rearrange("p (k c) -> p k c", c=P), ACT.Copy)
                ins.then_inc(S2["hi"][b], 1)

            def gate(i, b):
                act.wait_ge(S2["gate"][b], i + 1)
                act.wait_ge(S2["rt"][b], i + 1)
                act.activation(sig[:, b, :].rearrange("p (a n) -> p a n", a=2), ps[:, 3:5, :], ACT.Sigmoid).then_inc(S2["sig"][b], 1)

            def close(i, b):
                act.wait_ge(S2["res"][b], i + 1)
                act.activation(sig[:, b, :], y[:, b, :], ACT.Square, accum_out=st[:, b, 4:5]).then_inc(S2["sq2"][b], 1)
                act.wait_ge(S2["ms2"][b], i + 1)
                act.activation(st[:, b, 6:7], st[:, b, 5:6], ACT.Sqrt).then_inc(S2["rt2"][b], 1)

            walk(norm, turn, gate, skip, close, act.Fori)

        @block.vector
        def _(dve):
            dve.wait_ge(S["const"], 32)

            def rstd(i, b, chain, at, ms, rt, sq):
                s = lambda n: st[:, b, at + n:at + n + 1]
                dve.wait_ge(S2[sq][b], i + 1)
                dve.tensor_scalar(s(1), s(0), 1.0 / D, EPS, ALU.mult, ALU.add).then_inc(S2[ms][b], 1)
                dve.wait_ge(S2[rt][b], i + 1)
                chain[b].turn(i)
                chain[b].link(dve, dve.reciprocal(s(3), s(2)))
                newton(dve, chain[b], s(3), s(1), s(2))
                return s(3)

            def norm(i, b):
                rs = rstd(i, b, c1, 0, "ms", "rt", "sq")
                dve.wait_ge(S2["tr"][b], i)
                dve.scalar_tensor_tensor(xn[:, b, :], x[:, b, :], rs, g1[:, :], ALU.mult, ALU.mult).then_inc(S2["xn"][b], 1)

            def turn(i, b):
                dve.wait_ge(S2["hi"][b], i + 1)
                for n, ks in enumerate(tbanks):
                    t = slice(ks[0], ks[0] + len(ks))
                    ins = dve.tensor_tensor(tl[:, b, t, :], ps[:, n, 0:len(ks) * P].rearrange("p (k c) -> p k c", c=P),
                                            th[:, b, t, :].bitcast(F32), ALU.subtract)
                ins.then_inc(S2["lo"][b], 1)

            def close(i, b):
                halves = lambda a: a[:, b, :].rearrange("p (a n) -> p a n", a=2)
                dve.wait_ge(S2["sig"][b], i + 1)
                dve.wait_ge(S2["proj"][b], i + 1)
                dve.wait_ge(S2["out"][b], i * 16)
                dve.tensor_tensor(halves(y), halves(sig), ps[:, 5:7, :], ALU.mult).then_inc(S2["mul"][b], 1)
                dve.wait_ge(S2["mul"][b], i + 1)
                dve.tensor_tensor(y[:, b, :], y[:, b, :], x[:, b, :], ALU.add).then_inc(S2["res"][b], 1)
                rs = rstd(i, b, c2, 4, "ms2", "rt2", "sq2")
                dve.scalar_tensor_tensor(y[:, b, :], y[:, b, :], rs, g2[:, :], ALU.mult, ALU.mult).then_inc(S2["y"][b], 1)

            walk(norm, turn, skip, skip, close, dve.Fori)


def program(nc, io, stages=None):
    with ExitStack() as ctx:
        core = Core(nc, ctx, io)
        with ExitStack() as act_mem:
            ah = act_mem.enter_context(nc.sbuf_tensor("act_hi", [P, KT, T], F32R))
            al = act_mem.enter_context(nc.sbuf_tensor("act_lo", [P, KT, T], F32R))
            stage_norm(core, ah, al)
            ring = WeightRing(core, act_mem)
            stage_token_major(core, ah, al, ring)
            qt = act_mem.enter_context(nc.sbuf_tensor("q_t", [P, HEADS // 2, T], F32))
            kt = act_mem.enter_context(nc.sbuf_tensor("k_t", [P, KV_HEADS, T], F32))
            v = act_mem.enter_context(nc.sbuf_tensor("v_tok", [P, NT, KV_HEADS * HD], F32))
            stage_rope(core, ah, al, ring, qt, kt, v)
            stage_attention(core, ah, al, ring, qt, kt, v)
        stage_gla(core)
        core.recycle_sems()
        with ExitStack() as tail_mem:
            aff_hidden = tail_mem.enter_context(nc.sbuf_tensor("aff_hidden", [P, T], F32))
            stage_merge(core, aff_hidden[0:E, :])
            ple_gate = HeldWeights(core, tail_mem, "w_ple_gate", io["w_ple_gate"], KT)
            ple_proj = HeldWeights(core, tail_mem, "w_ple_proj", io["w_ple_proj"], PLE // P)
            stage_experts(core, aff_hidden, (ple_gate, ple_proj))
            stage_ple(core, ple_gate, ple_proj)


def host_inputs(**a):
    import numpy as np

    w = {k: np.asarray(v) for k, v in a.items()}
    out = {"ident": np.eye(P, dtype=np.float32)}
    out["x"] = np.concatenate([w["x_sample"][0], w["x_prompt"][0]])
    out["g_mix"] = w["g_mix"][0]
    for name in ("q_norm", "k_norm", "w_router", "w_gate_e", "w_up_e", "w_down_e", "w_out", "w_ple_gate", "w_ple_proj",
                 "g_moe", "g_ple"):
        out[name] = w[name][0]
    out["g_final"] = w["g_final"]
    out["w_up"] = np.concatenate([w["w_attn_up"][0], w["w_gla_up"][0]])
    out["p"] = np.concatenate([w["p_sample"][0, 0], w["p_prompt"][0, 0]])
    inv = (np.float32(10000.0) ** (-np.arange(0, 32, 2, dtype=np.float32) / np.float32(32))).astype(np.float32)
    pos = np.concatenate([np.arange(N_SAMPLE), np.arange(N_PROMPT)])
    row, col = ((n.astype(np.float32)[:, None] * inv).astype(np.float32) for n in (pos // 64, pos % 64))
    cos = np.concatenate([np.cos(a) for a in (row, row, col, col)], axis=1)
    sin = np.concatenate([-np.sin(row), np.sin(row), -np.sin(col), np.sin(col)], axis=1)
    out["rope"] = np.stack([cos, sin], axis=1).astype(np.float32).reshape(NT, P, 2, HD)
    lora_w = np.zeros((2 * LORA, 2, GLA_HP, P), np.float32)
    lora_w[:LORA, 0] = w["w_af"][0].reshape(LORA, GLA_HP, P)
    lora_w[LORA:, 1] = w["w_ab"][0].reshape(LORA, GLA_HP, P)
    out["w_lora"] = lora_w
    out["b_lora"] = np.ascontiguousarray(np.stack([w["b_af"][0], w["b_ab"][0]]).reshape(2, GLA_HP, P).transpose(2, 0, 1))
    out["gla_norm"] = w["gla_norm"][0].reshape(DV, 1)
    s_, t_ = np.arange(P)[:, None], np.arange(P)[None, :]
    masks = [(s_ // (2 * m) == t_ // (2 * m)) & (s_ // m != t_ // m) for m in LEVELS] + [s_ == t_]
    out["level_masks"] = np.ascontiguousarray(np.stack(masks, axis=1).astype(np.int32))
    w_in = w["w_in"][0]
    a0 = QKV_W
    qkv, lq_lk = w_in[:, :a0], w_in[:, a0:a0 + 2 * GLA_H * DK]
    a1 = a0 + 2 * GLA_H * DK
    lv, lr = w_in[:, a1:a1 + GLA_H * DV], w_in[:, a1 + GLA_H * DV:a1 + 2 * GLA_H * DV]
    a2 = a1 + 2 * GLA_H * DV
    lora, gates = w_in[:, a2:a2 + 2 * LORA], w_in[:, a2 + 2 * LORA:]
    pad = np.zeros((D, WB - 2 * LORA), np.float32)
    cols = np.concatenate([qkv, lv, lq_lk, lr, lora, pad, gates], axis=1)
    out["w_blk"] = np.ascontiguousarray(cols.reshape(KT, P, W_BLOCKS, WB).transpose(2, 1, 0, 3))
    return out


def kernel(**inputs):
    import numpy as np
    import concourse.bacc as bacc
    from concourse.bass_utils import run_bass_kernel_spmd

    nc = bacc.Bacc("TRN2", target_bir_lowering=False, num_devices=1)
    arrays = {f"in_{n}": a for n, a in host_inputs(**inputs).items()}
    io = {n[3:]: nc.dram_tensor(n, a.shape, mybir.dt.from_np(a.dtype), kind="ExternalInput").ap() for n, a in arrays.items()}
    io["out"] = nc.dram_tensor("out", (T, D), F32, kind="ExternalOutput").ap()
    program(nc, io)
    out = run_bass_kernel_spmd(nc, [arrays], core_ids=[0]).results[0]["out"]
    return out[N_SAMPLE:][None], out[:N_SAMPLE][None]
```

```python
from contextlib import ExitStack

import concourse.bass as bass
from concourse import mybir

ALU = mybir.AluOpType
ACT = mybir.ActivationFunctionType
F32 = mybir.dt.float32
F32R = mybir.dt.float32r
U32 = mybir.dt.uint32
I32 = mybir.dt.int32
AX = mybir.AxisListType
ds = bass.ds

P = 128
D = 1024
KT = D // P
N_SAMPLE, N_PROMPT = 1024, 256
T = N_SAMPLE + N_PROMPT
NT = T // P
NT_S = N_SAMPLE // P
EPS = 1e-6

HEADS, KV_HEADS, HD = 8, 2, 64
QKV_W = (HEADS + 2 * KV_HEADS) * HD
GLA_H, DK, DV, LORA, CHUNK = 4, 64, 128, 16, 64
PAIRS = T // (2 * CHUNK)
GLA_HP = GLA_H // 2
GATE_NORM = 16.0

WB = 256
TM_BLOCKS = (QKV_W + GLA_H * DV) // WB
FM_BLOCKS = (2 * GLA_H * DK + GLA_H * DV + 2 * D) // WB
W_BLOCKS = TM_BLOCKS + FM_BLOCKS + 1
MID_BLOCKS = 5
GATE_BLOCKS = W_BLOCKS - TM_BLOCKS - MID_BLOCKS
FM_TILES = 2 * (MID_BLOCKS + GATE_BLOCKS)
T_LQ, T_LK, T_LR, T_LORA, T_GA = 0, 2, 4, 8, 10
CHUNKS_512 = [(0, 512), (512, 512), (1024, 256)]

E = 16
FF = 1024
CAP_S, CAP_P = 2 * N_SAMPLE // E, 2 * N_PROMPT // E
CAP = CAP_S + CAP_P
PLE = 256
CW = 256
CHUNKS = T // CW
LEVELS = (32, 16, 8, 4, 2, 1)


class Chain:

    def __init__(self, sem, steps):
        self.sem, self.steps, self.at, self.i = sem, steps, 0, 0

    def turn(self, i):
        assert self.at in (0, self.steps), (self.at, self.steps)
        self.at, self.i = 0, i

    def step(self, ins):
        ins.then_inc(self.sem, 1)
        self.at += 1

    def link(self, eng, ins):
        self.step(ins)
        eng.wait_ge(self.sem, self.i * self.steps + self.at)


class Core:

    def __init__(self, nc, ctx, io):
        self.nc, self.ctx, self.io = nc, ctx, io
        self.in_use, self.old = [], []
        self.ps = ctx.enter_context(nc.psum_tensor("ps", [P, 8, 512], F32))
        self.ident = ctx.enter_context(nc.sbuf_tensor("ident", [P, P], F32))
        dram = lambda name, shape: nc.dram_tensor(name, shape, F32, kind="Internal").ap()
        self.tm = dram("tm_scratch", (TM_BLOCKS, NT, P, WB))
        self.fm = dram("fm_scratch", (FM_TILES, P, T))
        self.up_in = dram("up_in_scratch", (KT, P, T))
        self.x_res = dram("x_res_scratch", (T, D))
        self.xm = dram("xm_scratch", (T, D))

    def bank(self, n, width=512):
        return self.ps[:, n, 0:width]

    def sem(self, name):
        self.in_use.append(self.nc.alloc_semaphore(name=name))
        return self.in_use[-1]

    def sems(self, name, n):
        return [self.sem(f"{name}{b}") for b in range(n)]

    def kept_sems(self, name, n):
        return [self.nc.alloc_semaphore(name=f"{name}{b}") for b in range(n)]

    def stage_memory(self):
        self.old, self.in_use = self.in_use, []
        return ExitStack()

    def clear_old(self, pool):
        for sem in self.old:
            pool.sem_clear(sem)

    def release_old(self):
        for sem in self.old:
            self.nc.release_semaphore(sem)
        self.old = []


def hold(pool):
    pool.nop(nofuse=True)


def newton(dve, chain, rs, ms, tmp):
    chain.link(dve, dve.tensor_tensor(tmp, rs, rs, ALU.mult))
    chain.link(dve, dve.tensor_tensor(tmp, tmp, ms, ALU.mult))
    chain.link(dve, dve.tensor_scalar(tmp, tmp, -0.5, 1.5, ALU.mult, ALU.add))
    chain.link(dve, dve.tensor_tensor(rs, rs, tmp, ALU.mult))


NEWTON = 4


def split3(pe, out, lhs, rhs, start, stop):
    (lh, ll), (rh, rl) = lhs, rhs
    pe.matmul(out, lh, rh, start=start, stop=False)
    pe.matmul(out, lh, rl, start=False, stop=False)
    return pe.matmul(out, ll, rh, start=False, stop=stop)


class HeldWeights:

    def __init__(self, source):
        self.source = source.rearrange("(k p) n -> p k n", p=P)
        self.kt = self.source.shape[1]

    def place(self, core, mem, tag):
        self.hi, self.lo = (mem.enter_context(core.nc.sbuf_tensor(f"{tag}_{half}", [P, self.kt, D], F32R)) for half in ("hi", "lo"))


class Splitter:

    def __init__(self, core, tag, pieces):
        self.pieces = pieces
        self.loaded = core.kept_sems(f"{tag}_loaded", len(pieces))
        self.high_done, self.done = core.kept_sems(f"{tag}_split", 2)

    def load(self, eng, n):
        w, k, c, raw = self.pieces[n]
        eng.dma_start(raw, w.source[:, k, c]).then_inc(self.loaded[n], 16)

    def wait_piece(self, eng, n):
        eng.wait_ge(self.done, n + 1)

    def high(self, act, n):
        w, k, c, raw = self.pieces[n]
        act.wait_ge(self.loaded[n], 16)
        act.activation(w.hi[:, k, c], raw, ACT.Copy).then_inc(self.high_done, 1)

    def low(self, eng, n):
        w, k, c, raw = self.pieces[n]
        eng.wait_ge(self.high_done, n + 1)
        eng.tensor_tensor(w.lo[:, k, c], raw, w.hi[:, k, c].bitcast(F32), ALU.subtract).then_inc(self.done, 1)

    def wait(self, eng):
        eng.wait_ge(self.done, len(self.pieces))


def nth(first, i=0, per=0):
    assert per % 2 == 0
    return i * per + first, first % 2, i * (per // 2) + first // 2


class WeightRing:

    def __init__(self, core, mem):
        sb = lambda name, dt: [mem.enter_context(core.nc.sbuf_tensor(f"{name}{b}", [P, KT, WB], dt)) for b in range(2)]
        self.raw = mem.enter_context(core.nc.sbuf_tensor("w_raw", [P, KT, WB], F32))
        self.hi, self.lo = sb("w_hi", F32R), sb("w_lo", F32R)
        self.blocks = core.io["w_blk"]
        self.loaded, self.high_done, self.low_done, self.used = (core.kept_sems("w_" + x, 2) for x in "loaded high low used".split())

    def load(self, eng, block):
        n, b, use = block
        eng.wait_ge(self.low_done[1 - b], use + b)
        n = n if isinstance(n, int) else ds(n, 1)
        src = self.blocks[n:n + 1] if isinstance(n, int) else self.blocks[n]
        eng.dma_start(self.raw[:, :, :], src.rearrange("o p k c -> (o p) k c")).then_inc(self.loaded[b], 16)

    def high(self, act, block):
        _, b, use = block
        act.wait_ge(self.loaded[b], use * 16 + 16)
        act.wait_ge(self.used[b], use)
        act.activation(self.hi[b][:, :, :], self.raw[:, :, :], ACT.Copy).then_inc(self.high_done[b], 1)

    def low(self, eng, block):
        _, b, use = block
        eng.wait_ge(self.high_done[b], use + 1)
        eng.tensor_tensor(self.lo[b][:, :, :], self.raw[:, :, :], self.hi[b][:, :, :].bitcast(F32),
                          ALU.subtract).then_inc(self.low_done[b], 1)

    def ready(self, pe, block):
        _, b, use = block
        pe.wait_ge(self.low_done[b], use + 1)


def stage_norm_and_token_major(core, ah, al, ring):
    nc, io = core.nc, core.io
    with ExitStack() as mem:
        sb = lambda name, shape, dt=F32: mem.enter_context(nc.sbuf_tensor(name, shape, dt))
        g = sb("n_gain", [P, D])
        x = sb("n_x", [P, 2, D])
        sq = sb("n_sq", [P, 2, D])
        xn = sb("n_xn", [P, 2, D])
        st = sb("n_stat", [P, 2, 4])
        SLOTS = 5
        out = sb("tm_out", [P, SLOTS, WB])
        s_const = core.sem("n_const")
        x_in = core.sems("n_x_in", 2)
        sq_done = core.sems("n_sq_done", 2)
        ms_done = core.sems("n_ms_done", 2)
        rt_done = core.sems("n_rt_done", 2)
        rs_chain = [Chain(core.sem(f"n_rs_chain{b}"), 1 + NEWTON) for b in range(2)]
        xn_done = core.sems("n_xn_done", 2)
        tr_done = core.sem("n_tr_done")
        hi_done = core.sem("n_hi_done")
        lo_done = core.sem("n_lo_done")
        done = core.sems("tm_done", SLOTS)
        read = core.sems("tm_read", SLOTS)
        stored = core.kept_sems("tm_stored", SLOTS)
        pt = core.ps[:, 5:7, :]
        turned = pt.rearrange("p a (c n) -> p (a c) n", n=P)
        FIRST = 2
        order = [(n, t) for t in range(NT) for n in range(FIRST)] + [(n, t) for n in range(FIRST, TM_BLOCKS) for t in range(NT)]
        signals = lambda m: sum(o[1] < NT - 1 for o in order[m % SLOTS:m:SLOTS])
        block = mem.enter_context(nc.Block())

        def walk(split, norm, turn, product):
            products = iter(range(len(order)))
            for n in range(FIRST):
                split(nth(n))
            norm(0)
            norm(1)
            for t in range(NT + 1):
                if t < NT:
                    turn(t)
                if t + 2 < NT:
                    norm(t + 2)
                if t:
                    for _ in range(FIRST):
                        product(next(products))
            for n in range(FIRST, TM_BLOCKS + 1):
                if n == FIRST:
                    split(nth(n))
                if n < TM_BLOCKS:
                    split(nth(n + 1))
                    for t in range(NT):
                        product(next(products))

        def skip(_):
            pass

        tokens = lambda t: slice(t * P, (t + 1) * P)

        @block.sync
        def _(sp):
            def load_x(t):
                sp.wait_ge(xn_done[t % 2], t // 2)
                sp.dma_start(x[:, t % 2, :], io["x"][tokens(t), :]).then_inc(x_in[t % 2], 16)

            load_x(0)
            sp.dma_start(core.ident[:, :], io["ident"]).then_inc(s_const, 16)
            sp.dma_start(g[:, :], io["g_mix"].partition_broadcast(P)).then_inc(s_const, 16)
            ring.load(sp, nth(0))
            load_x(1)
            ring.load(sp, nth(1))
            for t in range(2, NT):
                load_x(t)
            for n in range(FIRST, TM_BLOCKS + 1):
                ring.load(sp, nth(n))

        @block.scalar
        def _(act):
            def norm(t):
                b, use = t % 2, t // 2
                act.wait_ge(x_in[b], use * 16 + 16)
                act.activation(sq[:, b, :], x[:, b, :], ACT.Square, accum_out=st[:, b, 0:1]).then_inc(sq_done[b], 1)
                act.wait_ge(ms_done[b], use + 1)
                act.activation(st[:, b, 2:3], st[:, b, 1:2], ACT.Sqrt).then_inc(rt_done[b], 1)

            def turn(t):
                act.wait_ge(tr_done, t + 1)
                act.activation(ah[:, :, tokens(t)], turned, ACT.Copy).then_inc(hi_done, 1)

            def product(m):
                (n, t), s, use = order[m], m % SLOTS, m // SLOTS
                if t < NT - 1:
                    act.wait_ge(done[s], signals(m) + 1)
                else:
                    act.wait_ge(ring.used[n % 2], n // 2 + 1)
                act.wait_ge(stored[s], use * 16)
                act.activation(out[:, s, :], core.bank(s, WB), ACT.Copy).then_inc(read[s], 1)

            walk(lambda blk: ring.high(act, blk), norm, turn, product)

        @block.vector
        def _(dve):
            def norm(t):
                b, use = t % 2, t // 2
                if t == 0:
                    dve.wait_ge(s_const, 32)
                dve.wait_ge(sq_done[b], use + 1)
                dve.tensor_scalar(st[:, b, 1:2], st[:, b, 0:1], 1.0 / D, EPS, ALU.mult, ALU.add).then_inc(ms_done[b], 1)
                dve.wait_ge(rt_done[b], use + 1)
                rs_chain[b].turn(use)
                rs_chain[b].link(dve, dve.reciprocal(st[:, b, 3:4], st[:, b, 2:3]))
                newton(dve, rs_chain[b], st[:, b, 3:4], st[:, b, 1:2], st[:, b, 2:3])
                if t >= 2:
                    dve.wait_ge(tr_done, t - 1)
                dve.scalar_tensor_tensor(xn[:, b, :], x[:, b, :], st[:, b, 3:4], g[:, :], ALU.mult, ALU.mult).then_inc(xn_done[b], 1)

            def turn(t):
                dve.wait_ge(hi_done, t + 1)
                dve.tensor_tensor(al[:, :, tokens(t)], turned, ah[:, :, tokens(t)].bitcast(F32), ALU.subtract).then_inc(lo_done, 1)

            walk(lambda blk: ring.low(dve, blk), norm, turn, skip)

        @block.gpsimd
        def _(pool):
            def product(m):
                (n, t), s, use = order[m], m % SLOTS, m // SLOTS
                pool.wait_ge(read[s], use + 1)
                pool.dma_start(core.tm[n, t], out[:, s, :]).then_inc(stored[s], 16)

            walk(skip, skip, skip, product)
            for s in range(SLOTS):
                pool.wait_ge(stored[s], 16 * (len(order) // SLOTS))

        @block.tensor
        def _(pe):
            def turn(t):
                if t == 0:
                    pe.wait_ge(s_const, 32)
                pe.wait_ge(xn_done[t % 2], t // 2 + 1)
                pe.wait_ge(lo_done, t)
                for k in range(KT):
                    last = pe.transpose(turned[:, k, :], xn[:, t % 2, k * P:(k + 1) * P], core.ident[:, :])
                last.then_inc(tr_done, 1)

            def product(m):
                (n, t), s, use = order[m], m % SLOTS, m // SLOTS
                b = n % 2
                pe.wait_ge(lo_done, t + 1)
                ring.ready(pe, nth(n))
                pe.wait_ge(read[s], use)
                for k in range(KT):
                    x_t = [a[:, k, tokens(t)] for a in (ah, al)]
                    last = split3(pe, core.bank(s, WB), x_t, (ring.hi[b][:, k, :], ring.lo[b][:, k, :]), k == 0, k == KT - 1)
                last.then_inc(done[s] if t < NT - 1 else ring.used[b], 1)

            walk(skip, skip, turn, product)


def stage_rope(core, ah, al, ring, qt, kt, v):
    nc, io = core.nc, core.io
    H = HEADS + KV_HEADS
    W = H * HD
    KD = 2 * KV_HEADS
    with ExitStack() as mem:
        sb = lambda name, shape, dt=F32: mem.enter_context(nc.sbuf_tensor(name, shape, dt))
        fm_out = sb("fm_out", [P, 2, T])
        gain = sb("r_gain", [P, H, HD])
        x = sb("r_x", [P, 2, W])
        tab = sb("r_tab", [P, 2, 2, HD])
        sq = sb("r_sq", [P, 2, W])
        u = sb("r_u", [P, 2, W])
        out = sb("r_out", [P, 2, (HEADS + KD) * HD])
        st = sb("r_stat", [P, 2, 4, H])
        s_const = core.sem("r_const")
        x_in = core.sems("r_x_in", 2)
        v_in = core.sem("r_v_in")
        ms_done = core.sems("r_ms_done", 2)
        rt_done = core.sems("r_rt_done", 2)
        out_done = core.sems("r_out_done", 2)
        tr_done = core.sem("r_tr_done")
        tr_read = core.sem("r_tr_read")
        fm_done = core.sem("r_fm_done")
        fm_read = core.sems("r_fm_read", 2)
        fm_stored = core.kept_sems("r_fm_stored", 2)
        STEPS = 1 + 1 + 1 + NEWTON + 2 + 1 + 2
        chain = [Chain(core.sem(f"r_chain{b}"), STEPS) for b in range(2)]
        fm_bank = [core.ps[:, 3 * t:3 * t + 3, :] for t in range(2)]
        pt = core.ps[:, 6:8, 0:384]
        PASSES = (MID_BLOCKS - 1) // 2
        assert NT == 4 * PASSES + 2
        block = mem.enter_context(nc.Block())

        def walk(split, fm, rope, loop):
            with loop(0, PASSES) as i:
                for f in range(4):
                    if f % 2 == 0:
                        split(nth(TM_BLOCKS + 1 + f // 2, i, 2))
                    fm(nth(TM_BLOCKS + f // 2, i, 2), f % 2, i * 2 + f // 2)
                    rope(i * 4 + f, f % 2, i * 2 + f // 2)
            fm(nth(TM_BLOCKS + MID_BLOCKS - 1), 0, MID_BLOCKS - 1)
            for t in (NT - 2, NT - 1):
                rope(t, t % 2, t // 2)

        def skip(*_):
            pass

        def ends_block(t, use):
            return t == 1 or (isinstance(use, int) and use == MID_BLOCKS - 1)

        def tile_of(t):
            return slice(t, t + 1) if isinstance(t, int) else ds(t, 1)

        def tokens(t):
            return slice(t * P, (t + 1) * P) if isinstance(t, int) else ds(t * P, P)

        @block.sync
        def _(sp):
            for h in range(HEADS):
                sp.dma_start(gain[:, h, :], io["q_norm"].partition_broadcast(P)).then_inc(s_const, 16)
            for h in range(KV_HEADS):
                sp.dma_start(gain[:, HEADS + h, :], io["k_norm"].partition_broadcast(P)).then_inc(s_const, 16)

            def rope(t, b, use):
                sp.wait_ge(out_done[b], use)
                for k in range(3):
                    w = WB if k < 2 else W - 2 * WB
                    sp.dma_start(x[:, b, k * WB:k * WB + w], core.tm[k, tile_of(t), :, 0:w].rearrange("o p c -> (o p) c")
                                 ).then_inc(x_in[b], 16)
                sp.dma_start(v[:, tile_of(t), :], core.tm[2, tile_of(t), :, W - 2 * WB:WB].rearrange("o p c -> p o c")).then_inc(v_in, 16)
                sp.dma_start(tab[:, b, :, :], io["rope"][tile_of(t), :, :, :].rearrange("o p a c -> (o p) a c")).then_inc(x_in[b], 16)

            walk(lambda blk: ring.load(sp, blk), skip, rope, sp.Fori)
            sp.wait_ge(v_in, 16 * NT)

        @block.gpsimd
        def _(pool):
            def fm(blk, t, use):
                pool.wait_ge(fm_read[t], use + 1)
                hold(pool)
                tile = use * 2 + t
                pool.dma_start(core.fm[tile_of(tile), :, :].rearrange("o p c -> (o p) c"), fm_out[:, t, :]).then_inc(fm_stored[t], 16)

            walk(lambda blk: ring.low(pool, blk), fm, skip, pool.Fori)
            pool.wait_ge(fm_stored[0], 16 * MID_BLOCKS)
            pool.wait_ge(fm_stored[1], 16 * (MID_BLOCKS - 1))

        @block.scalar
        def _(act):
            def fm(blk, t, use):
                _, b, w_use = blk
                if ends_block(t, use):
                    act.wait_ge(ring.used[b], w_use + 1)
                else:
                    act.wait_ge(fm_done, use + 1)
                act.wait_ge(fm_stored[t], use * 16)
                act.activation(fm_out[:, t, 0:1024], fm_bank[t][:, 0:2, :], ACT.Copy)
                act.activation(fm_out[:, t, 1024:T], fm_bank[t][:, 2, 0:256], ACT.Copy).then_inc(fm_read[t], 1)

            def root(b, use):
                act.wait_ge(ms_done[b], use + 1)
                act.activation(st[:, b, 2, :], st[:, b, 1, :], ACT.Sqrt).then_inc(rt_done[b], 1)

            def fm_and_root(blk, t, use):
                root(t, use)
                fm(blk, t, use)

            def rope(t, b, use):
                if isinstance(t, int) and t == NT - 1:
                    root(b, use)
                tok = tokens(t)
                act.wait_ge(tr_done, t + 1)
                act.activation(qt[:, 0:3, tok], pt[:, 0, :].rearrange("p (a n) -> p a n", n=P), ACT.Copy)
                act.activation(qt[:, 3:4, tok], pt[:, 1, 0:P].rearrange("p (a n) -> p a n", n=P), ACT.Copy)
                act.activation(kt[:, :, tok], pt[:, 1, P:3 * P].rearrange("p (a n) -> p a n", n=P), ACT.Copy).then_inc(tr_read, 1)

            walk(lambda blk: ring.high(act, blk), fm_and_root, rope, act.Fori)

        @block.vector
        def _(dve):
            dve.wait_ge(s_const, 16 * H)
            heads = lambda a: a.rearrange("p (h d) -> p h d", d=HD)

            def rope(t, b, use):
                c = chain[b]
                c.turn(use)
                s = lambda k: st[:, b, k, :]
                xb, ub = x[:, b, :], u[:, b, :]
                dve.wait_ge(x_in[b], use * 64 + 64)
                c.link(dve, dve.tensor_tensor(sq[:, b, :], xb, xb, ALU.mult))
                c.link(dve, dve.tensor_reduce(s(0), heads(sq[:, b, :]), AX.X, ALU.add))
                dve.tensor_scalar(s(1), s(0), 1.0 / HD, EPS, ALU.mult, ALU.add).then_inc(ms_done[b], 1)
                dve.wait_ge(rt_done[b], use + 1)
                c.link(dve, dve.reciprocal(s(3), s(2)))
                newton(dve, c, s(3), s(1), s(2))
                c.link(dve, dve.tensor_tensor(heads(xb), heads(xb), s(3).unsqueeze(2).broadcast_to((P, H, HD)), ALU.mult))
                c.link(dve, dve.tensor_tensor(heads(xb), heads(xb), gain[:, :, :], ALU.mult))
                cos = tab[:, b, 0, :].unsqueeze(1).broadcast_to((P, H, HD))
                c.link(dve, dve.tensor_tensor(heads(sq[:, b, :]), heads(xb), cos, ALU.mult))
                tsin = lambda k: tab[:, b, 1, :].rearrange("p (a s n) -> p a s n", s=2, n=16)[:, :, k, :].unsqueeze(1)\
                    .broadcast_to((P, H, 2, 16))
                q4 = lambda a, k: a.rearrange("p (h a s n) -> p h a s n", a=2, s=2, n=16)[:, :, :, k, :]
                c.step(dve.tensor_tensor(q4(ub, 0), q4(xb, 1), tsin(0), ALU.mult))
                c.link(dve, dve.tensor_tensor(q4(ub, 1), q4(xb, 0), tsin(1), ALU.mult))
                dve.wait_ge(tr_read, use * 2)
                ob, sb_ = out[:, b, :], sq[:, b, :]
                nq = HEADS * HD
                dve.tensor_tensor(ob[:, 0:nq], sb_[:, 0:nq], ub[:, 0:nq], ALU.add)
                kk = lambda a: heads(a[:, nq:W]).unsqueeze(2).broadcast_to((P, KV_HEADS, 2, HD))
                dve.tensor_tensor(ob[:, nq:].rearrange("p (h r d) -> p h r d", h=KV_HEADS, r=2), kk(sb_), kk(ub),
                                  ALU.add).then_inc(out_done[b], 1)

            walk(skip, skip, rope, dve.Fori)

        @block.tensor
        def _(pe):
            def fm(blk, t, use):
                _, b, _ = blk
                if t == 0:
                    ring.ready(pe, blk)
                pe.wait_ge(fm_read[t], use)
                for k in range(KT):
                    wh, wl = (a[:, k, t * P:(t + 1) * P] for a in (ring.hi[b], ring.lo[b]))
                    for w, a in ((wh, ah), (wh, al), (wl, ah)):
                        for n, (at, width) in enumerate(CHUNKS_512):
                            last = pe.matmul(fm_bank[t][:, n, 0:width], w, a[:, k, at:at + width],
                                             start=(k == 0 and w is wh and a is ah), stop=(k == KT - 1 and w is wl))
                last.then_inc(ring.used[b] if ends_block(t, use) else fm_done, 1)

            def rope(t, b, use):
                pe.wait_ge(out_done[b], use + 1)
                pe.wait_ge(tr_read, t)
                for n in range(6):
                    last = pe.transpose(pt[:, n // 3, (n % 3) * P:(n % 3 + 1) * P], out[:, b, n * P:(n + 1) * P], core.ident[:, :])
                last.then_inc(tr_done, 1)

            walk(skip, fm, rope, pe.Fori)


def stage_attention(core, ah, al, ring, qt, kt, v):
    nc = core.nc
    ROUNDS = KV_HEADS
    with core.stage_memory() as mem:
        sb = lambda name, shape, dt=F32: mem.enter_context(nc.sbuf_tensor(name, shape, dt))
        fm_out = sb("a_fm_out", [P, 2, T])
        qs = sb("a_qs", [P, 2, T])
        ks = sb("a_ks", [P, T])
        vs = sb("a_vs", [P, NT, HD])
        p = sb("a_p", [P, 2, N_SAMPLE])
        ptr = sb("a_ptr", [P, 2, NT_S, P])
        o = sb("a_o", [P, 2, 2, HD])
        at = sb("a_at", [P, T])
        st = sb("a_stat", [P, 2, 4])
        units = [(hp, t, h) for hp in range(2) for t in range(NT) for h in range(2)]
        U = len(units)
        keys = lambda t: (0, NT_S) if t < NT_S else (NT_S, NT)
        JB, CH = GATE_BLOCKS // ROUNDS, len(CHUNKS_512)
        groups = [(j, t, c) for j in range(JB) for t in range(2) for c in range(CH)]
        G = len(groups)
        long_units = [n for n, (_, t, _) in enumerate(units) if t < NT_S]
        LEAD = 2
        group_at = {long_units[LEAD + g * (len(long_units) - LEAD) // G]: g for g in range(G)}
        assert len(group_at) == G and JB % 2 == 0
        unit_of = {g: n for n, g in group_at.items()}
        split_at = {0: 0, **{unit_of[2 * CH * (j - 1) + CH]: j for j in range(1, JB)}}
        GATES = TM_BLOCKS + MID_BLOCKS
        block_of = lambda i, j: nth(GATES + j, i, JB)
        staged = core.sem("a_staged")
        s_done = core.sems("a_s_done", 2)
        max_done = core.sems("a_max_done", 2)
        bias_done = core.sems("a_bias_done", 2)
        exp_done = core.sems("a_exp_done", 2)
        t_done = core.sem("a_t_done")
        ta_read = core.sem("a_ta_read")
        tb_read = core.sem("a_tb_read")
        pv_done = core.sems("a_pv_done", 2)
        rc_done = core.sems("a_rc_done", 2)
        o_done = core.sems("a_o_done", 2)
        ot_done = core.sem("a_ot_done")
        ot_read = core.sem("a_ot_read")
        at_stored = core.sem("a_at_stored")
        g_done = core.sem("a_g_done")
        g_read = core.sem("a_g_read")
        fm_stored = core.kept_sems("a_fm_stored", 2)
        ps_s = [core.ps[:, 2 * b:2 * b + 2, :] for b in range(2)]
        ps_t = core.ps[:, 4:6, :]
        ps_o = [core.ps[:, 6, b * HD:(b + 1) * HD] for b in range(2)]
        ps_ot = core.ps[:, 7, 0:P]
        ps_g = core.ps[:, 7, :]
        SCALE = HD ** -0.5
        HU, TU = U // 2, U // 2
        block = mem.enter_context(nc.Block())

        @block.sync
        def _(sp):
            with sp.Fori(0, ROUNDS) as i:
                for j in range(JB):
                    ring.load(sp, block_of(i, j))
                for hp in range(2):
                    sp.wait_ge(ot_read, i * TU + (hp + 1) * NT)
                    sp.dma_start(core.up_in[ds(i * 2 + hp, 1), :, :].rearrange("o p t -> (o p) t"), at[:, :]).then_inc(at_stored, 16)
            sp.wait_ge(at_stored, 16 * 2 * ROUNDS)

        @block.gpsimd
        def _(pool):
            core.clear_old(pool)
            with pool.Fori(0, ROUNDS) as i:
                for u in range(U):
                    if u in split_at:
                        ring.low(pool, block_of(i, split_at[u]))
                    if u in group_at:
                        g = group_at[u]
                        j, t, c = groups[g]
                        if c == CH - 1:
                            pool.wait_ge(g_read, i * G + g + 1)
                            hold(pool)
                            pool.dma_start(core.fm[ds(i * (2 * JB) + T_GA + 2 * j + t, 1), :, :].rearrange("o p c -> (o p) c"),
                                           fm_out[:, t, :]).then_inc(fm_stored[t], 16)
            for t in range(2):
                pool.wait_ge(fm_stored[t], 16 * GATE_BLOCKS)

        def scores(b, t):
            a, z = keys(t)
            n = (z - a) * P
            return ps_s[b].rearrange("p a c -> p (a c)")[:, 0:n], n

        @block.tensor
        def _(pe):
            def qk(i, u):
                hp, t, h = units[u]
                b, use = u % 2, i * HU + u // 2
                pe.wait_ge(exp_done[b], use)
                rows = slice(h * HD, h * HD + HD)
                a, z = keys(t)
                for n in range(a * P, z * P, 512):
                    w = min(512, z * P - n)
                    last = pe.matmul(ps_s[b][:, (n - a * P) // 512, 0:w], qs[rows, hp, t * P:(t + 1) * P],
                                     ks[rows, n:n + w], start=True, stop=True)
                last.then_inc(s_done[b], 1)

            def turn(i, u):
                hp, t, h = units[u]
                b, use = u % 2, i * HU + u // 2
                pe.wait_ge(exp_done[b], use + 1)
                pe.wait_ge(ta_read, i * U + u)
                pe.wait_ge(tb_read, i * U + u)
                a, z = keys(t)
                for n in range(z - a):
                    last = pe.transpose(ps_t[:, n // 4, (n % 4) * P:(n % 4 + 1) * P], p[:, b, n * P:(n + 1) * P],
                                        core.ident[:, :])
                last.then_inc(t_done, 1)

            def pv(i, u):
                hp, t, h = units[u]
                b, use = u % 2, i * HU + u // 2
                pe.wait_ge(ta_read, i * U + u + 1)
                pe.wait_ge(tb_read, i * U + u + 1)
                pe.wait_ge(o_done[1 - b], i * HU + (u + 1) // 2)
                a, z = keys(t)
                for n in range(z - a):
                    last = pe.matmul(ps_o[b], ptr[:, b, n, :], vs[:, a + n, :], start=(n == 0), stop=(n == z - a - 1))
                last.then_inc(pv_done[b], 1)

            def turn_out(i, u):
                pe.wait_ge(o_done[1], i * HU + u // 2 + 1)
                pe.wait_ge(g_read, i * G + sum(n < u + 2 for n in group_at))
                pe.wait_ge(ot_read, i * TU + u // 2)
                pe.transpose(ps_ot, o[:, (u // 2) % 2, :, :].rearrange("p h d -> p (h d)"), core.ident[:, :]).then_inc(ot_done, 1)

            def group(i, u):
                g = group_at[u]
                j, t, c = groups[g]
                blk = block_of(i, j)
                b = blk[1]
                if (t, c) == (0, 0):
                    ring.ready(pe, blk)
                pe.wait_ge(g_read, i * G + g)
                pe.wait_ge(ot_read, i * TU + (u - 1) // 2)
                first, width = CHUNKS_512[c]
                for k in range(KT):
                    x = [a[:, k, first:first + width] for a in (ah, al)]
                    w = [a[:, k, t * P:(t + 1) * P] for a in (ring.hi[b], ring.lo[b])]
                    last = split3(pe, ps_g[:, 0:width], w, x, k == 0, k == KT - 1)
                last.then_inc(ring.used[b] if (t, c) == (1, CH - 1) else g_done, 1)

            with pe.Fori(0, ROUNDS) as i:
                pe.wait_ge(staged, i * 3 + 3)
                qk(i, 0)
                for u in range(U):
                    if u >= 3 and u % 2:
                        turn_out(i, u - 2)
                    if u + 1 < U:
                        qk(i, u + 1)
                    if u:
                        pv(i, u - 1)
                    if u in group_at:
                        group(i, u)
                    turn(i, u)
                pv(i, U - 1)
                turn_out(i, U - 1)

        @block.vector
        def _(dve):
            def row_max(i, u):
                b, use = u % 2, i * HU + u // 2
                flat, n = scores(b, units[u][1])
                dve.wait_ge(s_done[b], use + 1)
                dve.tensor_reduce(st[:, b, 0:1], flat, AX.X, ALU.max, negate=True).then_inc(max_done[b], 1)
                dve.wait_ge(max_done[b], use + 1)
                dve.tensor_scalar(st[:, b, 1:2], st[:, b, 0:1], SCALE, None, ALU.mult).then_inc(bias_done[b], 1)

            def evict(i, u):
                b, use = u % 2, i * HU + u // 2
                n = min(4, keys(units[u][1])[1] - keys(units[u][1])[0])
                dve.wait_ge(t_done, i * U + u + 1)
                dve.wait_ge(pv_done[b], use)
                dve.tensor_copy(ptr[:, b, 0:n, :].rearrange("p a c -> p (a c)"), ps_t[:, 0, 0:n * P]).then_inc(ta_read, 1)

            def normalise(i, u):
                b, use = u % 2, i * HU + u // 2
                dve.reciprocal(st[:, b, 3:4], st[:, b, 2:3]).then_inc(rc_done[b], 1)
                dve.wait_ge(rc_done[b], use + 1)
                dve.wait_ge(pv_done[b], use + 1)
                tile = u // 2
                dve.wait_ge(ot_done, i * TU + max(tile - 1, 0))
                dve.tensor_scalar(o[:, tile % 2, b, :], ps_o[b], st[:, b, 3:4], None, ALU.mult).then_inc(o_done[b], 1)

            with dve.Fori(0, ROUNDS) as i:
                dve.tensor_copy(ks[:, :].unsqueeze(1), kt[:, ds(i, 1), :]).then_inc(staged, 1)
                dve.tensor_copy(vs[:, :, :], v[:, :, ds(i * HD, HD)]).then_inc(staged, 1)
                row_max(i, 0)
                for u in range(U):
                    if u + 1 < U:
                        row_max(i, u + 1)
                    if u:
                        normalise(i, u - 1)
                    evict(i, u)
                normalise(i, U - 1)

        @block.scalar
        def _(act):
            def exp(i, u):
                b, use = u % 2, i * HU + u // 2
                flat, n = scores(b, units[u][1])
                act.wait_ge(bias_done[b], use + 1)
                act.wait_ge(o_done[b], use)
                act.activation(p[:, b, 0:n], flat, ACT.Exp, bias=st[:, b, 1:2], scale=SCALE,
                               accum_out=st[:, b, 2:3]).then_inc(exp_done[b], 1)

            def evict(i, u):
                b, use = u % 2, i * HU + u // 2
                t = units[u][1]
                act.wait_ge(t_done, i * U + u + 1)
                if t < NT_S:
                    act.wait_ge(pv_done[b], use)
                    act.activation(ptr[:, b, 4:8, :].rearrange("p a c -> p (a c)"), ps_t[:, 1, :], ACT.Copy).then_inc(tb_read, 1)
                else:
                    act.sem_inc(tb_read, 1)

            def evict_out(i, u):
                hp, t, _h = units[u]
                act.wait_ge(ot_done, i * TU + u // 2 + 1)
                if t == 0:
                    act.wait_ge(at_stored, (i * 2 + hp) * 16)
                act.activation(at[:, t * P:(t + 1) * P], ps_ot, ACT.Copy).then_inc(ot_read, 1)

            def group(i, u):
                g = group_at[u]
                j, t, c = groups[g]
                _, b, w_use = block_of(i, j)
                if (t, c) == (1, CH - 1):
                    act.wait_ge(ring.used[b], w_use + 1)
                else:
                    act.wait_ge(g_done, i * (G - JB) + g - j + 1)
                if c == 0:
                    act.wait_ge(fm_stored[t], (i * JB + j) * 16)
                first, width = CHUNKS_512[c]
                act.activation(fm_out[:, t, first:first + width], ps_g[:, 0:width], ACT.Copy).then_inc(g_read, 1)

            with act.Fori(0, ROUNDS) as i:
                act.activation(qs[:, :, :], qt[:, ds(i * 2, 2), :], ACT.Copy).then_inc(staged, 1)
                exp(i, 0)
                for u in range(U):
                    if u >= 3 and u % 2:
                        evict_out(i, u - 2)
                    if u in split_at:
                        ring.high(act, block_of(i, split_at[u]))
                    if u + 1 < U:
                        exp(i, u + 1)
                    if u in group_at:
                        group(i, u)
                    evict(i, u)
                evict_out(i, U - 1)


def stage_gla(core, split_up):
    nc, io = core.nc, core.io
    HP, NCH = GLA_HP, T // CHUNK
    SEAM = N_SAMPLE // CHUNK
    FLAT = HP * T
    with core.stage_memory() as mem:
        sb = lambda name, shape, dt=F32: mem.enter_context(nc.sbuf_tensor(name, shape, dt))
        q = sb("g_q", [P, HP, T])
        k = sb("g_k", [P, HP, T])
        bcum = sb("g_b", [P, 2, HP, T])
        v = sb("g_v", [P, PAIRS, GLA_H * DV])
        att = sb("g_att", [P, PAIRS, GLA_H, P])
        turns = [sb(f"g_turn{b}", [P, 2, HP, T]) for b in range(2)]
        ql, kl = ([turns[b][:, n, :, :] for b in range(2)] for n in range(2))
        both = sb("g_diff", [P, 2, HP, T])
        diff = [both[:, d, :, :] for d in range(2)]
        state = [sb(f"g_state{d}", [P, NCH, HP, DV]) for d in range(2)]
        decay = sb("g_decay", [P, 2, HP, NCH])
        mask = sb("g_mask", [P, len(LEVELS) + 1, P], I32)
        ones = sb("g_ones", [P, P])
        gain = sb("g_gain", [P, 1])
        bias = sb("g_bias", [P, 2, HP])
        w_lora = sb("g_w_lora", [2 * LORA, 2, HP, P])
        stat = sb("g_stat", [P, 4, PAIRS * GLA_H])
        lora = state[0][0:2 * LORA].rearrange("p c h d -> p (c h d)")[:, 0:T]
        reset = state[1][:, :, :, :].rearrange("p c h d -> p (c h d)")[:, 0:FLAT + 1]
        z = [ql[0], kl[0]]
        lg = [ql[1], kl[1]]
        kt = [diff[d].rearrange("p h t -> p (h t)").rearrange("p (a h c) -> p a h c", a=PAIRS, h=HP) for d in range(2)]
        by_pair = lambda x: x[:, :, :, :].rearrange("p d h t -> p (d h t)").rearrange("p (a h c) -> p a h c", a=PAIRS, h=GLA_H)
        out, sq = by_pair(both), by_pair(turns[0])
        r = att[:, :, :, :].rearrange("p a h c -> p (a h c)").rearrange("p (h t) -> p h t", h=GLA_H)
        sr = v[:, :, :].rearrange("p a c -> p (a c)").rearrange("p (h t) -> p h t", h=GLA_H)
        diag = [state[1][:, 2 * b:2 * b + 2, :, :].rearrange("p c h d -> p (c h d)") for b in range(2)]
        flat = lambda a: a.rearrange("p h t -> p (h t)")
        blocks = lambda a, m: flat(a).rearrange("p (n w) -> p n w", w=2 * m)
        chunks = lambda a: flat(a).rearrange("p (n w) -> p n w", w=CHUNK)
        tok = [(0, 512), (512, 512), (1024, 256)]

        ps = core.ps
        TWOS = PAIRS // 2
        TWO = [(a, h) for a in range(2) for h in range(GLA_H)]
        slot = lambda bank, a, h: ps[:, bank, (2 * a + h // 2) * P:(2 * a + h // 2 + 1) * P]
        spread = lambda bank: ps[:, bank, :].rearrange("p (a h t) -> p a h t", a=2, h=2)

        names = ("in_lora in_qk in_v in_mask in_r lora_z z_read z_abs z_exp z_ln g_done scan_done reset_done lvl_df lvl_db "
                 "lvl_exp lvl_q lvl_k lvl_mm lvl_read att_zero q_scaled dk_f dk_b dk_exp dk_kf dk_kb kt_tr kt_read "
                 "dec_done q_f q_b q_exp ds_mm s_step out_mm out_read sq_done ss_mm ms_done rt_done bc_mm bc_read diag_done "
                 "r_sig r_silu final stored ones_done")
        S = {n: core.sem("g_s_" + n) for n in names.split()}
        chain = Chain(core.sem("g_chain"), 0)
        NL = len(LEVELS)
        ENDS = ((SEAM - 1, NCH - 1), (0, SEAM))
        FIRSTS = ((0, SEAM), (NCH - 1, SEAM - 1))
        steps = [[(d, c) for d, c in ((0, n), (1, NCH - 1 - n)) if c not in ENDS[d]] for n in range(NCH)]
        states_by = [HP * sum(map(len, steps[:n])) for n in range(NCH + 1)]
        block = mem.enter_context(nc.Block())

        @block.sync
        def _(sp):
            sp.dma_start(lora, core.fm[T_LORA, 0:2 * LORA, :]).then_inc(S["in_lora"], 16)
            sp.dma_start(w_lora[:, :, :, :], io["w_lora"]).then_inc(S["in_lora"], 16)
            sp.dma_start(bias[:, :, :], io["b_lora"]).then_inc(S["in_lora"], 16)
            sp.dma_start(gain[:, :], io["gla_norm"]).then_inc(S["in_lora"], 16)
            sp.dma_start(q[:, :, :], core.fm[T_LQ:T_LQ + 2].rearrange("h p t -> p h t")).then_inc(S["in_qk"], 16)
            sp.dma_start(k[:, :, :], core.fm[T_LK:T_LK + 2].rearrange("h p t -> p h t")).then_inc(S["in_qk"], 16)
            sp.dma_start(mask[:, :, :], io["level_masks"]).then_inc(S["in_mask"], 16)
            for n in range(2):
                sp.dma_start(v[:, :, n * WB:(n + 1) * WB], core.tm[3 + n].rearrange("t p c -> p t c")).then_inc(S["in_v"], 16)
            split_up.load(sp, 0)
            sp.wait_ge(S["out_mm"], TWOS)
            sp.dma_start(r, core.fm[T_LR:T_LR + GLA_H].rearrange("h p t -> p h t")).then_inc(S["in_r"], 16)
            parts = [(a, min(a + 3, PAIRS)) for a in range(0, PAIRS, 3)]
            for a, z in parts:
                sp.wait_ge(S["final"], z)
                for h in range(GLA_H):
                    sp.dma_start(core.up_in[KT // 2 + h, :, a * P:z * P].rearrange("p (a c) -> p a c", c=P), out[:, a:z, h, :]
                                 ).then_inc(S["stored"], 16)
            sp.wait_ge(S["stored"], 16 * GLA_H * len(parts))

        @block.tensor
        def _(pe):
            pe.wait_ge(S["in_lora"], 64)
            for u in range(2 * HP):
                d, h = divmod(u, HP)
                if u >= 2:
                    pe.wait_ge(S["z_read"], u - 1)
                for n, (at, w) in enumerate(tok):
                    last = pe.matmul(ps[:, 3 * (u % 2) + n, 0:w], w_lora[:, d, h, :], lora[:, at:at + w], start=True, stop=True)
                last.then_inc(S["lora_z"], 1)
            pe.wait_ge(S["z_read"], 2 * HP)
            for l in range(NL + 1):
                if l < NL:
                    pe.wait_ge(S["lvl_q"], l + 1)
                    pe.wait_ge(S["lvl_k"], l + 1)
                    qq, kk = ql[l % 2], kl[l % 2]
                else:
                    qq, kk = q, k
                for n in range(TWOS):
                    use = l * TWOS + n
                    if use >= 2:
                        pe.wait_ge(S["lvl_read"], 2 * (use - 1))
                    for a, h in TWO:
                        rows, t = slice((h % 2) * DK, (h % 2 + 1) * DK), slice((2 * n + a) * P, (2 * n + a + 1) * P)
                        last = pe.matmul(slot(2 * (use % 2) + h % 2, a, h), kk[rows, h // 2, t], qq[rows, h // 2, t],
                                         start=True, stop=True)
                    last.then_inc(S["lvl_mm"], 1)
            for d in range(2):
                pe.wait_ge(S["dk_kf" if d == 0 else "dk_kb"], 1)
                for n in range(PAIRS * HP // 4):
                    use = d * (PAIRS * HP // 4) + n
                    if use >= 4:
                        pe.wait_ge(S["kt_read"], use - 3)
                    for m in range(4):
                        a, h = divmod(n * 4 + m, HP)
                        last = pe.transpose(ps[:, 4 + use % 4, m * P:(m + 1) * P], (kl[0] if d == 0 else ql[0])[:, h, a * P:(a + 1) * P],
                                            core.ident[:, :])
                    last.then_inc(S["kt_tr"], 1)
            pe.wait_ge(S["kt_read"], 2 * (PAIRS * HP // 4))
            pe.wait_ge(S["lvl_read"], 2 * (NL + 1) * TWOS)
            pe.wait_ge(S["in_v"], 32)
            for n in range(NCH):
                if n >= 2:
                    pe.wait_ge(S["s_step"], states_by[n - 1])
                if not steps[n]:
                    continue
                for d, c in steps[n]:
                    rows = slice((c % 2) * CHUNK, (c % 2 + 1) * CHUNK)
                    for h in range(GLA_H):
                        o = (h % 2) * DK
                        last = pe.matmul(ps[o:o + DK, 2 * (n % 2) + d, (h // 2) * DV:(h // 2 + 1) * DV],
                                         kt[d][rows, c // 2, h // 2, o:o + DK], v[rows, c // 2, h * DV:(h + 1) * DV],
                                         start=True, stop=True, skip_group_check=True)
                last.then_inc(S["ds_mm"], 1)
            pe.wait_ge(S["s_step"], states_by[NCH])
            pe.wait_ge(S["q_f"], 1)
            pe.wait_ge(S["q_b"], 1)
            for n in range(TWOS):
                if n >= 2:
                    pe.wait_ge(S["out_read"], 2 * (n - 1))
                for pair, h in TWO:
                    a = 2 * n + pair
                    rows = slice((h % 2) * DK, (h % 2 + 1) * DK)
                    o = slot(4 + 2 * (n % 2) + h % 2, pair, h)
                    terms = []
                    for j in range(2):
                        c = 2 * a + j
                        cols, t = slice(j * CHUNK, (j + 1) * CHUNK), slice(c * CHUNK, (c + 1) * CHUNK)
                        if c not in (0, SEAM):
                            terms.append((o[:, cols], state[0][rows, c, h // 2, :], ql[1][rows, h // 2, t]))
                        if c not in (SEAM - 1, NCH - 1):
                            terms.append((o[:, cols], state[1][rows, c, h // 2, :], kl[1][rows, h // 2, t]))
                    pe.matmul(o, v[:, a, h * DV:(h + 1) * DV], att[:, a, h, :], start=True, stop=False, skip_group_check=True)
                    for m, (dst, lhs, rhs) in enumerate(terms):
                        last = pe.matmul(dst, lhs, rhs, start=False, stop=(m == len(terms) - 1), skip_group_check=True)
                last.then_inc(S["out_mm"], 1)
            pe.wait_ge(S["ones_done"], 1)
            for a in range(PAIRS):
                pe.wait_ge(S["sq_done"], a + 1)
                for h in range(GLA_H):
                    last = pe.matmul(ps[:, 0, a * GLA_H + h:a * GLA_H + h + 1], sq[:, a, h, :], ones[:, 0:1], start=True, stop=True)
            last.then_inc(S["ss_mm"], 1)
            for a in range(PAIRS):
                pe.wait_ge(S["diag_done"], a + 1)
                if a >= 2:
                    pe.wait_ge(S["bc_read"], a - 1)
                pe.matmul(ps[:, 2 + a % 2, :], ones[:, :], diag[a % 2], start=True, stop=True).then_inc(S["bc_mm"], 1)

        @block.scalar
        def _(act):
            for step in range(2 * HP + 1):
                if step < 2 * HP:
                    d, h = divmod(step, HP)
                    act.wait_ge(S["z_read"], step + 1)
                    act.activation(lg[d][:, h, :], z[d][:, h, :], ACT.Abs).then_inc(S["z_abs"], 1)
                if step:
                    d, h = divmod(step - 1, HP)
                    act.wait_ge(S["z_abs"], step)
                    act.activation(lg[d][:, h, :], lg[d][:, h, :], ACT.Exp, scale=-1.0).then_inc(S["z_exp"], 1)
            for u in range(2 * HP):
                d, h = divmod(u, HP)
                act.wait_ge(S["z_exp"], u + 1)
                act.activation(lg[d][:, h, :], lg[d][:, h, :], ACT.Ln, bias=1.0).then_inc(S["z_ln"], 1)
            g = 1.0 / GATE_NORM
            for l, m in enumerate(LEVELS):
                b = l % 2
                if l >= 2:
                    act.wait_ge(S["lvl_mm"], (l - 1) * TWOS)
                else:
                    act.wait_ge(S["scan_done"], 2)
                act.wait_ge(S["lvl_df"], l + 1)
                df, db, qb, kb = (blocks(x, m) for x in (diff[0], diff[1], ql[b], kl[b]))
                act.activation(qb[:, :, m:2 * m], df[:, :, m:2 * m], ACT.Exp, scale=g)
                act.activation(kb[:, :, 0:m], df[:, :, 0:m], ACT.Exp, scale=-g)
                act.wait_ge(S["lvl_db"], l + 1)
                act.activation(qb[:, :, 0:m], db[:, :, 0:m], ACT.Exp, scale=g)
                act.activation(kb[:, :, m:2 * m], db[:, :, m:2 * m], ACT.Exp, scale=-g).then_inc(S["lvl_exp"], 1)
            act.wait_ge(S["dk_f"], 1)
            act.wait_ge(S["lvl_mm"], (NL - 1) * TWOS)
            act.activation(kl[0][:, :, :], diff[0][:, :, :], ACT.Exp, scale=-g)
            act.wait_ge(S["dk_b"], 1)
            act.activation(ql[0][:, :, :], diff[1][:, :, :], ACT.Exp, scale=-g).then_inc(S["dk_exp"], 1)
            act.activation(decay[:, 0, :, :], bcum[:, 0, :, CHUNK - 1::CHUNK], ACT.Exp, scale=g)
            act.activation(decay[:, 1, :, :], bcum[:, 1, :, 0::CHUNK], ACT.Exp, scale=g).then_inc(S["dec_done"], 1)
            act.wait_ge(S["lvl_mm"], NL * TWOS)
            act.activation(ql[1][:, :, :], bcum[:, 0, :, :], ACT.Exp, scale=g)
            act.activation(kl[1][:, :, :], bcum[:, 1, :, :], ACT.Exp, scale=g).then_inc(S["q_exp"], 1)
            n_kt = PAIRS * HP // 4
            for use in range(2 * n_kt):
                d, n = divmod(use, n_kt)
                act.wait_ge(S["kt_tr"], use + 1)
                act.activation(kt[d].rearrange("p a h c -> p (a h c)")[:, n * 512:(n + 1) * 512], ps[:, 4 + use % 4, :],
                               ACT.Copy).then_inc(S["kt_read"], 1)
            for a in range(PAIRS):
                act.wait_ge(S["out_read"], 2 * (a // 2 + 1))
                act.activation(sq[:, a, :, :], out[:, a, :, :], ACT.Square).then_inc(S["sq_done"], 1)
            act.wait_ge(S["in_r"], 16)
            act.activation(sr, r, ACT.Sigmoid).then_inc(S["r_sig"], 1)
            act.wait_ge(S["ms_done"], 1)
            act.activation(stat[:, 2, :], stat[:, 1, :], ACT.Sqrt).then_inc(S["rt_done"], 1)

        @block.vector
        def _(dve):
            link = lambda ins: chain.link(dve, ins)
            dve.memset(ones[:, :], 1.0).then_inc(S["ones_done"], 1)
            dve.memset(att[:, :, :, :].bitcast(U32), 0).then_inc(S["att_zero"], 1)
            link(dve.memset(reset, 1.0))
            link(dve.memset(reset[:, 0::CHUNK], 0.0))
            for u in range(2 * HP):
                d, h = divmod(u, HP)
                dve.wait_ge(S["in_lora"], 64)
                dve.wait_ge(S["lora_z"], u + 1)
                b = 3 * (u % 2)
                for to, src in ((slice(0, 1024), ps[:, b:b + 2, :].rearrange("p a c -> p (a c)")), (slice(1024, T), ps[:, b + 2, 0:256])):
                    last = dve.tensor_scalar(z[d][:, h, to], src, bias[:, d, h:h + 1], None, ALU.add)
                last.then_inc(S["z_read"], 1)
            dve.wait_ge(S["in_qk"], 32)
            dve.tensor_scalar(q[:, :, :], q[:, :, :], DK ** -0.5, None, ALU.mult).then_inc(S["q_scaled"], 1)
            fwd, bwd = (flat(bcum[:, d, :, :]) for d in range(2))
            for d in range(2):
                for h in range(HP):
                    dve.wait_ge(S["z_ln"], HP * d + h + 1)
                    link(dve.scalar_tensor_tensor(z[d][:, h, :], z[d][:, h, :], 0.0, lg[d][:, h, :], ALU.min, ALU.subtract))
                if d == 0:
                    dve.tensor_tensor_scan(fwd, reset[:, 0:FLAT], flat(z[0]), 0.0, ALU.mult, ALU.add).then_inc(S["scan_done"], 1)
                else:
                    dve.tensor_tensor_scan(bwd[:, ::-1], reset[:, 1:FLAT + 1][:, ::-1], flat(z[1])[:, ::-1], 0.0, ALU.mult,
                                           ALU.add).then_inc(S["scan_done"], 1)
            dve.wait_ge(S["scan_done"], 2)
            dve.wait_ge(S["in_mask"], 16)

            def gather(l, twos):
                for n in twos:
                    use = l * TWOS + n
                    dve.wait_ge(S["lvl_mm"], use + 1)
                    for par in range(2):
                        dve.copy_predicated(att[:, 2 * n:2 * n + 2, par::2, :],
                                            mask[:, l, :].unsqueeze(1).unsqueeze(1).broadcast_to((P, 2, 2, P)),
                                            spread(2 * (use % 2) + par)).then_inc(S["lvl_read"], 1)

            FIRST, LATE = list(range(TWOS - 2)), list(range(TWOS - 2, TWOS))
            bf, bb = bcum[:, 0, :, :], bcum[:, 1, :, :]
            for l, m in enumerate(LEVELS):
                if l:
                    dve.wait_ge(S["lvl_exp"], l)
                seam = blocks(bf, m)[:, :, m - 1:m].broadcast_to((P, FLAT // (2 * m), 2 * m))
                dve.tensor_tensor(blocks(diff[0], m), blocks(bf, m), seam, ALU.subtract).then_inc(S["lvl_df"], 1)
                if l:
                    gather(l - 1, FIRST)
                dve.wait_ge(S["lvl_exp"], l + 1)
                dve.wait_ge(S["q_scaled"], 1)
                dve.tensor_tensor(flat(ql[l % 2]), flat(ql[l % 2]), flat(q), ALU.mult).then_inc(S["lvl_q"], 1)
                if l:
                    gather(l - 1, LATE)
            last = chunks(bf)[:, :, CHUNK - 1:CHUNK].broadcast_to((P, HP * NCH, CHUNK))
            dve.tensor_tensor(chunks(diff[0]), chunks(bf), last, ALU.subtract).then_inc(S["dk_f"], 1)
            gather(NL - 1, FIRST + LATE)
            dve.wait_ge(S["dk_exp"], 1)
            dve.tensor_tensor(flat(kl[0]), flat(kl[0]), flat(k), ALU.mult).then_inc(S["dk_kf"], 1)
            gather(NL, FIRST + LATE)
            dve.wait_ge(S["q_exp"], 1)
            dve.tensor_tensor(flat(ql[1]), flat(ql[1]), flat(q), ALU.mult).then_inc(S["q_f"], 1)
            dve.wait_ge(S["dec_done"], 1)
            for n in range(NCH):
                dve.wait_ge(S["ds_mm"], sum(map(bool, steps[:n + 1])))
                if n:
                    dve.wait_ge(S["s_step"], states_by[n])
                for d, c in steps[n]:
                    to = c + 1 if d == 0 else c - 1
                    for h in range(HP):
                        add = ps[:, 2 * (n % 2) + d, h * DV:(h + 1) * DV]
                        if c in FIRSTS[d]:
                            dve.tensor_copy(state[d][:, to, h, :], add).then_inc(S["s_step"], 1)
                        else:
                            dve.scalar_tensor_tensor(state[d][:, to, h, :], state[d][:, c, h, :], decay[:, d, h, c:c + 1], add,
                                                     ALU.mult, ALU.add).then_inc(S["s_step"], 1)
            for n in range(TWOS):
                dve.wait_ge(S["out_mm"], n + 1)
                for par in range(2):
                    dve.tensor_copy(out[:, 2 * n:2 * n + 2, par::2, :], spread(4 + 2 * (n % 2) + par)).then_inc(S["out_read"], 1)
            dve.wait_ge(S["ss_mm"], 1)
            s = lambda n: stat[:, n, :]
            dve.tensor_scalar(s(1), ps[:, 0, 0:PAIRS * GLA_H], 1.0 / DV, EPS, ALU.mult, ALU.add).then_inc(S["ms_done"], 1)
            dve.wait_ge(S["rt_done"], 1)
            link(dve.reciprocal(s(3), s(2)))
            newton(dve, chain, s(3), s(1), s(2))

            def final(a):
                o = out[:, a, :, :].rearrange("p h t -> p (h t)")
                dve.wait_ge(S["bc_mm"], a + 1)
                dve.scalar_tensor_tensor(o, o, gain[:, 0:1], ps[:, 2 + a % 2, :], ALU.mult, ALU.mult).then_inc(S["bc_read"], 1)
                dve.wait_ge(S["bc_read"], a + 1)
                dve.wait_ge(S["r_silu"], 1)
                dve.tensor_tensor(out[:, a, :, :], out[:, a, :, :], sr[:, :, a * P:(a + 1) * P], ALU.mult).then_inc(S["final"], 1)

            for a in range(PAIRS):
                if a >= 2:
                    dve.wait_ge(S["bc_mm"], a - 1)
                dve.tensor_tensor(diag[a % 2].rearrange("p (h t) -> p h t", h=GLA_H),
                                  core.ident[:, :].unsqueeze(1).broadcast_to((P, GLA_H, P)),
                                  stat[:, 3, a * GLA_H:(a + 1) * GLA_H].unsqueeze(2).broadcast_to((P, GLA_H, P)),
                                  ALU.mult).then_inc(S["diag_done"], 1)
                if a:
                    final(a - 1)
            final(PAIRS - 1)

        @block.gpsimd
        def _(pool):
            core.clear_old(pool)
            bb = bcum[:, 1, :, :]
            pool.wait_ge(S["in_qk"], 32)
            pool.wait_ge(S["scan_done"], 2)
            for l, m in enumerate(LEVELS):
                if l:
                    pool.wait_ge(S["lvl_exp"], l)
                seam = blocks(bb, m)[:, :, m:m + 1].broadcast_to((P, FLAT // (2 * m), 2 * m))
                pool.tensor_tensor(blocks(diff[1], m), blocks(bb, m), seam, ALU.subtract).then_inc(S["lvl_db"], 1)
                pool.wait_ge(S["lvl_exp"], l + 1)
                pool.tensor_tensor(flat(kl[l % 2]), flat(kl[l % 2]), flat(k), ALU.mult).then_inc(S["lvl_k"], 1)
            first = chunks(bb)[:, :, 0:1].broadcast_to((P, HP * NCH, CHUNK))
            pool.tensor_tensor(chunks(diff[1]), chunks(bb), first, ALU.subtract).then_inc(S["dk_b"], 1)
            pool.wait_ge(S["dk_exp"], 1)
            pool.tensor_tensor(flat(ql[0]), flat(ql[0]), flat(k), ALU.mult).then_inc(S["dk_kb"], 1)
            pool.wait_ge(S["q_exp"], 1)
            pool.wait_ge(S["q_scaled"], 1)
            pool.tensor_tensor(flat(kl[1]), flat(kl[1]), flat(q), ALU.mult).then_inc(S["q_b"], 1)
            pool.wait_ge(S["r_sig"], 1)
            pool.tensor_tensor(sr, sr, r, ALU.mult).then_inc(S["r_silu"], 1)


def stage_merge(core, top, w_up, split_up, early):
    nc, io = core.nc, core.io
    with core.stage_memory() as mem:
        sb = lambda name, shape, dt=F32: mem.enter_context(nc.sbuf_tensor(name, shape, dt))
        x = sb("m_x", [P, KT, CW])
        aff = top.aff
        places = [early[:, :, :]] + [sb(f"m_place{n}", [P, KT, WB])[:, :, :] for n in (1, 2)]
        split_up.pieces = [piece[:3] + (places[(0, 1, 2, 1)[n]],) for n, piece in enumerate(split_up.pieces)]
        w_up.place(core, mem, "w_up")
        w_out = HeldWeights(io["w_out"])
        w_out.place(core, mem, "w_out")
        OUT_PLACES = (2, 1, 2, 1)
        split_out = Splitter(core, "m_out", [(w_out, slice(0, KT), slice(c * WB, (c + 1) * WB), places[OUT_PLACES[c]])
                                             for c in range(D // WB)])
        place = lambda n: places[n].rearrange("p k c -> p (k c)")
        xh, xl = sb("m_xh", [P, KT, CW], F32R), sb("m_xl", [P, KT, CW], F32R)
        mh, ml = sb("m_mh", [P, KT, CW], F32R), sb("m_ml", [P, KT, CW], F32R)
        GS = 4
        gates = place(0).rearrange("p (s h c) -> p s h c", s=GS, h=2)
        xn, res = (place(n).rearrange("p (b d) -> p b d", b=2) for n in (1, 2))
        xt = sb("m_xt", [P, D])
        g = sb("m_gain", [P, D])
        w_r = sb("m_w_r", [P, KT, E])
        st = sb("m_stat", [P, 2, 8])
        lg = sb("m_lg", [P, 2, 2, E])
        one = lambda names: {n: core.sem("m_s_" + n) for n in names.split()}
        two = lambda names: {n: core.sems("m_s_" + n, 2) for n in names.split()}
        S = one("const first_x_in xh xl mlo gate")
        S["x_in"] = core.kept_sems("m_s_x_in", 1)[0]
        S2 = two("up prod sum mhi out x1 sq ms rt xn tr xt rt_mm nmax ex aff aff_tr aff_out")
        S2 |= {n: core.kept_sems("m_s_" + n, 2) for n in ("res_in", "x1_out", "xn_out")}
        g_in = core.sems("m_s_g_in", GS)
        chain = [Chain(core.sem(f"m_chain{b}"), 1 + NEWTON) for b in range(2)]
        chain2 = [Chain(core.sem(f"m_chain_r{b}"), 1) for b in range(2)]
        ps = core.ps
        LAST = CHUNKS - 1
        first_pass = lambda c: isinstance(c, int) and c == 0
        pieces_after = lambda c, ft: {1: [(split_up, 3)], 3: [(split_out, 0)], 5: [(split_out, 1)],
                                      7: [(split_out, 2), (split_out, 3)]}.get(ft, []) if first_pass(c) else []
        FT = KT
        block = mem.enter_context(nc.Block())

        @block.sync
        def _(sp):
            sp.dma_start(x[:, :, :], core.up_in[:, :, 0:CW].rearrange("k p t -> p k t")).then_inc(S["first_x_in"], 16)
            for n in (1, 2):
                split_up.load(sp, n)

            def load_gates(c, fts):
                for ft in fts:
                    sp.wait_ge(S["mlo"], c * FT + (ft - GS + 1 if ft >= GS else 0))
                    for h in range(2):
                        sp.dma_start(gates[:, ft % GS, h, :], core.fm[T_GA + h * FT + ft, :, ds(c * CW, CW)]).then_inc(g_in[ft % GS], 16)

            split_up.wait_piece(sp, 0)
            load_gates(0, range(0, 4))
            split_up.wait_piece(sp, 1)
            split_up.load(sp, 3)
            sp.dma_start(g[:, :], io["g_moe"].partition_broadcast(P)).then_inc(S["const"], 16)
            sp.dma_start(w_r[:, :, :], io["w_router"].rearrange("(k p) n -> p k n", p=P)).then_inc(S["const"], 16)
            split_up.wait_piece(sp, 2)
            split_out.load(sp, 0)
            load_gates(0, range(4, 6))
            split_up.wait_piece(sp, 3)
            split_out.load(sp, 1)
            load_gates(0, range(6, 7))
            split_out.wait_piece(sp, 0)
            split_out.load(sp, 2)
            load_gates(0, range(7, 8))
            split_out.wait_piece(sp, 1)
            split_out.load(sp, 3)
            with sp.Fori(1, CHUNKS) as c:
                load_gates(c, range(FT))

        @block.gpsimd
        def _(pool):
            def load_res(c):
                for b in range(2):
                    pool.wait_ge(S2["x1_out"][b], c * 16)
                    pool.wait_ge(S2["xn"][b], c)
                    hold(pool)
                    pool.dma_start(res[:, b, :], io["x"][ds(c * CW + b * P, P), :]).then_inc(S2["res_in"][b], 16)

            def store(c):
                for b in range(2):
                    rows = ds(c * CW + b * P, P)
                    pool.wait_ge(S2["x1"][b], c + 1)
                    hold(pool)
                    pool.dma_start(core.x_res[rows, :], res[:, b, :]).then_inc(S2["x1_out"][b], 16)
                    pool.wait_ge(S2["xn"][b], c + 1)
                    hold(pool)
                    pool.dma_start(core.xm[rows, :], xn[:, b, :]).then_inc(S2["xn_out"][b], 16)

            def load_x(c):
                pool.wait_ge(S["xl"], c)
                hold(pool)
                pool.dma_start(x[:, :, :], core.up_in[:, :, ds(c * CW, CW)].rearrange("k p t -> p k t")).then_inc(S["x_in"], 16)

            core.clear_old(pool)
            split_out.wait(pool)
            with pool.Fori(0, LAST) as c:
                load_x(c + 1)
                load_res(c)
                store(c)
            load_res(LAST)
            store(LAST)
            for b in range(2):
                pool.wait_ge(S2["x1_out"][b], 16 * CHUNKS)
                pool.wait_ge(S2["xn_out"][b], 16 * CHUNKS)

        def walk(split, up, tail, out, late, loop):
            split(0)
            up(0)
            split(1)
            out(0)
            with loop(1, LAST) as c:
                up(c)
                tail(c - 1)
                split(c + 1)
                out(c)
                late(c - 1)
            up(LAST, range(0, FT // 2))
            tail(LAST - 1)
            up(LAST, range(FT // 2, FT - 2))
            late(LAST - 1)
            up(LAST, range(FT - 2, FT))
            out(LAST)
            tail(LAST)
            late(LAST)

        @block.tensor
        def _(pe):
            def split(c):
                pass

            def up(c, fts=range(FT)):
                pe.wait_ge(S["xl"], c + 1)
                for ft in fts:
                    b, use = ft % 2, c * (FT // 2) + ft // 2
                    split_up.wait_piece(pe, ft * P // WB)
                    pe.wait_ge(S2["prod"][b], use)
                    cols = slice(ft * P, (ft + 1) * P)
                    for part in range(2):
                        for k in range(4):
                            kk = 4 * part + k
                            last = split3(pe, ps[:, b, part * CW:(part + 1) * CW], (w_up.hi[:, kk, cols], w_up.lo[:, kk, cols]),
                                          (xh[:, kk, :], xl[:, kk, :]), k == 0, k == 3)
                    last.then_inc(S2["up"][b], 1)

            def out(c):
                split_out.wait(pe)
                for b in range(2):
                    pe.wait_ge(S["mlo"], FT * (c + 1))
                    pe.wait_ge(S2["x1"][b], c)
                    pe.wait_ge(S2["xt"][b], c)
                    for n in range(2):
                        for k in range(KT):
                            rows, cols = slice(b * P, (b + 1) * P), slice(n * 512, (n + 1) * 512)
                            last = split3(pe, ps[:, 2 + 2 * b + n, :], (mh[:, k, rows], ml[:, k, rows]),
                                          (w_out.hi[:, k, cols], w_out.lo[:, k, cols]), k == 0, k == KT - 1)
                    last.then_inc(S2["out"][b], 1)

            def tail(c):
                pe.wait_ge(S["const"], 32)
                for b in range(2):
                    pe.wait_ge(S2["xn"][b], c + 1)
                    for k in range(KT):
                        last = pe.transpose(ps[:, 2 + 2 * b + k // 4, (k % 4) * P:(k % 4 + 1) * P], xn[:, b, k * P:(k + 1) * P],
                                            core.ident[:, :])
                    last.then_inc(S2["tr"][b], 1)
                for b in range(2):
                    pe.wait_ge(S2["xt"][b], c + 1)
                    pe.wait_ge(S2["aff_out"][b], c)
                    for k in range(KT):
                        last = pe.matmul(ps[:, 6 + b, 0:E], xt[:, k * P:(k + 1) * P], w_r[:, k, :], start=(k == 0), stop=(k == KT - 1))
                    last.then_inc(S2["rt_mm"][b], 1)

            def late(c):
                for b in range(2):
                    pe.wait_ge(S2["aff"][b], c + 1)
                    pe.transpose(ps[0:E, 6 + b, P:2 * P], lg[:, b, 1, :], core.ident[:, :]).then_inc(S2["aff_tr"][b], 1)

            walk(split, up, tail, out, late, pe.Fori)

        @block.scalar
        def _(act):
            def gate(c, ft):
                s = ft % GS
                act.wait_ge(g_in[s], 32 * (c * (FT // GS) + ft // GS + 1))
                act.activation(gates[:, s, :, :], gates[:, s, :, :], ACT.Sigmoid).then_inc(S["gate"], 1)

            def split(c):
                if isinstance(c, int) and c == 0:
                    split_up.high(act, 0)
                act.wait_ge(S["first_x_in"], 16)
                act.wait_ge(S["x_in"], c * 16)
                act.wait_ge(S2["up"][1], c * (FT // 2))
                act.activation(xh[:, :, :], x[:, :, :], ACT.Copy).then_inc(S["xh"], 1)
                if first_pass(c):
                    split_up.high(act, 1)
                    split_up.high(act, 2)

            def up(c, fts=range(FT)):
                if fts[0] == 0:
                    gate(c, 0)
                for ft in fts:
                    b, use = ft % 2, c * (FT // 2) + ft // 2
                    if ft + 1 < FT:
                        gate(c, ft + 1)
                    act.wait_ge(S2["sum"][b], use + 1)
                    if ft == 0:
                        act.wait_ge(S2["out"][1], c)
                    act.activation(mh[:, ft, :], gates[:, ft % GS, 0, :], ACT.Copy).then_inc(S2["mhi"][b], 1)
                    for splitter, n in pieces_after(c, ft):
                        splitter.high(act, n)

            def out(c):
                for b in range(2):
                    act.wait_ge(S2["x1"][b], c + 1)
                    act.wait_ge(S2["xn_out"][b], c * 16)
                    act.wait_ge(S2["tr"][b], c)
                    act.activation(xn[:, b, :], res[:, b, :], ACT.Square, accum_out=st[:, b, 0:1]).then_inc(S2["sq"][b], 1)
                    act.wait_ge(S2["ms"][b], c + 1)
                    act.activation(st[:, b, 2:3], st[:, b, 1:2], ACT.Sqrt).then_inc(S2["rt"][b], 1)

            def tail(c):
                for b in range(2):
                    act.wait_ge(S2["tr"][b], c + 1)
                    act.wait_ge(S2["rt_mm"][1 - b], c + b)
                    act.activation(xt[:, :].rearrange("p (a n) -> p a n", a=2), ps[:, 2 + 2 * b:4 + 2 * b, :], ACT.Copy).then_inc(S2["xt"][b], 1)
                for b in range(2):
                    act.wait_ge(S2["nmax"][b], c + 1)
                    act.activation(lg[:, b, 0, :], ps[:, 6 + b, 0:E], ACT.Exp, bias=st[:, b, 4:5], accum_out=st[:, b, 5:6]).then_inc(S2["ex"][b], 1)

            def late(c):
                for b in range(2):
                    act.wait_ge(S2["aff_tr"][b], c + 1)
                    act.activation(aff[:, ds(c * CW + b * P, P)], ps[0:E, 6 + b, P:2 * P], ACT.Copy).then_inc(S2["aff_out"][b], 1)

            walk(split, up, tail, out, late, act.Fori)

        @block.vector
        def _(dve):
            def split(c):
                if isinstance(c, int) and c == 0:
                    split_up.low(dve, 0)
                dve.wait_ge(S["xh"], c + 1)
                dve.tensor_tensor(xl[:, :, :], x[:, :, :], xh[:, :, :].bitcast(F32), ALU.subtract).then_inc(S["xl"], 1)
                if first_pass(c):
                    split_up.low(dve, 1)
                    split_up.low(dve, 2)

            def up(c, fts=range(FT)):
                for ft in fts:
                    b, use = ft % 2, c * (FT // 2) + ft // 2
                    s = ft % GS
                    dve.wait_ge(S2["up"][b], use + 1)
                    dve.wait_ge(S["gate"], c * FT + ft + 1)
                    both = gates[:, s, :, :].rearrange("p a t -> p (a t)")
                    dve.tensor_tensor(both, ps[:, b, :], both, ALU.mult).then_inc(S2["prod"][b], 1)
                    dve.wait_ge(S2["prod"][b], use + 1)
                    dve.tensor_tensor(gates[:, s, 0, :], gates[:, s, 0, :], gates[:, s, 1, :], ALU.add).then_inc(S2["sum"][b], 1)
                    if ft > fts[0]:
                        low(c, ft - 1)
                    for splitter, n in pieces_after(c, ft):
                        splitter.low(dve, n)
                low(c, fts[-1])
                if isinstance(c, int) and c == LAST and fts[-1] == FT - 1:
                    top.some(dve, 9)

            def low(c, ft):
                b, use = ft % 2, c * (FT // 2) + ft // 2
                dve.wait_ge(S2["mhi"][b], use + 1)
                dve.tensor_tensor(ml[:, ft, :], gates[:, ft % GS, 0, :], mh[:, ft, :].bitcast(F32), ALU.subtract).then_inc(S["mlo"], 1)

            def out(c):
                dve.wait_ge(S["const"], 32)
                for b in range(2):
                    s = lambda n: st[:, b, n:n + 1]
                    dve.wait_ge(S2["out"][b], c + 1)
                    dve.wait_ge(S2["res_in"][b], 16 * (c + 1))
                    dve.tensor_tensor(res[:, b, :].rearrange("p (a n) -> p a n", a=2), ps[:, 2 + 2 * b:4 + 2 * b, :],
                                      res[:, b, :].rearrange("p (a n) -> p a n", a=2), ALU.add).then_inc(S2["x1"][b], 1)
                for b in range(2):
                    s = lambda n: st[:, b, n:n + 1]
                    dve.wait_ge(S2["sq"][b], c + 1)
                    dve.tensor_scalar(s(1), s(0), 1.0 / D, EPS, ALU.mult, ALU.add).then_inc(S2["ms"][b], 1)
                    dve.wait_ge(S2["rt"][b], c + 1)
                    chain[b].turn(c)
                    chain[b].link(dve, dve.reciprocal(s(3), s(2)))
                    newton(dve, chain[b], s(3), s(1), s(2))
                    dve.wait_ge(S2["xn_out"][b], 16 * c)
                    dve.wait_ge(S2["tr"][b], c)
                    dve.scalar_tensor_tensor(xn[:, b, :], res[:, b, :], s(3), g[:, :], ALU.mult, ALU.mult).then_inc(S2["xn"][b], 1)

            def tail(c):
                for b in range(2):
                    dve.wait_ge(S2["rt_mm"][b], c + 1)
                    dve.tensor_reduce(st[:, b, 4:5], ps[:, 6 + b, 0:E], AX.X, ALU.max, negate=True).then_inc(S2["nmax"][b], 1)
                for b in range(2):
                    dve.wait_ge(S2["ex"][b], c + 1)
                    chain2[b].turn(c)
                    chain2[b].link(dve, dve.reciprocal(st[:, b, 6:7], st[:, b, 5:6]))
                    dve.wait_ge(S2["aff_tr"][b], c)
                    dve.tensor_scalar(lg[:, b, 1, :], lg[:, b, 0, :], st[:, b, 6:7], None, ALU.mult).then_inc(S2["aff"][b], 1)

            def late(c):
                if isinstance(c, int) and c == LAST - 1:
                    for b in range(2):
                        dve.wait_ge(S2["aff_out"][b], LAST)

            walk(split, up, tail, out, late, dve.Fori)


class TopK:

    def __init__(self, core, mem, aff):
        sb = lambda name, shape, dt=F32: mem.enter_context(core.nc.sbuf_tensor(name, shape, dt))
        self.core, self.aff = core, aff
        self.val = sb("t_val", [E, CAP])
        self.pos = sb("t_pos", [E, CAP], U32)
        self.chain = Chain(core.kept_sems("t_chain", 1)[0], 0)
        self.rounds = [(slice(0, N_SAMPLE), n) for n in range(0, CAP_S, 8)] + [(slice(N_SAMPLE, T), n) for n in range(CAP_S, CAP, 8)]
        self.at = 0
        self.tr_done, self.done = core.kept_sems("t_done", 2)

    def place_results(self, core, mem):
        sb = lambda name, shape, dt=F32: mem.enter_context(core.nc.sbuf_tensor(name, shape, dt))
        self.posf = sb("t_posf", [E, CAP])
        self.idx = (sb("idx_s", [CAP_S, E], U32), sb("idx_p", [CAP_P, E], U32))
        self.gate = (sb("gate_s", [CAP_S, E]), sb("gate_p", [CAP_P, E]))

    def some(self, dve, count):
        for tokens, n in self.rounds[self.at:self.at + count]:
            a, v8 = self.aff[:, tokens], self.val[:, n:n + 8]
            self.chain.link(dve, dve.max(v8, a))
            self.chain.step(dve.max_index(self.pos[:, n:n + 8], v8, a))
            self.chain.link(dve, dve.match_replace(a, v8, a, -1.0))
        self.at += count

    def rest(self, dve):
        link = lambda ins: self.chain.link(dve, ins)
        val, pos, posf, ps = self.val, self.pos, self.posf, self.core.ps
        self.some(dve, len(self.rounds) - self.at)
        link(dve.tensor_copy(posf[:, :], pos[:, :]))
        link(dve.tensor_scalar(posf[:, CAP_S:CAP], posf[:, CAP_S:CAP], float(N_SAMPLE), None, ALU.add))
        dve.wait_ge(self.tr_done, 1)
        dve.tensor_copy(self.idx[0][:, :], ps[:, 0, 0:E])
        dve.tensor_copy(self.idx[1][:, :], ps[0:CAP_P, 1, 0:E])
        dve.tensor_copy(self.gate[0][:, :], ps[:, 2, 0:E])
        dve.tensor_copy(self.gate[1][:, :], ps[0:CAP_P, 3, 0:E]).then_inc(self.done, 1)
        dve.wait_ge(self.done, 1)

    def tensor(self, pe):
        pe.wait_ge(self.chain.sem, 3 * (CAP // 8) + 2)
        i16, ps = self.core.ident[0:E, 0:E], self.core.ps
        pe.transpose(ps[:, 0, 0:E], self.posf[:, 0:CAP_S], i16)
        pe.transpose(ps[0:CAP_P, 1, 0:E], self.posf[:, CAP_S:CAP], i16)
        pe.transpose(ps[:, 2, 0:E], self.val[:, 0:CAP_S], i16)
        pe.transpose(ps[0:CAP_P, 3, 0:E], self.val[:, CAP_S:CAP], i16).then_inc(self.tr_done, 1)


def stage_experts(core, top, spare, w_ahead, w_mem):
    nc, io = core.nc, core.io
    FB = FF // WB
    FT, DT = FF // P, D // P
    HL, HALF_N = 2 * CAP, 256
    groups = ((0, CAP_S, 0), (1, CAP_P, CAP_S))
    w_ahead.place(core, w_mem, "w_ple_gate")
    with core.stage_memory() as mem:
        sb = lambda name, shape, dt=F32: mem.enter_context(nc.sbuf_tensor(name, shape, dt))
        top.place_results(core, mem)
        idx, gate = top.idx, top.gate
        RING, BLOCKS = 4, 3 * FB
        PASSES = BLOCKS // RING
        raw = [sb(f"e_raw{n}", [P, KT, WB]) for n in range(RING)]
        w_hi = [sb(f"e_w_hi{n}", [P, KT, WB], F32R) for n in range(RING)]
        w_lo = [sb(f"e_w_lo{n}", [P, KT, WB], F32R) for n in range(RING)]
        rows = [sb("e_rows_s", [CAP_S, D]), sb("e_rows_p", [CAP_P, D])]
        x = sb("e_x", [P, KT, HL], F32R)
        h = sb("e_h", [P, KT, HL], F32R)
        yt = sb("e_yt", [P, 2, CAP])
        y = [sb("e_y_s", [CAP_S, D]), sb("e_y_p", [CAP_P, D])]
        at_get = [sb("e_at_get_s", [CAP_S, 1], U32), sb("e_at_get_p", [CAP_P, 1], U32)]
        at_put = [sb("e_at_put_s", [CAP_S, 1], U32), sb("e_at_put_p", [CAP_P, 1], U32)]
        g_sum, sig, u_sum, hidden = (spare[:, n * 2 * CAP:(n + 1) * 2 * CAP].rearrange("p (b c) -> p b c", b=2) for n in range(4))
        loaded, high_done, low_done, used = (core.sems("e_w_" + n, RING) for n in "loaded high low used".split())
        names = "get_ready x_tr x_hi x_lo put_ready y_tr y_read g_done u_done dn_done"
        S = {n: core.sem("e_s_" + n) for n in names.split()}
        S["rows_in"], S["added"] = core.kept_sems("e_s_dma", 2)
        S2 = {n: core.sems("e_s_" + n, 2) for n in "g_copy u_copy dn_copy g_sum u_sum sig silu hid h_hi h_lo dn_read".split()}
        splitter = Splitter(core, "e_ahead", [(w_ahead, slice(0, KT), slice(n * WB, (n + 1) * WB), raw[n][:, :, :]) for n in range(RING)])
        ps = core.ps
        X_BANK, Y_BANK, QUARTER = 6, 7, D // 4
        x_groups = ((-1, range(0, 3)), (2, range(3, 6)), (4, range(6, 8)))
        XG = len(x_groups)
        x_group_after = {at: n for n, (at, _) in enumerate(x_groups)}
        PAIRS_W = BLOCKS // 2
        block_use = lambda e, j: (j % RING, e * PASSES + j // RING)
        block = mem.enter_context(nc.Block())

        def walk(split, turn, hidden_pair, down_pair, loop):
            def expert(e, more):
                for q in range(PAIRS_W):
                    nxt = (e, q + 1) if q + 1 < PAIRS_W else (e + 1, 0)
                    step = (lambda n: split(nxt[0], 2 * nxt[1] + n)) if q + 1 < PAIRS_W or more else (lambda n: None)
                    if q < FB:
                        hidden_pair(e, q, step)
                    else:
                        down_pair(e, q - FB, step, more)
            split(0, 0)
            split(0, 1)
            for n in range(XG):
                turn(0, n)
            with loop(0, E - 1) as e:
                expert(e, True)
            expert(E - 1, False)

        @block.sync
        def _(sp):
            for n in range(RING):
                splitter.load(sp, n)
            with sp.Fori(0, E) as e:
                for j in range(BLOCKS):
                    if j < RING:
                        splitter.wait_piece(sp, j)
                    slot, use = block_use(e, j)
                    w, n = (("w_gate_e", "w_up_e")[j % 2], j // 2) if j < 2 * FB else ("w_down_e", j - 2 * FB)
                    sp.wait_ge(low_done[slot], use)
                    sp.dma_start(raw[slot][:, :, :], io[w][ds(e, 1), :, n * WB:(n + 1) * WB].rearrange("o (k p) c -> (o p) k c", p=P)
                                 ).then_inc(loaded[slot], 16)

        def split_low(eng, e, j):
            slot, use = block_use(e, j)
            eng.wait_ge(high_done[slot], use + 1)
            eng.tensor_tensor(w_lo[slot][:, :, :], raw[slot][:, :, :], w_hi[slot][:, :, :].bitcast(F32),
                              ALU.subtract).then_inc(low_done[slot], 1)

        @block.gpsimd
        def _(pool):
            def gather(e):
                pool.wait_ge(S["x_tr"], e * XG)
                for g, size, _ in groups:
                    pool.tensor_copy(at_get[g][:, :], idx[g][:, ds(e, 1)]).then_inc(S["get_ready"], 1)
                pool.wait_ge(S["get_ready"], e * 2 + 2)
                for g, size, _ in groups:
                    hold(pool)
                    pool.indirect_dma_start(rows[g][:, :], None, core.xm, bass.IndirectOffsetOnAxis(ap=at_get[g][:, 0:1], axis=0)
                                            ).then_inc(S["rows_in"], 16)

            def add(e):
                pool.wait_ge(S["added"], e * 32)
                for g, size, _ in groups:
                    pool.tensor_copy(at_put[g][:, :], idx[g][:, ds(e, 1)]).then_inc(S["put_ready"], 1)
                pool.wait_ge(S["put_ready"], e * 2 + 2)
                pool.wait_ge(S["y_read"], e * 8 + 8)
                for g, size, _ in groups:
                    hold(pool)
                    pool.indirect_dma_start(core.x_res, bass.IndirectOffsetOnAxis(ap=at_put[g][:, 0:1], axis=0), y[g][:, :], None,
                                            compute_op=ALU.add).then_inc(S["added"], 16)

            core.clear_old(pool)
            for n in range(RING):
                splitter.low(pool, n)

            def lows(e, first, last):
                for j in range(first, last, 2):
                    split_low(pool, *((e, j) if j < BLOCKS else (e + 1, 0)))

            split_low(pool, 0, 0)
            pool.wait_ge(top.done, 1)
            gather(0)
            lows(0, 2, 6)
            gather(1)
            lows(0, 6, BLOCKS + 1)
            with pool.Fori(1, E - 1) as e:
                lows(e, 2, 4)
                add(e - 1)
                lows(e, 4, 6)
                gather(e + 1)
                lows(e, 6, BLOCKS + 1)
            lows(E - 1, 2, 4)
            add(E - 2)
            lows(E - 1, 4, BLOCKS)
            add(E - 1)
            pool.wait_ge(S["added"], 32 * E)

        @block.tensor
        def _(pe):
            top.tensor(pe)

            def product(bank, slot, cols, src, before=lambda k: None):
                for k in range(KT):
                    before(k)
                    high = (ps[:, bank, 0:HL], w_hi[slot][:, k, cols], src[:, k, :])
                    low = (ps[:, bank, 0:HALF_N], w_lo[slot][:, k, cols], src[:, k, 0:HALF_N])
                    for out, w, r in (high, low) if k == 0 else (low, high):
                        last = pe.matmul(out, w, r, start=(k == 0 and w is high[1]), stop=(k == KT - 1 and w is high[1]))
                return last

            def turn(e, n):
                pe.wait_ge(S["rows_in"], e * 32 + 32)
                pe.wait_ge(S["x_lo"], e * XG + n)
                ks = x_groups[n][1]
                for k in ks:
                    for g, size, first in groups:
                        o = (k - ks[0]) * CAP + first
                        last = pe.transpose(ps[:, X_BANK, o:o + size], rows[g][:, k * P:(k + 1) * P], core.ident[0:size, 0:size])
                last.then_inc(S["x_tr"], 1)

            def hidden_pair(e, q, step):
                if q == 0:
                    pe.wait_ge(S["x_lo"], e * XG + XG)
                for half in range(2):
                    ft = 2 * q + half
                    for m, (done, read) in enumerate((("g_done", "g_sum"), ("u_done", "u_sum"))):
                        slot, use = block_use(e, 2 * q + m)
                        if half == 0:
                            pe.wait_ge(low_done[slot], use + 1)
                        pe.wait_ge(S2[read][half], e * (FT // 2) + q)
                        last = product(2 * m + half, slot, slice(half * P, (half + 1) * P), x)
                        last.then_inc(used[slot] if half else S[done], 1)

            def turn_back(e, dt):
                pe.wait_ge(S2["dn_read"][dt % 2], e * (DT // 2) + dt // 2 + 1)
                if dt % 2 == 0:
                    pe.wait_ge(S["y_read"], e * 8 + dt)
                o = (dt % 2) * P
                pe.transpose(ps[:, Y_BANK, o:o + P], yt[:, dt % 2, 0:CAP_S], core.ident[:, :])
                last = pe.transpose(ps[0:CAP_P, Y_BANK, QUARTER + o:QUARTER + o + P], yt[:, dt % 2, CAP_S:CAP], core.ident[:, :])
                if dt % 2:
                    last.then_inc(S["y_tr"], 1)

            def down_pair(e, q, step, more):
                if q == 0 and more:
                    turn(e + 1, 0)
                for dt in range(4 * q, 4 * q + 4):
                    half = dt % 2
                    slot, use = block_use(e, 2 * FB + dt // 2)
                    if half == 0:
                        pe.wait_ge(low_done[slot], use + 1)
                    pe.wait_ge(S2["dn_read"][half], e * (DT // 2) + dt // 2)

                    def before(k):
                        if dt == 0:
                            if k == 0:
                                for b in range(2):
                                    pe.wait_ge(S2["h_lo"][b], e * (FT // 2) + FT // 2 - 1)
                            if k >= KT - 2:
                                pe.wait_ge(S2["h_lo"][k % 2], e * (FT // 2) + FT // 2)

                    last = product(4 + half, slot, slice(half * P, (half + 1) * P), h, before)
                    last.then_inc(used[slot] if half else S["dn_done"], 1)
                    if more and dt in x_group_after:
                        turn(e + 1, x_group_after[dt])
                    if dt:
                        turn_back(e, dt - 1)
                if q == 1:
                    turn_back(e, DT - 1)

            pe.wait_ge(top.done, 1)
            walk(lambda e, j: None, turn, hidden_pair, down_pair, pe.Fori)

        def part_done(eng, e, j, half, even):
            slot, use = block_use(e, j)
            if half:
                eng.wait_ge(used[slot], use + 1)
            else:
                eng.wait_ge(S[even], e * FB + (j // 2 if j < 2 * FB else j - 2 * FB) + 1)

        @block.scalar
        def _(act):
            for n in range(RING):
                splitter.high(act, n)

            def split(e, j):
                slot, use = block_use(e, j)
                act.wait_ge(loaded[slot], use * 16 + 16)
                act.wait_ge(used[slot], use)
                act.activation(w_hi[slot][:, :, :], raw[slot][:, :, :], ACT.Copy).then_inc(high_done[slot], 1)

            def read_turned(e, n):
                ks = x_groups[n][1]
                act.wait_ge(S["x_tr"], e * XG + n + 1)
                act.activation(x[:, ks[0]:ks[0] + len(ks), 0:CAP], ps[:, X_BANK, 0:len(ks) * CAP].rearrange("p (k c) -> p k c", c=CAP),
                               ACT.Copy).then_inc(S["x_hi"], 1)

            def copy_half(out, bank):
                return act.activation(out, ps[:, bank, CAP:HL], ACT.Copy)

            def high_of(e, ft):
                act.wait_ge(S2["hid"][ft % 2], e * (FT // 2) + ft // 2 + 1)
                if ft == 0:
                    act.wait_ge(used[FB - 1], e * PASSES)
                act.activation(h[:, ft, 0:CAP], hidden[:, ft % 2, :], ACT.Copy).then_inc(S2["h_hi"][ft % 2], 1)

            def hidden_pair(e, q, step):
                for half in range(2):
                    ft = 2 * q + half
                    use = e * (FT // 2) + q
                    if half == 0:
                        step(0)
                    part_done(act, e, 2 * q, half, "g_done")
                    act.wait_ge(S2["hid"][half], use)
                    copy_half(g_sum[:, half, :], half).then_inc(S2["g_copy"][half], 1)
                    if ft:
                        high_of(e, ft - 1)
                    act.wait_ge(S2["g_sum"][half], use + 1)
                    act.activation(sig[:, half, :], g_sum[:, half, :], ACT.Sigmoid).then_inc(S2["sig"][half], 1)
                    if half == 0:
                        step(1)
                    part_done(act, e, 2 * q + 1, half, "u_done")
                    copy_half(u_sum[:, half, :], 2 + half).then_inc(S2["u_copy"][half], 1)
                if q == FB - 1:
                    high_of(e, FT - 1)

            def down_pair(e, q, step, more):
                if q == 0 and more:
                    read_turned(e + 1, 0)
                for dt in range(4 * q, 4 * q + 4):
                    if dt % 4 == 0:
                        step(0)
                    part_done(act, e, 2 * FB + dt // 2, dt % 2, "dn_done")
                    copy_half(yt[:, dt % 2, :], 4 + dt % 2).then_inc(S2["dn_copy"][dt % 2], 1)
                    if more and dt in x_group_after:
                        read_turned(e + 1, x_group_after[dt])
                    if dt % 4 == 0:
                        step(1)

            walk(split, read_turned, hidden_pair, down_pair, act.Fori)

        @block.vector
        def _(dve):
            top.rest(dve)
            splitter.wait(dve)

            def split(e, j):
                if j % 2:
                    split_low(dve, e, j)

            def read_turned(e, n):
                ks = x_groups[n][1]
                dve.wait_ge(S["x_hi"], e * XG + n + 1)
                to = slice(ks[0], ks[0] + len(ks))
                dve.tensor_tensor(x[:, to, CAP:HL], ps[:, X_BANK, 0:len(ks) * CAP].rearrange("p (k c) -> p k c", c=CAP),
                                  x[:, to, 0:CAP].bitcast(F32), ALU.subtract).then_inc(S["x_lo"], 1)

            def low_of(e, ft):
                dve.wait_ge(S2["h_hi"][ft % 2], e * (FT // 2) + ft // 2 + 1)
                dve.tensor_tensor(h[:, ft, CAP:HL], hidden[:, ft % 2, :], h[:, ft, 0:CAP].bitcast(F32), ALU.subtract
                                  ).then_inc(S2["h_lo"][ft % 2], 1)

            def add_halves(out, bank):
                return dve.tensor_tensor(out, ps[:, bank, 0:CAP], out, ALU.add)

            def hidden_pair(e, q, step):
                for b in range(2):
                    ft, use = 2 * q + b, e * (FT // 2) + q
                    dve.wait_ge(S2["g_copy"][b], use + 1)
                    add_halves(g_sum[:, b, :], b).then_inc(S2["g_sum"][b], 1)
                    if ft:
                        low_of(e, ft - 1)
                    dve.wait_ge(S2["sig"][b], use + 1)
                    dve.tensor_tensor(sig[:, b, :], g_sum[:, b, :], sig[:, b, :], ALU.mult).then_inc(S2["silu"][b], 1)
                    dve.wait_ge(S2["u_copy"][b], use + 1)
                    add_halves(u_sum[:, b, :], 2 + b).then_inc(S2["u_sum"][b], 1)
                    dve.wait_ge(S2["silu"][b], use + 1)
                    dve.wait_ge(S2["u_sum"][b], use + 1)
                    dve.wait_ge(S2["h_lo"][b], use)
                    dve.tensor_tensor(hidden[:, b, :], u_sum[:, b, :], sig[:, b, :], ALU.mult).then_inc(S2["hid"][b], 1)
                    if b == 0:
                        step(1)
                if q == FB - 1:
                    low_of(e, FT - 1)

            def scale_back(e, quarter):
                dve.wait_ge(S["y_tr"], e * 4 + quarter + 1)
                for g, size, _ in groups:
                    dve.tensor_scalar(y[g][:, quarter * QUARTER:(quarter + 1) * QUARTER],
                                      ps[0:size, Y_BANK, g * QUARTER:(g + 1) * QUARTER], gate[g][:, ds(e, 1) if not isinstance(e, int) else slice(e, e + 1)],
                                      None, ALU.mult).then_inc(S["y_read"], 1)

            def down_pair(e, q, step, more):
                if q == 0:
                    if more:
                        read_turned(e + 1, 0)
                    dve.wait_ge(S["added"], e * 32)
                for dt in range(4 * q, 4 * q + 4):
                    b = dt % 2
                    dve.wait_ge(S2["dn_copy"][b], e * (DT // 2) + dt // 2 + 1)
                    add_halves(yt[:, b, :], 4 + b).then_inc(S2["dn_read"][b], 1)
                    if dt >= 2 and dt % 2 == 0:
                        scale_back(e, dt // 2 - 1)
                    if more and dt in x_group_after:
                        read_turned(e + 1, x_group_after[dt])
                    if dt % 4 == 1:
                        step(1)
                if q == 1:
                    scale_back(e, 3)

            walk(split, read_turned, hidden_pair, down_pair, dve.Fori)


def stage_ple(core, w_gate):
    nc, io = core.nc, core.io
    w_proj = HeldWeights(io["w_ple_proj"])
    PT = PLE // P
    with ExitStack() as mem:
        sb = lambda name, shape, dt=F32: mem.enter_context(nc.sbuf_tensor(name, shape, dt))
        x = sb("l_x", [P, 2, D])
        xn = sb("l_xn", [P, 2, D])
        g1, g2 = sb("l_gain", [P, D]), sb("l_gain_final", [P, D])
        p = sb("l_p", [P, 2, PLE])
        AT = KT + PT
        th, tl = sb("l_th", [P, 2, AT, P], F32R), sb("l_tl", [P, 2, AT, P], F32R)
        sig = sb("l_sig", [P, 2, D])
        y = sb("l_y", [P, 2, D])
        st = sb("l_stat", [P, 2, 8])
        w_proj.place(core, mem, "w_ple_proj")
        split_proj = Splitter(core, "l_proj", [(w_proj, slice(0, PT), slice(0, D), y[:, :, :])])
        S = {n: core.sem("l_s_" + n) for n in ("gain_in", "final_gain_in")}
        S2 = {n: core.sems("l_s_" + n, 2) for n in "x_in sq ms rt xn tr hi lo gate proj sig mul res sq2 ms2 rt2 y out".split()}
        c1 = [Chain(core.sem(f"l_chain_a{b}"), 1 + NEWTON) for b in range(2)]
        c2 = [Chain(core.sem(f"l_chain_b{b}"), 1 + NEWTON) for b in range(2)]
        ps = core.ps
        tbanks = [range(0, 4), range(4, 8), range(8, AT)]
        H = NT // 2
        block = mem.enter_context(nc.Block())

        def walk(norm, turn, gate, proj, close, loop):
            norm(0, 0)
            turn(0, 0)
            norm(0, 1)
            with loop(0, H - 1) as i:
                for b in range(2):
                    gate(i, b)
                    turn(i + b, 1 - b)
                    proj(i, b)
                    close(i, b)
                    norm(i + 1, b)
            gate(H - 1, 0)
            turn(H - 1, 1)
            proj(H - 1, 0)
            close(H - 1, 0)
            gate(H - 1, 1)
            proj(H - 1, 1)
            close(H - 1, 1)

        def skip(i, b):
            pass

        @block.sync
        def _(sp):
            def load(i, b):
                rows = ds(i * 2 * P + b * P, P)
                sp.wait_ge(S2["res"][b], i)
                sp.wait_ge(S2["tr"][b], i)
                sp.dma_start(x[:, b, :], core.x_res[rows, :]).then_inc(S2["x_in"][b], 16)
                sp.dma_start(p[:, b, :], io["p"][rows, :]).then_inc(S2["x_in"][b], 16)

            def store(i, b):
                sp.wait_ge(S2["y"][b], i + 1)
                sp.dma_start(io["out"][ds(i * 2 * P + b * P, P), :], y[:, b, :]).then_inc(S2["out"][b], 16)

            load(0, 0)
            sp.dma_start(g1[:, :], io["g_ple"].partition_broadcast(P)).then_inc(S["gain_in"], 16)
            load(0, 1)
            split_proj.load(sp, 0)
            sp.dma_start(g2[:, :], io["g_final"].partition_broadcast(P)).then_inc(S["final_gain_in"], 16)
            with sp.Fori(0, H - 1) as i:
                for b in range(2):
                    load(i + 1, b)
                    store(i, b)
            for b in range(2):
                store(H - 1, b)
            for b in range(2):
                sp.wait_ge(S2["out"][b], 16 * H)

        @block.tensor
        def _(pe):
            def turn(i, b):
                pe.wait_ge(S2["xn"][b], i + 1)
                pe.wait_ge(S2["lo"][1 - b], i + b)
                for n, ks in enumerate(tbanks):
                    for k in ks:
                        src = xn[:, b, k * P:(k + 1) * P] if k < KT else p[:, b, (k - KT) * P:(k - KT + 1) * P]
                        last = pe.transpose(ps[:, n, (k - ks[0]) * P:(k - ks[0] + 1) * P], src, core.ident[:, :])
                last.then_inc(S2["tr"][b], 1)

            def product(b, first, w, bank):
                for half in range(2):
                    cols = slice(half * 512, (half + 1) * 512)
                    for k in range(w.kt):
                        last = split3(pe, ps[:, bank + half, :], (th[:, b, first + k, :], tl[:, b, first + k, :]),
                                      (w.hi[:, k, cols], w.lo[:, k, cols]), k == 0, k == w.kt - 1)
                return last

            def gate(i, b):
                pe.wait_ge(S2["lo"][b], i + 1)
                pe.wait_ge(S2["sig"][1 - b], i + b)
                product(b, 0, w_gate, 3).then_inc(S2["gate"][b], 1)

            def proj(i, b):
                split_proj.wait(pe)
                pe.wait_ge(S2["mul"][1 - b], i + b)
                product(b, KT, w_proj, 5).then_inc(S2["proj"][b], 1)

            walk(skip, turn, gate, proj, skip, pe.Fori)

        @block.scalar
        def _(act):
            def norm(i, b):
                act.wait_ge(S2["x_in"][b], i * 32 + 32)
                act.activation(sig[:, b, :], x[:, b, :], ACT.Square, accum_out=st[:, b, 0:1]).then_inc(S2["sq"][b], 1)
                act.wait_ge(S2["ms"][b], i + 1)
                act.activation(st[:, b, 2:3], st[:, b, 1:2], ACT.Sqrt).then_inc(S2["rt"][b], 1)

            def turn(i, b):
                act.wait_ge(S2["tr"][b], i + 1)
                act.wait_ge(S2["proj"][b], i)
                for n, ks in enumerate(tbanks):
                    ins = act.activation(th[:, b, ks[0]:ks[0] + len(ks), :],
                                         ps[:, n, 0:len(ks) * P].rearrange("p (k c) -> p k c", c=P), ACT.Copy)
                ins.then_inc(S2["hi"][b], 1)
                if isinstance(i, int) and (i, b) == (0, 0):
                    split_proj.high(act, 0)

            def gate(i, b):
                act.wait_ge(S2["gate"][b], i + 1)
                act.wait_ge(S2["rt"][b], i + 1)
                act.activation(sig[:, b, :].rearrange("p (a n) -> p a n", a=2), ps[:, 3:5, :], ACT.Sigmoid).then_inc(S2["sig"][b], 1)

            def close(i, b):
                act.wait_ge(S2["res"][b], i + 1)
                act.activation(sig[:, b, :], y[:, b, :], ACT.Square, accum_out=st[:, b, 4:5]).then_inc(S2["sq2"][b], 1)
                act.wait_ge(S2["ms2"][b], i + 1)
                act.activation(st[:, b, 6:7], st[:, b, 5:6], ACT.Sqrt).then_inc(S2["rt2"][b], 1)

            walk(norm, turn, gate, skip, close, act.Fori)

        @block.vector
        def _(dve):
            def rstd(i, b, chain, at, ms, rt, sq):
                s = lambda n: st[:, b, at + n:at + n + 1]
                dve.wait_ge(S2[sq][b], i + 1)
                dve.tensor_scalar(s(1), s(0), 1.0 / D, EPS, ALU.mult, ALU.add).then_inc(S2[ms][b], 1)
                dve.wait_ge(S2[rt][b], i + 1)
                chain[b].turn(i)
                chain[b].link(dve, dve.reciprocal(s(3), s(2)))
                newton(dve, chain[b], s(3), s(1), s(2))
                return s(3)

            def norm(i, b):
                rs = rstd(i, b, c1, 0, "ms", "rt", "sq")
                dve.wait_ge(S["gain_in"], 16)
                dve.wait_ge(S2["tr"][b], i)
                dve.scalar_tensor_tensor(xn[:, b, :], x[:, b, :], rs, g1[:, :], ALU.mult, ALU.mult).then_inc(S2["xn"][b], 1)

            def turn(i, b):
                dve.wait_ge(S2["hi"][b], i + 1)
                for n, ks in enumerate(tbanks):
                    t = slice(ks[0], ks[0] + len(ks))
                    ins = dve.tensor_tensor(tl[:, b, t, :], ps[:, n, 0:len(ks) * P].rearrange("p (k c) -> p k c", c=P),
                                            th[:, b, t, :].bitcast(F32), ALU.subtract)
                ins.then_inc(S2["lo"][b], 1)
                if isinstance(i, int) and (i, b) == (0, 0):
                    split_proj.low(dve, 0)

            def close(i, b):
                halves = lambda a: a[:, b, :].rearrange("p (a n) -> p a n", a=2)
                dve.wait_ge(S2["sig"][b], i + 1)
                dve.wait_ge(S2["proj"][b], i + 1)
                dve.wait_ge(S2["out"][b], i * 16)
                dve.tensor_tensor(halves(y), halves(sig), ps[:, 5:7, :], ALU.mult).then_inc(S2["mul"][b], 1)
                dve.wait_ge(S2["mul"][b], i + 1)
                dve.tensor_tensor(y[:, b, :], y[:, b, :], x[:, b, :], ALU.add).then_inc(S2["res"][b], 1)
                rs = rstd(i, b, c2, 4, "ms2", "rt2", "sq2")
                dve.wait_ge(S["final_gain_in"], 16)
                dve.scalar_tensor_tensor(y[:, b, :], y[:, b, :], rs, g2[:, :], ALU.mult, ALU.mult).then_inc(S2["y"][b], 1)

            walk(norm, turn, skip, skip, close, dve.Fori)


def program(nc, io):
    with ExitStack() as ctx:
        core = Core(nc, ctx, io)
        with ExitStack() as act_mem:
            ah = act_mem.enter_context(nc.sbuf_tensor("act_hi", [P, KT, T], F32R))
            al = act_mem.enter_context(nc.sbuf_tensor("act_lo", [P, KT, T], F32R))
            ring = WeightRing(core, act_mem)
            stage_norm_and_token_major(core, ah, al, ring)
            qt = act_mem.enter_context(nc.sbuf_tensor("q_t", [P, HEADS // 2, T], F32))
            kt = act_mem.enter_context(nc.sbuf_tensor("k_t", [P, KV_HEADS, T], F32))
            v = act_mem.enter_context(nc.sbuf_tensor("v_tok", [P, NT, KV_HEADS * HD], F32))
            stage_rope(core, ah, al, ring, qt, kt, v)
            stage_attention(core, ah, al, ring, qt, kt, v)
            core.release_old()
        with ExitStack() as tail_mem:
            aff_hidden = tail_mem.enter_context(nc.sbuf_tensor("aff_hidden", [P, T], F32))
            top = TopK(core, tail_mem, aff_hidden[0:E, :])
            with ExitStack() as early_mem:
                early = early_mem.enter_context(nc.sbuf_tensor("early", [P, KT, WB], F32))
                w_up = HeldWeights(io["w_up"])
                split_up = Splitter(core, "m_up", [(w_up, slice(0, KT), slice(c * WB, (c + 1) * WB), early[:, :, :])
                                                   for c in range(D // WB)])
                stage_gla(core, split_up)
                core.release_old()
                stage_merge(core, top, w_up, split_up, early)
                core.release_old()
            w_ple_gate = HeldWeights(io["w_ple_gate"])
            stage_experts(core, top, aff_hidden, w_ple_gate, tail_mem)
            core.release_old()
            stage_ple(core, w_ple_gate)


def host_inputs(**a):
    import numpy as np

    w = {k: np.asarray(v) for k, v in a.items()}
    out = {"ident": np.eye(P, dtype=np.float32)}
    out["x"] = np.concatenate([w["x_sample"][0], w["x_prompt"][0]])
    out["g_mix"] = w["g_mix"][0]
    for name in ("q_norm", "k_norm", "w_router", "w_gate_e", "w_up_e", "w_down_e", "w_out", "w_ple_gate", "w_ple_proj",
                 "g_moe", "g_ple"):
        out[name] = w[name][0]
    out["g_final"] = w["g_final"]
    out["w_up"] = np.concatenate([w["w_attn_up"][0], w["w_gla_up"][0]])
    out["p"] = np.concatenate([w["p_sample"][0, 0], w["p_prompt"][0, 0]])
    inv = (np.float32(10000.0) ** (-np.arange(0, 32, 2, dtype=np.float32) / np.float32(32))).astype(np.float32)
    pos = np.concatenate([np.arange(N_SAMPLE), np.arange(N_PROMPT)])
    row, col = ((n.astype(np.float32)[:, None] * inv).astype(np.float32) for n in (pos // 64, pos % 64))
    cos = np.concatenate([np.cos(a) for a in (row, row, col, col)], axis=1)
    sin = np.concatenate([-np.sin(row), np.sin(row), -np.sin(col), np.sin(col)], axis=1)
    out["rope"] = np.stack([cos, sin], axis=1).astype(np.float32).reshape(NT, P, 2, HD)
    lora_w = np.zeros((2 * LORA, 2, GLA_HP, P), np.float32)
    lora_w[:LORA, 0] = w["w_af"][0].reshape(LORA, GLA_HP, P)
    lora_w[LORA:, 1] = w["w_ab"][0].reshape(LORA, GLA_HP, P)
    out["w_lora"] = lora_w
    out["b_lora"] = np.ascontiguousarray(np.stack([w["b_af"][0], w["b_ab"][0]]).reshape(2, GLA_HP, P).transpose(2, 0, 1))
    out["gla_norm"] = w["gla_norm"][0].reshape(DV, 1)
    s_, t_ = np.arange(P)[:, None], np.arange(P)[None, :]
    masks = [(s_ // (2 * m) == t_ // (2 * m)) & (s_ // m != t_ // m) for m in LEVELS] + [s_ == t_]
    out["level_masks"] = np.ascontiguousarray(np.stack(masks, axis=1).astype(np.int32))
    w_in = w["w_in"][0]
    a0 = QKV_W
    qkv, lq_lk = w_in[:, :a0], w_in[:, a0:a0 + 2 * GLA_H * DK]
    a1 = a0 + 2 * GLA_H * DK
    lv, lr = w_in[:, a1:a1 + GLA_H * DV], w_in[:, a1 + GLA_H * DV:a1 + 2 * GLA_H * DV]
    a2 = a1 + 2 * GLA_H * DV
    lora, gates = w_in[:, a2:a2 + 2 * LORA], w_in[:, a2 + 2 * LORA:]
    pad = np.zeros((D, WB - 2 * LORA), np.float32)
    cols = np.concatenate([qkv, lv, lq_lk, lr, lora, pad, gates], axis=1)
    out["w_blk"] = np.ascontiguousarray(cols.reshape(KT, P, W_BLOCKS, WB).transpose(2, 1, 0, 3))
    return out


def kernel(**inputs):
    import numpy as np
    import concourse.bacc as bacc
    from concourse.bass_utils import run_bass_kernel_spmd

    nc = bacc.Bacc("TRN2", target_bir_lowering=False, num_devices=1)
    arrays = {f"in_{n}": a for n, a in host_inputs(**inputs).items()}
    io = {n[3:]: nc.dram_tensor(n, a.shape, mybir.dt.from_np(a.dtype), kind="ExternalInput").ap() for n, a in arrays.items()}
    io["out"] = nc.dram_tensor("out", (T, D), F32, kind="ExternalOutput").ap()
    program(nc, io)
    out = run_bass_kernel_spmd(nc, [arrays], core_ids=[0]).results[0]["out"]
    return out[N_SAMPLE:][None], out[:N_SAMPLE][None]
```
